# Optimizing a Trainium2 kernel written in Bass

```python
import math
import jax
import jax.numpy as jnp
from jax import lax
import numpy as np
import jax, jax.numpy as jnp

D_MODEL = 1024
BATCH = 1
SEQ = 256
DEPTH = 2

CHUNK = 64
GDN_HEADS = 8
GDN_DK = 128
GDN_DV = 128
GDN_CONV = 4
GDN_QK = GDN_HEADS * GDN_DK
GDN_V = GDN_HEADS * GDN_DV
GDN_IN = 2 * GDN_QK + 2 * GDN_V + 2 * GDN_HEADS
GDN_DT_MIN = 1e-3
GDN_DT_MAX = 1e-1
S5_GROUP = 16
S5_GROUPS = D_MODEL // S5_GROUP
S5_STATE = 64
S5_DT_MIN = 1e-3
S5_DT_MAX = 1e-1
D_FF = 11 * D_MODEL // 4
N_EXPERTS = 8
TOP_K = 2
D_FF_EXPERT = D_FF // 2
N_EVEN = (DEPTH + 1) // 2
N_ODD = DEPTH // 2
ALPHA = (2 * DEPTH) ** 0.25
BETA_INIT = (8 * DEPTH) ** -0.25
LN_EPS = 1e-5
NORM_EPS = 1e-6


def layer_norm(x, g, b):
    xf = x.astype(jnp.float32)
    mu = jnp.mean(xf, -1, keepdims=True)
    var = jnp.mean(jnp.square(xf - mu), -1, keepdims=True)
    y = (xf - mu) * lax.rsqrt(var + LN_EPS) * g.astype(jnp.float32) + b.astype(jnp.float32)
    return y.astype(x.dtype)

def l2norm(t):
    return t * lax.rsqrt(jnp.sum(t * t, -1, keepdims=True) + NORM_EPS)

def causal_dwconv(x, w):
    k = w.shape[0]
    return lax.conv_general_dilated(x, w[:, None, :].astype(x.dtype), window_strides=(1,),
                                    padding=[(k - 1, 0)], dimension_numbers=('NWC', 'WIO', 'NWC'),
                                    feature_group_count=x.shape[-1])

def gated_delta_rule_chunked(q, k, v, g, beta):
    bsz, seq, nh, dk = q.shape
    dv = v.shape[-1]
    n = seq // CHUNK

    def to_chunks(t):
        t = t.reshape((bsz, n, CHUNK) + t.shape[2:])
        return jnp.moveaxis(t, 3, 1)

    q, k, v, g, beta = (to_chunks(t) for t in (q, k, v, g, beta))
    g = jnp.cumsum(g, axis=-1)
    idx = jnp.arange(CHUNK)
    causal = idx[:, None] >= idx[None, :]
    strict = idx[:, None] > idx[None, :]
    decay = jnp.exp(jnp.where(causal, g[..., :, None] - g[..., None, :], -jnp.inf))
    k_beta = k * beta[..., None]
    v_beta = v * beta[..., None]
    lmat = jnp.where(strict, jnp.einsum('bhncd,bhnsd->bhncs', k_beta, k) * decay, 0.0)
    eye = jnp.eye(CHUNK, dtype=jnp.float32)
    t_inv = lax.linalg.triangular_solve(eye + lmat, jnp.broadcast_to(eye, lmat.shape),
                                        left_side=True, lower=True, unit_diagonal=True)
    u = jnp.einsum('bhncs,bhnsd->bhncd', t_inv, v_beta)
    w = jnp.einsum('bhncs,bhnsd->bhncd', t_inv, k_beta * jnp.exp(g)[..., None])
    a_intra = jnp.einsum('bhncd,bhnsd->bhncs', q, k) * decay

    def step(state, inp):
        q_c, k_c, u_c, w_c, g_c, a_c = inp
        v_new = u_c - jnp.einsum('bhcd,bhde->bhce', w_c, state)
        o = (jnp.einsum('bhcd,bhde->bhce', q_c * jnp.exp(g_c)[..., None], state)
             + jnp.einsum('bhcs,bhse->bhce', a_c, v_new))
        g_last = g_c[..., -1]
        state = (state * jnp.exp(g_last)[..., None, None]
                 + jnp.einsum('bhcd,bhce->bhde', k_c * jnp.exp(g_last[..., None] - g_c)[..., None], v_new))
        return state, o

    xs = tuple(jnp.moveaxis(t, 2, 0) for t in (q, k, u, w, g, a_intra))
    s0 = jnp.zeros((bsz, nh, dk, dv), jnp.float32)
    _, o = lax.scan(step, s0, xs)
    o = jnp.moveaxis(jnp.moveaxis(o, 0, 2), 1, 3)
    return o.reshape(bsz, seq, nh, dv)

def gdn_mixer(x, w_in, conv_w, a_log, dt_bias, norm_g, w_out):
    bsz, seq, _ = x.shape
    f32 = jnp.float32
    proj = x @ w_in
    qkv, z, b, a = jnp.split(proj, [2 * GDN_QK + GDN_V, 2 * GDN_QK + 2 * GDN_V,
                                    2 * GDN_QK + 2 * GDN_V + GDN_HEADS], axis=-1)
    qkv = jax.nn.silu(causal_dwconv(qkv, conv_w)).astype(f32)
    q, k, v = jnp.split(qkv, [GDN_QK, 2 * GDN_QK], axis=-1)
    q = l2norm(q.reshape(bsz, seq, GDN_HEADS, GDN_DK)) * (GDN_DK ** -0.5)
    k = l2norm(k.reshape(bsz, seq, GDN_HEADS, GDN_DK))
    v = v.reshape(bsz, seq, GDN_HEADS, GDN_DV)
    beta = jax.nn.sigmoid(b.astype(f32))
    g = -jnp.exp(a_log.astype(f32)) * jax.nn.softplus(a.astype(f32) + dt_bias.astype(f32))
    o = gated_delta_rule_chunked(q, k, v, g, beta)
    o = o * lax.rsqrt(jnp.mean(o * o, -1, keepdims=True) + NORM_EPS) * norm_g.astype(f32)
    o = o * jax.nn.silu(z.reshape(bsz, seq, GDN_HEADS, GDN_DV).astype(f32))
    return o.reshape(bsz, seq, GDN_V).astype(x.dtype) @ w_out

def s5_mixer(x, w_in, lam_re, lam_im, log_dt, b_re, b_im, c_re, c_im, d_skip, w_glu):
    bsz, seq, _ = x.shape
    f32 = jnp.float32
    n = seq // CHUNK
    u = (x @ w_in).astype(f32)
    lam = lax.complex(lam_re.astype(f32), lam_im.astype(f32))
    dt = jnp.exp(log_dt.astype(f32))[:, None]
    a_bar = jnp.exp(lam * dt)
    b_bar = ((a_bar - 1.0) / lam)[..., None] * lax.complex(b_re.astype(f32), b_im.astype(f32))
    c = lax.complex(c_re.astype(f32), c_im.astype(f32))
    steps = jnp.arange(1, CHUNK + 1, dtype=f32)[:, None, None]
    a_pow = jnp.exp((lam * dt)[None] * steps)

    def binop(e1, e2):
        a1, b1 = e1
        a2, b2 = e2
        return a2 * a1, a2 * b1 + b2

    def step(h, u_c):
        bu = jnp.einsum('gpc,btgc->btgp', b_bar, u_c.astype(jnp.complex64))
        _, hs = lax.associative_scan(binop, (jnp.broadcast_to(a_bar, bu.shape), bu), axis=1)
        hs = hs + a_pow[None] * h[:, None]
        y = jnp.einsum('gcp,btgp->btgc', c, hs).real
        return hs[:, -1], y

    uc = jnp.moveaxis(u.reshape(bsz, n, CHUNK, S5_GROUPS, S5_GROUP), 1, 0)
    h0 = jnp.zeros((bsz, S5_GROUPS, S5_STATE), jnp.complex64)
    _, ys = lax.scan(step, h0, uc)
    y = jnp.moveaxis(ys, 0, 1).reshape(bsz, seq, D_MODEL) + d_skip.astype(f32) * u
    hid = jax.nn.gelu(y.astype(x.dtype), approximate=False)
    val, gate = jnp.split(hid @ w_glu, 2, axis=-1)
    return val * jax.nn.sigmoid(gate)

def swiglu(x, w1, w3, w2):
    return (jax.nn.silu(x @ w1) * (x @ w3)) @ w2

def moe_swiglu(x, w_router, b_router, w1, w3, w2):
    bsz, seq, d = x.shape
    xt = x.reshape(-1, d)
    logits = (xt @ w_router).astype(jnp.float32) + b_router.astype(jnp.float32)
    top_v, top_i = lax.top_k(logits, TOP_K)
    gates = jax.nn.softmax(top_v, axis=-1)
    dense_gate = jnp.sum(jax.nn.one_hot(top_i, N_EXPERTS, dtype=jnp.float32) * gates[..., None], axis=1)
    y = jnp.zeros_like(xt)
    for e in range(N_EXPERTS):
        y = y + dense_gate[:, e:e + 1].astype(x.dtype) * swiglu(xt, w1[e], w3[e], w2[e])
    return y.reshape(bsz, seq, d)

def first_inputs(seed: int = 0) -> dict:
    key = jax.random.key(seed)
    ks = jax.random.split(key, 27)
    f32 = jnp.float32

    def nrm(i, shape, scale):
        return jax.random.normal(ks[i], shape, f32) * scale

    x = nrm(0, (BATCH, SEQ, D_MODEL), 1.0)
    gdn_w_in = nrm(1, (N_EVEN, D_MODEL, GDN_IN), D_MODEL ** -0.5)
    gdn_conv_w = nrm(2, (N_EVEN, GDN_CONV, 2 * GDN_QK + GDN_V), GDN_CONV ** -0.5)
    gdn_a_log = jnp.log(jax.random.uniform(ks[3], (N_EVEN, GDN_HEADS), f32, 1.0, 16.0))
    dt = jnp.exp(jax.random.uniform(ks[4], (N_EVEN, GDN_HEADS), f32, math.log(GDN_DT_MIN), math.log(GDN_DT_MAX)))
    gdn_dt_bias = dt + jnp.log(-jnp.expm1(-dt))
    gdn_norm_g = 1.0 + nrm(5, (N_EVEN, GDN_DV), 0.02)
    gdn_w_out = nrm(6, (N_EVEN, GDN_V, D_MODEL), GDN_V ** -0.5 * BETA_INIT)
    ffn_w1 = nrm(7, (N_EVEN, D_MODEL, D_FF), D_MODEL ** -0.5)
    ffn_w3 = nrm(8, (N_EVEN, D_MODEL, D_FF), D_MODEL ** -0.5)
    ffn_w2 = nrm(9, (N_EVEN, D_FF, D_MODEL), D_FF ** -0.5 * BETA_INIT)
    s5_w_in = nrm(10, (N_ODD, D_MODEL, D_MODEL), D_MODEL ** -0.5)
    s5_lam_re = -0.5 + nrm(11, (N_ODD, S5_GROUPS, S5_STATE), 0.01)
    s5_lam_im = math.pi * jnp.arange(S5_STATE, dtype=f32) + nrm(12, (N_ODD, S5_GROUPS, S5_STATE), 0.01)
    s5_log_dt = jax.random.uniform(ks[13], (N_ODD, S5_GROUPS), f32, math.log(S5_DT_MIN), math.log(S5_DT_MAX))
    s5_b_re = nrm(14, (N_ODD, S5_GROUPS, S5_STATE, S5_GROUP), (2 * S5_GROUP) ** -0.5)
    s5_b_im = nrm(15, (N_ODD, S5_GROUPS, S5_STATE, S5_GROUP), (2 * S5_GROUP) ** -0.5)
    s5_c_re = nrm(16, (N_ODD, S5_GROUPS, S5_GROUP, S5_STATE), S5_STATE ** -0.5)
    s5_c_im = nrm(17, (N_ODD, S5_GROUPS, S5_GROUP, S5_STATE), S5_STATE ** -0.5)
    s5_d = nrm(18, (N_ODD, D_MODEL), 1.0)
    s5_w_glu = nrm(19, (N_ODD, D_MODEL, 2 * D_MODEL), D_MODEL ** -0.5 * BETA_INIT)
    moe_w_router = nrm(20, (N_ODD, D_MODEL, N_EXPERTS), D_MODEL ** -0.5)
    moe_b_router = nrm(21, (N_ODD, N_EXPERTS), 0.01)
    moe_w1 = nrm(22, (N_ODD, N_EXPERTS, D_MODEL, D_FF_EXPERT), D_MODEL ** -0.5)
    moe_w3 = nrm(23, (N_ODD, N_EXPERTS, D_MODEL, D_FF_EXPERT), D_MODEL ** -0.5)
    moe_w2 = nrm(24, (N_ODD, N_EXPERTS, D_FF_EXPERT, D_MODEL), D_FF_EXPERT ** -0.5 * BETA_INIT)
    ln_g = 1.0 + nrm(25, (DEPTH, 2, D_MODEL), 0.02)
    ln_b = nrm(26, (DEPTH, 2, D_MODEL), 0.02)
    return {'x': x, 'gdn_w_in': gdn_w_in, 'gdn_conv_w': gdn_conv_w, 'gdn_a_log': gdn_a_log,
            'gdn_dt_bias': gdn_dt_bias, 'gdn_norm_g': gdn_norm_g, 'gdn_w_out': gdn_w_out,
            'ffn_w1': ffn_w1, 'ffn_w3': ffn_w3, 'ffn_w2': ffn_w2,
            's5_w_in': s5_w_in, 's5_lam_re': s5_lam_re, 's5_lam_im': s5_lam_im, 's5_log_dt': s5_log_dt,
            's5_b_re': s5_b_re, 's5_b_im': s5_b_im, 's5_c_re': s5_c_re, 's5_c_im': s5_c_im,
            's5_d': s5_d, 's5_w_glu': s5_w_glu,
            'moe_w_router': moe_w_router, 'moe_b_router': moe_b_router,
            'moe_w1': moe_w1, 'moe_w3': moe_w3, 'moe_w2': moe_w2,
            'ln_g': ln_g, 'ln_b': ln_b}

def first_block(x, gdn_w_in, gdn_conv_w, gdn_a_log, gdn_dt_bias, gdn_norm_g, gdn_w_out,
              ffn_w1, ffn_w3, ffn_w2,
              s5_w_in, s5_lam_re, s5_lam_im, s5_log_dt, s5_b_re, s5_b_im, s5_c_re, s5_c_im,
              s5_d, s5_w_glu,
              moe_w_router, moe_b_router, moe_w1, moe_w3, moe_w2,
              ln_g, ln_b):
    for i in range(DEPTH):
        j = i // 2
        if i % 2 == 0:
            h = gdn_mixer(x, gdn_w_in[j], gdn_conv_w[j], gdn_a_log[j], gdn_dt_bias[j],
                          gdn_norm_g[j], gdn_w_out[j])
        else:
            h = s5_mixer(x, s5_w_in[j], s5_lam_re[j], s5_lam_im[j], s5_log_dt[j], s5_b_re[j],
                         s5_b_im[j], s5_c_re[j], s5_c_im[j], s5_d[j], s5_w_glu[j])
        x = layer_norm(ALPHA * x + h, ln_g[i, 0], ln_b[i, 0])
        if i % 2 == 0:
            f = swiglu(x, ffn_w1[j], ffn_w3[j], ffn_w2[j])
        else:
            f = moe_swiglu(x, moe_w_router[j], moe_b_router[j], moe_w1[j], moe_w3[j], moe_w2[j])
        x = layer_norm(ALPHA * x + f, ln_g[i, 1], ln_b[i, 1])
    return x


DEPTH_2 = 1

PLE_DIM = 256
CONV_WIDTH = D_MODEL // 2
CONV_HEADS = 8
CONV_K = 3
SGU_WIDTH = D_MODEL // 2
SGU_HEADS = 8
SGU_HEAD_DIM = SGU_WIDTH // SGU_HEADS
CHUNK_2 = 128
MIX_WIDTH = CONV_WIDTH + SGU_WIDTH
IN_PROJ_WIDTH = 3 * CONV_WIDTH + 2 * SGU_WIDTH
N_GROUPS = 4
EXPERTS_PER_GROUP = 8
TOP_K_INNER = 2
D_EXPERT = D_MODEL // 2
EPS = 1e-6


def rmsnorm(x, g):
    xf = x.astype(jnp.float32)
    y = xf * lax.rsqrt(jnp.mean(xf * xf, axis=-1, keepdims=True) + EPS)
    return (y * g.astype(jnp.float32)).astype(x.dtype)

def layernorm(x, g):
    xf = x.astype(jnp.float32)
    mu = jnp.mean(xf, axis=-1, keepdims=True)
    xc = xf - mu
    y = xc * lax.rsqrt(jnp.mean(xc * xc, axis=-1, keepdims=True) + EPS)
    return (y * g.astype(jnp.float32)).astype(x.dtype)

def short_conv_mixer(b_gate, c_gate, x_in, w_conv):
    seq = x_in.shape[1]
    z = c_gate * x_in
    zp = jnp.pad(z, ((0, 0), (CONV_K - 1, 0), (0, 0)))
    conv = sum(zp[:, k:k + seq, :] * w_conv[k] for k in range(CONV_K))
    return b_gate * conv

def sgu_mixer(u, v, g_sgu, w_spatial, b_spatial):
    bsz, seq, _ = v.shape
    v = layernorm(v, g_sgu)
    vc = v.reshape(bsz, seq // CHUNK_2, CHUNK_2, SGU_HEADS, SGU_HEAD_DIM)
    causal = jnp.tril(jnp.ones((CHUNK_2, CHUNK_2), dtype=bool))
    ws = jnp.where(causal[None], w_spatial, jnp.zeros_like(w_spatial))
    mixed = jnp.einsum('hts,bcshd->bcthd', ws, vc) + b_spatial.T[None, None, :, :, None]
    return u * mixed.reshape(bsz, seq, SGU_WIDTH)

def hierarchical_moe(h, w_group, b_group, w_router, b_router, w_gate, w_up, w_down):
    bsz, seq, d = h.shape
    t = h.reshape(bsz * seq, d)
    g_logits = (t @ w_group).astype(jnp.float32) + b_group.astype(jnp.float32)
    g_prob = jax.nn.softmax(g_logits, axis=-1)
    g_w, g_idx = lax.top_k(g_prob, 1)
    e_logits = jnp.einsum('td,gde->tge', t, w_router).astype(jnp.float32) + b_router.astype(jnp.float32)
    e_sel = jnp.take_along_axis(e_logits, g_idx[:, :, None], axis=1)[:, 0]
    e_val, e_idx = lax.top_k(e_sel, TOP_K_INNER)
    e_w = jax.nn.softmax(e_val, axis=-1) * g_w
    inner = jnp.sum(jax.nn.one_hot(e_idx, EXPERTS_PER_GROUP, dtype=jnp.float32) * e_w[..., None], axis=1)
    comb = (jax.nn.one_hot(g_idx[:, 0], N_GROUPS, dtype=jnp.float32)[:, :, None]
            * inner[:, None, :]).astype(h.dtype)
    y = jnp.zeros_like(t)
    for g in range(N_GROUPS):
        a = jnp.einsum('td,edf->tef', t, w_gate[g])
        b = jnp.einsum('td,edf->tef', t, w_up[g])
        hid = jax.nn.silu(a) * b * comb[:, g, :, None]
        y = y + jnp.einsum('tef,efd->td', hid, w_down[g])
    return y.reshape(bsz, seq, d)

def second_inputs(seed: int = 0) -> dict:
    key = jax.random.key(seed)
    ks = jax.random.split(key, 24)
    f32 = jnp.float32
    n = lambda k, shape, scale: jax.random.normal(k, shape, f32) * scale
    gain = lambda k, shape: 1.0 + 0.05 * jax.random.normal(k, shape, f32)
    L, G, E = DEPTH_2, N_GROUPS, EXPERTS_PER_GROUP
    return {
        "x": n(ks[0], (BATCH, SEQ, D_MODEL), 1.0),
        "p": n(ks[1], (DEPTH_2, BATCH, SEQ, PLE_DIM), 1.0),
        "g_mix": gain(ks[2], (L, D_MODEL)),
        "w_in": n(ks[3], (L, D_MODEL, IN_PROJ_WIDTH), D_MODEL ** -0.5),
        "w_conv": n(ks[4], (L, CONV_K, CONV_WIDTH), CONV_K ** -0.5),
        "g_sgu": gain(ks[5], (L, SGU_WIDTH)),
        "w_spatial": n(ks[6], (L, SGU_HEADS, CHUNK_2, CHUNK_2), CHUNK_2 ** -0.5),
        "b_spatial": 1.0 + n(ks[7], (L, SGU_HEADS, CHUNK_2), 0.1),
        "w_out": n(ks[8], (L, MIX_WIDTH, D_MODEL), MIX_WIDTH ** -0.5),
        "g_ffn": gain(ks[9], (L, D_MODEL)),
        "w_group": n(ks[10], (L, D_MODEL, G), D_MODEL ** -0.5),
        "b_group": n(ks[11], (L, G), 0.01),
        "w_router": n(ks[12], (L, G, D_MODEL, E), D_MODEL ** -0.5),
        "b_router": n(ks[13], (L, G, E), 0.01),
        "w_gate": n(ks[14], (L, G, E, D_MODEL, D_EXPERT), D_MODEL ** -0.5),
        "w_up": n(ks[15], (L, G, E, D_MODEL, D_EXPERT), D_MODEL ** -0.5),
        "w_down": n(ks[16], (L, G, E, D_EXPERT, D_MODEL), D_EXPERT ** -0.5),
        "g_ple": gain(ks[17], (L, D_MODEL)),
        "w_ple_gate": n(ks[18], (L, D_MODEL, D_MODEL), D_MODEL ** -0.5),
        "w_ple_proj": n(ks[19], (L, PLE_DIM, D_MODEL), PLE_DIM ** -0.5),
        "g_final": gain(ks[20], (D_MODEL,)),
    }

def second_block(x, p, g_mix, w_in, w_conv, g_sgu, w_spatial, b_spatial, w_out, g_ffn,
              w_group, b_group, w_router, b_router, w_gate, w_up, w_down,
              g_ple, w_ple_gate, w_ple_proj, g_final):
    splits = [CONV_WIDTH, 2 * CONV_WIDTH, 3 * CONV_WIDTH, 3 * CONV_WIDTH + SGU_WIDTH]
    for i in range(DEPTH_2):
        h = rmsnorm(x, g_mix[i])
        z = h @ w_in[i]
        b_gate, c_gate, x_in, u, v = jnp.split(z, splits, axis=-1)
        y_conv = short_conv_mixer(b_gate, c_gate, x_in, w_conv[i])
        y_sgu = sgu_mixer(jax.nn.gelu(u), jax.nn.gelu(v), g_sgu[i],
                          w_spatial[i], b_spatial[i])
        x = x + jnp.concatenate([y_conv, y_sgu], axis=-1) @ w_out[i]
        x = x + hierarchical_moe(rmsnorm(x, g_ffn[i]), w_group[i], b_group[i], w_router[i],
                                 b_router[i], w_gate[i], w_up[i], w_down[i])
        gate = jax.nn.sigmoid(rmsnorm(x, g_ple[i]) @ w_ple_gate[i])
        x = x + gate * (p[i] @ w_ple_proj[i])
    return rmsnorm(x, g_final)


def setup_inputs(seed=0):
    out = dict(first_inputs(seed))
    for name, value in second_inputs(seed + 1).items():
        if name != "x":
            out[name + "_2"] = value
    return out


def reference(
    x, gdn_w_in, gdn_conv_w, gdn_a_log, gdn_dt_bias, gdn_norm_g, gdn_w_out, ffn_w1, ffn_w3,
    ffn_w2, s5_w_in, s5_lam_re, s5_lam_im, s5_log_dt, s5_b_re, s5_b_im, s5_c_re, s5_c_im, s5_d,
    s5_w_glu, moe_w_router, moe_b_router, moe_w1, moe_w3, moe_w2, ln_g, ln_b, p_2, g_mix_2,
    w_in_2, w_conv_2, g_sgu_2, w_spatial_2, b_spatial_2, w_out_2, g_ffn_2, w_group_2, b_group_2,
    w_router_2, b_router_2, w_gate_2, w_up_2, w_down_2, g_ple_2, w_ple_gate_2, w_ple_proj_2,
    g_final_2,
):
    x = first_block(
        x, gdn_w_in, gdn_conv_w, gdn_a_log, gdn_dt_bias, gdn_norm_g, gdn_w_out, ffn_w1, ffn_w3,
        ffn_w2, s5_w_in, s5_lam_re, s5_lam_im, s5_log_dt, s5_b_re, s5_b_im, s5_c_re, s5_c_im,
        s5_d, s5_w_glu, moe_w_router, moe_b_router, moe_w1, moe_w3, moe_w2, ln_g, ln_b,
    )
    return second_block(
        x, p_2, g_mix_2, w_in_2, w_conv_2, g_sgu_2, w_spatial_2, b_spatial_2, w_out_2, g_ffn_2,
        w_group_2, b_group_2, w_router_2, b_router_2, w_gate_2, w_up_2, w_down_2, g_ple_2,
        w_ple_gate_2, w_ple_proj_2, g_final_2,
    )


_drawn_inputs = setup_inputs


def setup_inputs(seed=0):
    import zlib

    import numpy as np

    out = dict(_drawn_inputs(seed))
    spreads = {}
    factors = {'gdn_norm_g': 2.873,
     's5_lam_re': 8.0,
     's5_b_re': 3.083,
     's5_c_re': 3.142,
     'moe_b_router': 8.0,
     'g_sgu_2': 3.185,
     'b_group_2': 6.615,
     'b_router_2': 3.582,
     'g_ple_2': 7.891}
    for name, (base, spread) in spreads.items():
        noise = np.random.default_rng([zlib.crc32(name.encode()), seed]).standard_normal(out[name].shape)
        drawn = base * np.exp(spread * noise) if base else spread * noise
        out[name] = jnp.asarray(drawn.astype(out[name].dtype))
    for name, factor in factors.items():
        out[name] = (out[name] * factor).astype(out[name].dtype)
    return out
```

```python
from contextlib import ExitStack
from typing import NamedTuple

import numpy as np
import concourse.bass as bass
from concourse import mybir

F32 = mybir.dt.float32
I32 = mybir.dt.int32
U32 = mybir.dt.uint32
ALU = mybir.AluOpType
ACT = mybir.ActivationFunctionType
AX = mybir.AxisListType

P = 128
SEQ, D = 256, 1024
HALVES, DC = SEQ // P, D // P
HEADS, CHUNK = 8, 64
QKV = 3 * HEADS
TAPS = 4
S5_GROUPS, S5_STATE, S5_CH = 64, 64, 16
PAIRS = S5_GROUPS // 2
STEP = 2
NSTEP = SEQ // STEP
FF_E = 1408
FF_BLOCKS = (4, 4, 3)
EXPERTS, SLOTS1 = 8, 128
GROUPS2, PER_GROUP = 4, 8
EXPERTS2 = GROUPS2 * PER_GROUP
PACK, SLOTS2, FF2 = 2, 64, 512
PACKS = EXPERTS2 // PACK
CONV2_TAPS, CW, SGU_HEADS = 3, 512, 8
ALPHA = 4.0 ** 0.25
LN_EPS, NORM_EPS = 1e-5, 1e-6
UNIT = 4096
RING = 3
NEG = -1e30

U_QKV, U_Z, U_WOUT, U_FFN, U_S5IN, U_GLU, U_MOE1, U_WIN2, U_WOUT2, U_MOE2, U_PLE = (
    0, 6, 8, 10, 28, 30, 34, 106, 111, 113, 209)
DENSE_AT = {U_QKV: 0, U_Z: 6, U_WOUT: 8, U_S5IN: 10, U_GLU: 12, U_WIN2: 16, U_WOUT2: 21, U_PLE: 23}
UP_K, DOWN_C = UNIT // (PACK * 2 * FF2), UNIT // (PACK * D)
UP_UNITS, DOWN_UNITS = DC // UP_K, FF2 // P // DOWN_C
UNITS_EXPERT, UNITS_PACK = 9, UP_UNITS + DOWN_UNITS


class Order(NamedTuple):
    first: int
    names: list


class Chain:

    def __init__(self, sem):
        self.sem, self.n = sem, 0

    def __call__(self, eng, ins):
        self.n += 1
        ins.then_inc(self.sem, 1)
        eng.wait_ge(self.sem, self.n)


def program(nc, I, out, upto="all"):
    ctx = ExitStack()
    with ctx:
        def sb(name, shape, dt=F32):
            return ctx.enter_context(nc.sbuf_tensor("sb_" + name, shape, dt))

        sems = {}

        def sem(name):
            if name not in sems:
                sems[name] = ctx.enter_context(nc.semaphore(name))
            return sems[name]

        ring = sb("ring", [P, RING, UNIT])
        xres = sb("xres", [P, HALVES, D])
        xT = sb("xT", [P, DC, SEQ])
        lnp = sb("lnp", [P, 2, D])
        consts = sb("consts", [P, 18, P])
        (ident, cum, negm, lvl0, lvl1, lvl2, lvl3, lvl4, lvl5, blk, first64, last64,
         before, ones, iota, upto_t, blk32, half_mask) = (consts[:, i, :] for i in range(18))
        lvl = (lvl0, lvl1, lvl2, lvl3, lvl4, lvl5)
        small = sb("small", [P, 1400])
        smalli = sb("smalli", [P, 32], I32)
        WORK = 30800
        work = sb("work", [P, WORK])
        psum = ctx.enter_context(nc.psum_tensor("psum", [P, 8, 512], F32))
        bank = [psum[:, i, :] for i in range(8)]

        class Carver:
            def __init__(self, tile, at, end):
                self.tile, self.at, self.end = tile, at, end

            def __call__(self, *shape):
                n = int(np.prod(shape))
                a = self.tile[:, self.at:self.at + n]
                self.at += n
                assert self.at <= self.end, (self.at, self.end)
                if len(shape) == 2:
                    a = a.rearrange("p (a b) -> p a b", a=shape[0])
                if len(shape) == 3:
                    a = a.rearrange("p (a b c) -> p a b c", a=shape[0], b=shape[1])
                if len(shape) == 4:
                    a = a.rearrange("p (a b c d) -> p a b c d", a=shape[0], b=shape[1], c=shape[2])
                return a

        cs = Carver(small, 0, 1400)
        stats = cs(HALVES, 2, 6)
        mv = cs(HALVES, 2)
        rstd = cs(HALVES, 1)
        rtmp = cs(HALVES, 1)
        w_ba = cs(DC, 16)
        conv_w = cs(QKV, TAPS)
        a_log, dt_bias = cs(HEADS), cs(HEADS)
        norm_g = cs(P)
        ba = cs(HALVES, 16)
        g_t, beta, sp_t, sp_a = (cs(HALVES, HEADS) for _ in range(4))
        rn = cs(HALVES, 2 * HEADS)
        gc, eg, kd_s, kb_s, kbg_s, rq_s = (cs(HALVES, HEADS) for _ in range(6))
        s_scale = cs(2 * HALVES, HEADS)
        oms, of = cs(HALVES, HEADS), cs(HALVES, HEADS)
        g_cols = cs(3, DC)
        conv2_w = cs(CW // P, CONV2_TAPS)
        b_sp = cs(SGU_HEADS)
        s5_d = cs(DC)

        def bc(ap, axis, n):
            a = ap.unsqueeze(axis)
            shape = list(a.shape)
            shape[axis] = n
            return a.to_broadcast(shape)

        def slot(u):
            return ring[:, u % RING, :]

        def unit_ready(pe, u):
            pe.wait_ge(sem(f"unit_loaded{u % RING}"), 16 * (u // RING + 1))

        def unit_ready_it(pe, u, it, per):
            pe.wait_ge(sem(f"unit_loaded{u % RING}"), it * (16 * (per // RING)) + 16 * (u // RING + 1))

        pe_link = Chain(sem("pe_link"))
        act_link = Chain(sem("act_link"))
        dve_link = Chain(sem("dve_link"))
        pool_link = Chain(sem("pool_link"))
        NLOADS = 11

        def phase_end(eng, n):
            eng.drain().then_inc(sem("phase_done"), 1)
            eng.wait_ge(sem("phase_done"), 4 * n)

        def mm(o, lhsT, rhs, start=True, stop=True, **kw):
            return nc.tensor.matmul(o, lhsT, rhs, start=start, stop=stop, **kw)

        TSTAGE = {0: 0, 1: 1, 2: 2, 4: 3, 5: 4, 6: 5}

        def norm_vector(v, n, y, xn):
            for h in range(HALVES):
                if n < 4:
                    v.bn_stats(stats[:, h, 0, :], y[:, h, 0:512])
                    dve_link(v, v.bn_stats(stats[:, h, 1, :], y[:, h, 512:1024]))
                    dve_link(v, v.bn_aggr(mv[:, h, :], stats[:, h, :, :].rearrange("p a b -> p (a b)")))
                    dve_link(v, v.tensor_scalar(rtmp[:, h, :], mv[:, h, 1:2], LN_EPS, None, ALU.add))
                else:
                    dve_link(v, v.tensor_tensor(xn[:, h, :], y[:, h, :], y[:, h, :], ALU.mult))
                    dve_link(v, v.tensor_reduce(mv[:, h, 0:1], xn[:, h, :], AX.X, ALU.add))
                    dve_link(v, v.tensor_scalar(rtmp[:, h, :], mv[:, h, 0:1], 1.0 / D, NORM_EPS, ALU.mult, ALU.add))
                v.reciprocal(rtmp[:, h, :], rtmp[:, h, :]).then_inc(sem("var_inv"), 1)
            for h in range(HALVES):
                v.wait_ge(sem("rstd_ready"), 2 * n + h + 1)
                if n < 4:
                    dve_link(v, v.tensor_scalar(xn[:, h, :], y[:, h, :], mv[:, h, 0:1], rstd[:, h, :],
                                                ALU.subtract, ALU.mult))
                    if h == 0:
                        v.wait_ge(sem("lnp_loaded"), 32 * (n + 1))
                    dve_link(v, v.tensor_tensor(xn[:, h, :], xn[:, h, :], lnp[:, 0, :], ALU.mult))
                    v.tensor_tensor(xn[:, h, :], xn[:, h, :], lnp[:, 1, :], ALU.add).then_inc(sem("rows_normed"), 1)
                elif n < 7:
                    v.tensor_scalar(xn[:, h, :], y[:, h, :], rstd[:, h, :], None, ALU.mult).then_inc(sem("rows_normed"), 1)
                else:
                    dve_link(v, v.tensor_scalar(xn[:, h, :], y[:, h, :], rstd[:, h, :], None, ALU.mult))
                    v.tensor_tensor(xn[:, h, :], xn[:, h, :], lnp[:, 0, :], ALU.mult).then_inc(sem("rows_normed"), 1)
            v.wait_ge(sem("rows_normed"), 2 * n + 2)

        def norm_scalar(act, n):
            for h in range(HALVES):
                act.wait_ge(sem("var_inv"), 2 * n + h + 1)
                act.activation(rstd[:, h, :], rtmp[:, h, :], ACT.Sqrt).then_inc(sem("rstd_ready"), 1)

        def turn_tensor(pe, n, xn):
            t = TSTAGE[n]
            for h in range(HALVES):
                pe.wait_ge(sem("rows_normed"), 2 * n + h + 1)
                for q in range(2):
                    for c in range(4):
                        ins = pe.transpose(bank[4 + 2 * h + q][:, c * P:(c + 1) * P],
                                           xn[:, h, (4 * q + c) * P:(4 * q + c + 1) * P], ident)
                    ins.then_inc(sem("turned"), 1)
            pe.wait_ge(sem("xT_ready"), 4 * (t + 1))

        def turn_evacuate(eng, n, gain):
            t = TSTAGE[n]
            for h in range(HALVES):
                for q in range(2):
                    eng.wait_ge(sem("turned"), 4 * t + 2 * h + q + 1)
                    o = xT[:, 4 * q:4 * q + 4, h * P:(h + 1) * P]
                    i = bank[4 + 2 * h + q][:, :].rearrange("p (c t) -> p c t", c=4)
                    if gain is None:
                        ins = eng.activation(o, i, ACT.Copy)
                    else:
                        ins = eng.tensor_tensor(o, i, bc(gain[:, 4 * q:4 * q + 4], 2, P), ALU.mult)
                    ins.then_inc(sem("xT_ready"), 1)

        cw = Carver(work, 0, WORK)
        raw = cw(QKV, SEQ + TAPS - 1)
        qkvT = cw(QKV, SEQ)
        zs = cw(HALVES, D)
        IDX = HALVES * HEADS
        DT = cw(IDX, P)
        LT = cw(IDX, P)
        Ut = cw(IDX, P)
        Wm = cw(IDX, P)
        gB = cw(IDX, P)
        kbB = cw(IDX, P)
        S = cw(HEADS, P)
        c2 = Carver(work, 0, QKV * (SEQ + TAPS - 1))
        vb, kd, kbg = c2(IDX, P), c2(IDX, P), c2(IDX, P)
        qT, kT, vT = (qkvT[:, HEADS * i:HEADS * (i + 1), :] for i in range(3))
        Tm = kT.rearrange("p h t -> p (h t)").rearrange("p (i c) -> p i c", i=IDX)
        Am = vT.rearrange("p h t -> p (h t)").rearrange("p (i c) -> p i c", i=IDX)
        sq = [t.rearrange("p i c -> p (i c)").rearrange("p (h t) -> p h t", h=HEADS) for t in (Wm, gB)]
        uu, wT, vnew, o_rows = LT, Am, Tm, gB
        oT = kbB.rearrange("p i c -> p (i c)").rearrange("p (h t) -> p h t", h=HEADS)
        HD = HEADS // 2

        def grp(t, G):
            return t[:, HD * G:HD * (G + 1), :]

        def bank3(b):
            return bank[b][:, :].rearrange("p (i c) -> p i c", i=HD)

        NGRP = IDX // HD

        def gdn_tensor(pe):
            pe.wait_ge(sem("xT_loaded"), 16)
            for c in range(QKV):
                if c % 4 == 0:
                    unit_ready(pe, U_QKV + c // 4)
                if c >= 4:
                    pe.wait_ge(sem("qkv_evac"), c - 3)
                w = slot(U_QKV + c // 4).rearrange("p (k n) -> p k n", k=DC)
                for k in range(DC):
                    ins = mm(bank[c % 4][:, 0:SEQ], w[:, k, (c % 4) * P:(c % 4 + 1) * P], xT[:, k, :],
                             k == 0, k == DC - 1)
                ins.then_inc(sem("qkv_ps"), 1)
            pe.wait_ge(sem("small_loaded"), 16 * NLOADS)
            pe.wait_ge(sem("qkv_evac"), QKV - 3)
            for h in range(HALVES):
                for k in range(DC):
                    ins = mm(bank[0][:, 16 * h:16 * h + 16], xT[:, k, h * P:(h + 1) * P], w_ba[:, k, :],
                             k == 0, k == DC - 1)
            ins.then_inc(sem("ba_ps"), 1)
            for j in range(2):
                unit_ready(pe, U_Z + j)
                w = slot(U_Z + j).rearrange("p (k n) -> p k n", k=DC)
                for h in range(HALVES):
                    for k in range(DC):
                        ins = mm(bank[4 + 2 * j + h][:, :], xT[:, k, h * P:(h + 1) * P], w[:, k, :], k == 0, k == DC - 1)
                    ins.then_inc(sem("z_ps"), 1)
            pe.wait_ge(sem("qkv_evac"), QKV - 2)
            for c in range(2 * HEADS):
                pe.wait_ge(sem("sq_done"), c + 1)
                for h in range(HALVES):
                    ins = mm(bank[1][:, 2 * HEADS * h + c:2 * HEADS * h + c + 1],
                             sq[c // HEADS][:, c % HEADS, h * P:(h + 1) * P], ones[:, 0:1])
            ins.then_inc(sem("l2_ps"), 1)
            pe.wait_ge(sem("qkv_evac"), QKV)
            pe.wait_ge(sem("silu_done"), QKV)
            pe.wait_ge(sem("z_done"), 4)
            pe.wait_ge(sem("g_ready"), 1)
            for h in range(HALVES):
                mm(bank[0][:, 32 + 8 * h:40 + 8 * h], cum, g_t[:, h, :])
                mm(bank[0][:, 48 + 8 * h:56 + 8 * h], blk, g_t[:, h, :])
                mm(bank[0][:, 64 + 16 * h:72 + 16 * h], first64, g_t[:, h, :])
                ins = mm(bank[0][:, 72 + 16 * h:80 + 16 * h], last64, g_t[:, h, :])
            ins.then_inc(sem("gsum_ps"), 1)
            for G in range(NGRP):
                h, h0 = G // 2, HD * (G % 2)
                if G >= 2:
                    pe.wait_ge(sem("kd_done"), G - 1)
                    pe.wait_ge(sem("kbg_done"), G - 1)
                    pe.wait_ge(sem("vrows_done"), G - 1)
                for i in range(HD):
                    ins = pe.transpose(bank[4 + G % 2][:, i * P:(i + 1) * P], kT[:, h0 + i, h * P:(h + 1) * P], ident)
                ins.then_inc(sem("krows_ps"), 1)
                for i in range(HD):
                    ins = pe.transpose(bank[6 + G % 2][:, i * P:(i + 1) * P], vT[:, h0 + i, h * P:(h + 1) * P], ident)
                ins.then_inc(sem("vrows_ps"), 1)
            pe.wait_ge(sem("bcast_done"), 2)
            for G in range(NGRP):
                h, h0 = G // 2, HD * (G % 2)
                if G >= 1:
                    pe.wait_ge(sem("decay_arg"), HD * G)
                    pe.wait_ge(sem("lt_done"), G)
                for i in range(HD):
                    ins = mm(bank[2][:, i * P:(i + 1) * P], gB[:, HD * G + i, :], cum)
                ins.then_inc(sem("decay_ps"), 1)
                for i in range(HD):
                    mm(bank[3][:, i * P:(i + 1) * P], kbB[:, HD * G + i, :], ident)
                if G < 2:
                    pe.wait_ge(sem("kd_done"), G + 3)
                    pe.wait_ge(sem("kbg_done"), G + 3)
                    pe.wait_ge(sem("vrows_done"), G + 3)
                else:
                    pe.wait_ge(sem("at_done"), G - 1)
                for i in range(HD):
                    kk = kT[:, h0 + i, h * P:(h + 1) * P]
                    ins = mm(bank[4 + G % 2][:, i * P:(i + 1) * P], kk, kk)
                ins.then_inc(sem("kk_ps"), 1)
                for i in range(HD):
                    ins = mm(bank[6 + G % 2][:, i * P:(i + 1) * P], kT[:, h0 + i, h * P:(h + 1) * P],
                             qT[:, h0 + i, h * P:(h + 1) * P])
                ins.then_inc(sem("kq_ps"), 1)
            for m in range(6):
                for G in range(NGRP + 1):
                    if G < NGRP:
                        g = NGRP * m + G
                        pe.wait_ge(sem("a_done"), g + 1)
                        if m > 0:
                            pe.wait_ge(sem("t_done"), g - NGRP + 1)
                            pe.wait_ge(sem("u_done"), g - NGRP + 1)
                        if g >= 2:
                            pe.wait_ge(sem("w_evac"), g - 1)
                        for i in range(HD):
                            j = HD * G + i
                            ins = mm(bank[g % 2][:, i * P:(i + 1) * P], Am[:, j, :], ident if m == 0 else Tm[:, j, :])
                        ins.then_inc(sem("w_ps"), 1)
                    if G > 0 and m > 0:
                        g = NGRP * m + G - 1
                        pe.wait_ge(sem("w_evac"), g + 1)
                        if g >= NGRP + 2:
                            pe.wait_ge(sem("t_done"), min(g - 1, 5 * NGRP))
                            pe.wait_ge(sem("u_done"), g - 1)
                        if m < 5:
                            for i in range(HD):
                                j = HD * (G - 1) + i
                                ins = mm(bank[2 + g % 2][:, i * P:(i + 1) * P], Ut[:, j, :], Wm[:, j, :])
                            ins.then_inc(sem("tw_ps"), 1)
                        for i in range(HD):
                            j = HD * (G - 1) + i
                            ins = mm(bank[4 + g % 2][:, i * P:(i + 1) * P], Wm[:, j, :], Ut[:, j, :])
                        ins.then_inc(sem("wu_ps"), 1)
            pe.wait_ge(sem("w_evac"), 6 * NGRP)
            pe.wait_ge(sem("t_done"), 5 * NGRP)
            for G in range(NGRP):
                pe.wait_ge(sem("u_done"), 5 * NGRP + G + 1)
                if G >= 2:
                    pe.wait_ge(sem("uu_done"), G - 1)
                    pe.wait_ge(sem("wt_done"), G - 1)
                for i in range(HD):
                    j = HD * G + i
                    ins = mm(bank[G % 2][:, i * P:(i + 1) * P], Ut[:, j, :], vb[:, j, :])
                ins.then_inc(sem("uu_ps"), 1)
                for i in range(HD):
                    j = HD * G + i
                    ins = mm(bank[2 + G % 2][:, i * P:(i + 1) * P], kbg[:, j, :], Ut[:, j, :])
                ins.then_inc(sem("wt_ps"), 1)
            pe.wait_ge(sem("uu_done"), NGRP)
            pe.wait_ge(sem("wt_done"), NGRP)
            for n in range(2 * HALVES):
                h, r = n // 2, CHUNK * (n % 2)
                rows = slice(r, r + CHUNK)
                if n > 0:
                    for e in range(HEADS):
                        j = HEADS * h + e
                        pe.wait_ge(sem("state_done"), HEADS * (n - 1) + e + 1)
                        ins = mm(bank[e // HD][rows, (e % HD) * P:(e % HD + 1) * P], wT[:, j, rows], S[:, e, :])
                        if e % HD == HD - 1:
                            ins.then_inc(sem("ws_ps"), 1)
                    for e in range(HEADS):
                        ins = mm(bank[2 + e // HD][rows, (e % HD) * P:(e % HD + 1) * P],
                                 qT[:, e, h * P + r:h * P + r + CHUNK], S[:, e, :])
                        if e % HD == HD - 1:
                            ins.then_inc(sem("qs_ps"), 1)
                for b in range(2):
                    pe.wait_ge(sem("vnew_done"), 2 * n + b + 1)
                    if n < 2 * HALVES - 1:
                        for i in range(HD):
                            j = HEADS * h + HD * b + i
                            ins = mm(bank[4 + b][:, i * P:(i + 1) * P], kd[rows, j, :], vnew[rows, j, :])
                        ins.then_inc(sem("ds_ps"), 1)
                if n % 2 == 1:
                    for b in range(2):
                        if h > 0:
                            pe.wait_ge(sem("o_sum"), b + 1)
                        for i in range(HD):
                            j = HEADS * h + HD * b + i
                            ins = mm(bank[6 + b][:, i * P:(i + 1) * P], DT[:, j, :], vnew[:, j, :])
                        ins.then_inc(sem("oi_ps"), 1)
            for G in range(NGRP):
                h, h0 = G // 2, HD * (G % 2)
                pe.wait_ge(sem("o_gated"), h + 1)
                for i in range(HD):
                    ins = pe.transpose(bank[G][:, i * P:(i + 1) * P], o_rows[:, HD * G + i, :], ident)
                ins.then_inc(sem("ot_ps"), 1)
            pe.wait_ge(sem("ot_done"), NGRP)
            for j in range(2):
                unit_ready(pe, U_WOUT + j)
                w = slot(U_WOUT + j).rearrange("p (k n) -> p k n", k=DC)
                for h in range(HALVES):
                    for k in range(DC):
                        ins = mm(bank[4 + 2 * j + h][:, :], oT[:, k, h * P:(h + 1) * P], w[:, k, :], k == 0, k == DC - 1)
                    ins.then_inc(sem("wout_ps"), 1)

        def gdn_scalar(act):
            for name, dst in (("w_ba", w_ba), ("conv_w", conv_w), ("a_log", a_log), ("dt_bias", dt_bias),
                              ("norm_g", norm_g), ("consts", consts[:, :, :]), ("x_rows", xres[:, :, :]),
                              ("g_cols", g_cols), ("conv2_w", conv2_w), ("b_sp", b_sp), ("s5_d", s5_d)):
                act.dma_start(dst, I[name]).then_inc(sem("small_loaded"), 16)
            load_norm(act, 0)
            for c in range(QKV + 2):
                if c < QKV:
                    act.wait_ge(sem("qkv_ps"), c + 1)
                    act.activation(raw[:, c, TAPS - 1:], bank[c % 4][:, 0:SEQ], ACT.Copy).then_inc(sem("qkv_evac"), 1)
                if c >= 2:
                    act.wait_ge(sem("conv_done"), c - 1)
                    act.activation(qkvT[:, c - 2, :], qkvT[:, c - 2, :], ACT.Silu).then_inc(sem("silu_done"), 1)
            for j in range(2):
                for h in range(HALVES):
                    act.wait_ge(sem("z_ps"), 2 * j + h + 1)
                    act.activation(zs[:, h, 512 * j:512 * j + 512], bank[4 + 2 * j + h][:, :], ACT.Silu).then_inc(sem("z_done"), 1)
            act.wait_ge(sem("gate_in"), 1)
            act.activation(beta[:, :, :], ba[:, :, 0:HEADS], ACT.Sigmoid).then_inc(sem("beta_done"), 1)
            act_link(act, act.activation(sp_a[:, :, :], sp_a[:, :, :], ACT.Exp, scale=-1.0))
            act.activation(a_log, a_log, ACT.Exp).then_inc(sem("sp_done"), 1)
            act.activation(sp_a[:, :, :], sp_a[:, :, :], ACT.Ln, bias=1.0).then_inc(sem("sp_done"), 1)
            act.wait_ge(sem("rn_inv"), 1)
            act.activation(rn[:, :, :], rn[:, :, :], ACT.Sqrt).then_inc(sem("rn_done"), 1)
            act.wait_ge(sem("gsum_done"), 2)
            act.activation(eg[:, :, :], gc[:, :, :], ACT.Exp).then_inc(sem("eg_done"), 1)
            act.activation(kd_s[:, :, :], kd_s[:, :, :], ACT.Exp).then_inc(sem("eg_done"), 1)
            act.activation(s_scale[:, :, :], bank[0][:, 64:96].rearrange("p (n h) -> p n h", n=2 * HALVES),
                           ACT.Exp).then_inc(sem("eg_done"), 1)
            act.wait_ge(sem("scalars_done"), 1)
            for G in range(NGRP):
                act.wait_ge(sem("krows_ps"), G + 1)
                for i in range(HD):
                    h, e = G // 2, HD * (G % 2) + i
                    ins = act.activation(kd[:, HD * G + i, :], bank[4 + G % 2][:, i * P:(i + 1) * P], ACT.Copy,
                                         scale=kd_s[:, h, e:e + 1])
                ins.then_inc(sem("kd_done"), 1)
                act.wait_ge(sem("vrows_ps"), G + 1)
                for i in range(HD):
                    h, e = G // 2, HD * (G % 2) + i
                    ins = act.activation(vb[:, HD * G + i, :], bank[6 + G % 2][:, i * P:(i + 1) * P], ACT.Copy,
                                         scale=beta[:, h, e:e + 1])
                ins.then_inc(sem("vrows_done"), 1)
            for G in range(NGRP):
                act.wait_ge(sem("decay_arg"), HD * (G + 1))
                act.activation(grp(DT, G), grp(DT, G), ACT.Exp).then_inc(sem("decay_done"), 1)
            for g in range(6 * NGRP):
                act.wait_ge(sem("w_ps"), g + 1)
                if g >= 2 * NGRP:
                    act.wait_ge(sem("wu_ps"), g - 2 * NGRP + 1)
                act.activation(grp(Wm, g % NGRP), bank3(g % 2), ACT.Copy).then_inc(sem("w_evac"), 1)
            for G in range(NGRP):
                act.wait_ge(sem("wt_ps"), G + 1)
                act.activation(grp(wT, G), bank3(2 + G % 2), ACT.Copy).then_inc(sem("wt_done"), 1)
            act.wait_ge(sem("oms_inv"), 1)
            act.activation(of[:, :, :], of[:, :, :], ACT.Sqrt).then_inc(sem("of_done"), 1)
            for G in range(NGRP):
                h, h0 = G // 2, HD * (G % 2)
                act.wait_ge(sem("ot_ps"), G + 1)
                act.activation(oT[:, h0:h0 + HD, h * P:(h + 1) * P], bank3(G), ACT.Copy).then_inc(sem("ot_done"), 1)
            norm_scalar(act, 0)
            turn_evacuate(act, 0, None)

        def gdn_vector(v):
            v.wait_ge(sem("pad_done"), 1)
            v.wait_ge(sem("small_loaded"), 16 * NLOADS)
            for c in range(QKV):
                v.wait_ge(sem("qkv_evac"), c + 1)
                acc = qkvT[:, c, :]
                dve_link(v, v.tensor_scalar(acc, raw[:, c, 0:SEQ], conv_w[:, c, 0:1], None, ALU.mult))
                for k in range(1, TAPS):
                    ins = v.scalar_tensor_tensor(acc, raw[:, c, k:k + SEQ], conv_w[:, c, k:k + 1], acc, ALU.mult, ALU.add)
                    if k < TAPS - 1:
                        dve_link(v, ins)
                ins.then_inc(sem("conv_done"), 1)
            v.wait_ge(sem("ba_ps"), 1)
            dve_link(v, v.tensor_copy(ba[:, :, :], bank[0][:, 0:32].rearrange("p (h n) -> p h n", h=HALVES)))
            dve_link(v, v.tensor_tensor(sp_t[:, :, :], ba[:, :, HEADS:], bc(dt_bias, 1, HALVES), ALU.add))
            dve_link(v, v.tensor_scalar(sp_a[:, :, :], sp_t[:, :, :], -1.0, None, ALU.mult))
            v.tensor_tensor(sp_a[:, :, :], sp_a[:, :, :], sp_t[:, :, :], ALU.max).then_inc(sem("gate_in"), 1)
            v.wait_ge(sem("gate_in"), 1)
            dve_link(v, v.tensor_scalar(sp_t[:, :, :], sp_t[:, :, :], 0.0, None, ALU.max))
            v.wait_ge(sem("l2_ps"), 1)
            dve_link(v, v.tensor_scalar(rn[:, :, :], bank[1][:, 0:4 * HEADS].rearrange("p (h n) -> p h n", h=HALVES),
                                        NORM_EPS, None, ALU.add))
            v.reciprocal(rn[:, :, :], rn[:, :, :]).then_inc(sem("rn_inv"), 1)
            v.wait_ge(sem("sp_done"), 2)
            dve_link(v, v.tensor_tensor(sp_t[:, :, :], sp_t[:, :, :], sp_a[:, :, :], ALU.add))
            v.scalar_tensor_tensor(g_t[:, :, :], sp_t[:, :, :], -1.0, bc(a_log, 1, HALVES), ALU.mult, ALU.mult)\
             .then_inc(sem("g_ready"), 1)
            v.wait_ge(sem("gsum_ps"), 1)
            v.tensor_copy(gc[:, :, :], bank[0][:, 32:48].rearrange("p (h n) -> p h n", h=HALVES)).then_inc(sem("gsum_done"), 1)
            v.wait_ge(sem("gsum_done"), 1)
            v.tensor_tensor(kd_s[:, :, :], bank[0][:, 48:64].rearrange("p (h n) -> p h n", h=HALVES), gc[:, :, :],
                            ALU.subtract).then_inc(sem("gsum_done"), 1)
            v.wait_ge(sem("eg_done"), 3)
            v.wait_ge(sem("rn_done"), 1)
            v.wait_ge(sem("beta_done"), 1)
            dve_link(v, v.tensor_tensor(kb_s[:, :, :], rn[:, :, HEADS:], beta[:, :, :], ALU.mult))
            v.tensor_scalar(rq_s[:, :, :], rn[:, :, 0:HEADS], float(P) ** -0.5, None, ALU.mult)
            v.tensor_tensor(kbg_s[:, :, :], kb_s[:, :, :], eg[:, :, :], ALU.mult)
            v.tensor_tensor(kd_s[:, :, :], kd_s[:, :, :], rn[:, :, HEADS:], ALU.mult).then_inc(sem("scalars_done"), 1)
            v.wait_ge(sem("scalars_done"), 1)
            v.wait_ge(sem("l2_ps"), 1)
            v.tensor_copy(gB[:, :, :], bc(g_t.rearrange("p a b -> p (a b)"), 2, P)).then_inc(sem("bcast_done"), 1)
            v.tensor_copy(kbB[:, :, :], bc(kb_s.rearrange("p a b -> p (a b)"), 2, P)).then_inc(sem("bcast_done"), 1)
            for G in range(NGRP):
                v.wait_ge(sem("kd_done"), G + 1)
                for i in range(HD):
                    h, e = G // 2, HD * (G % 2) + i
                    ins = v.tensor_scalar(kbg[:, HD * G + i, :], bank[4 + G % 2][:, i * P:(i + 1) * P],
                                          kbg_s[:, h, e:e + 1], None, ALU.mult)
                ins.then_inc(sem("kbg_done"), 1)
            for G in range(NGRP):
                h, h0 = G // 2, HD * (G % 2)
                v.wait_ge(sem("decay_ps"), G + 1)
                for i in range(HD):
                    v.scalar_tensor_tensor(DT[:, HD * G + i, :], bank[2][:, i * P:(i + 1) * P], gc[:, h, h0 + i:h0 + i + 1],
                                           negm, ALU.subtract, ALU.add).then_inc(sem("decay_arg"), 1)
                v.wait_ge(sem("kk_ps"), G + 1)
                v.wait_ge(sem("decay_done"), G + 1)
                for i in range(HD):
                    ins = v.scalar_tensor_tensor(LT[:, HD * G + i, :], bank[4 + G % 2][:, i * P:(i + 1) * P],
                                                 rn[:, h, HEADS + h0 + i:HEADS + h0 + i + 1], DT[:, HD * G + i, :],
                                                 ALU.mult, ALU.mult)
                dve_link(v, ins)
                v.tensor_tensor(grp(LT, G), grp(LT, G), bank3(3), ALU.mult).then_inc(sem("lt_done"), 1)
                v.wait_ge(sem("kq_ps"), G + 1)
                for i in range(HD):
                    ins = v.scalar_tensor_tensor(DT[:, HD * G + i, :], bank[6 + G % 2][:, i * P:(i + 1) * P],
                                                 rn[:, h, HEADS + h0 + i:HEADS + h0 + i + 1], DT[:, HD * G + i, :],
                                                 ALU.mult, ALU.mult)
                ins.then_inc(sem("at_done"), 1)
            v.wait_ge(sem("at_done"), NGRP)
            for m in range(6):
                for G in range(NGRP):
                    g = NGRP * m + G
                    if m > 0:
                        v.wait_ge(sem("w_ps"), g - NGRP + 1)
                    if m == 1:
                        v.wait_ge(sem("u_done"), G + 1)
                    v.wait_ge(sem("lt_done"), G + 1)
                    v.tensor_tensor(grp(Am, G), grp(LT, G), bc(lvl[m], 1, HD), ALU.mult).then_inc(sem("a_done"), 1)
                for G in range(NGRP):
                    g = NGRP * m + G
                    idb = bc(ident, 1, HD)
                    if m == 0:
                        v.wait_ge(sem("w_evac"), g + 1)
                        v.tensor_tensor(grp(Tm, G), idb, grp(Wm, G), ALU.subtract).then_inc(sem("t_done"), 1)
                        v.wait_ge(sem("a_done"), g + 1)
                        v.tensor_tensor(grp(Ut, G), idb, grp(Am, G), ALU.subtract).then_inc(sem("u_done"), 1)
                        continue
                    v.wait_ge(sem("wu_ps"), g - NGRP + 1)
                    if m < 5:
                        v.wait_ge(sem("t_done"), g - NGRP + 1)
                        v.tensor_tensor(grp(Tm, G), grp(Tm, G), bank3(2 + g % 2), ALU.subtract).then_inc(sem("t_done"), 1)
                    v.wait_ge(sem("u_done"), g - NGRP + 1)
                    v.tensor_tensor(grp(Ut, G), grp(Ut, G), bank3(4 + g % 2), ALU.subtract).then_inc(sem("u_done"), 1)
            for G in range(NGRP):
                v.wait_ge(sem("uu_ps"), G + 1)
                v.tensor_copy(grp(uu, G), bank3(G % 2)).then_inc(sem("uu_done"), 1)
            v.wait_ge(sem("uu_done"), NGRP)
            v.wait_ge(sem("t_done"), 5 * NGRP)
            for n in range(2 * HALVES):
                h, r = n // 2, CHUNK * (n % 2)
                rows = slice(r, r + CHUNK)
                for b in range(2):
                    j = slice(HEADS * h + HD * b, HEADS * h + HD * b + HD)
                    if n == 0:
                        v.tensor_copy(vnew[rows, j, :], uu[rows, j, :]).then_inc(sem("vnew_done"), 1)
                    else:
                        v.wait_ge(sem("ws_ps"), 2 * (n - 1) + b + 1)
                        v.tensor_tensor(vnew[rows, j, :], uu[rows, j, :], bank3(b)[rows], ALU.subtract).then_inc(sem("vnew_done"), 1)
                for b in range(2):
                    j = slice(HEADS * h + HD * b, HEADS * h + HD * b + HD)
                    if n == 0:
                        v.memset(o_rows[rows, j, :], 0.0).then_inc(sem("o1_done"), 1)
                    else:
                        v.wait_ge(sem("qs_ps"), 2 * (n - 1) + b + 1)
                        v.tensor_tensor(o_rows[rows, j, :], bank3(2 + b)[rows], bc(eg[rows, h, HD * b:HD * b + HD], 2, P),
                                        ALU.mult).then_inc(sem("o1_done"), 1)
                if n < 2 * HALVES - 1:
                    for e in range(HEADS):
                        if e % HD == 0:
                            v.wait_ge(sem("ds_ps"), 2 * n + e // HD + 1)
                        src = bank[4 + e // HD][:, (e % HD) * P:(e % HD + 1) * P]
                        if n == 0:
                            ins = v.tensor_copy(S[:, e, :], src)
                        else:
                            v.wait_ge(sem("state_done"), HEADS * (n - 1) + e + 1)
                            ins = v.scalar_tensor_tensor(S[:, e, :], S[:, e, :], s_scale[:, n, e:e + 1], src, ALU.mult, ALU.add)
                        ins.then_inc(sem("state_done"), 1)
                if n % 2 == 1:
                    v.wait_ge(sem("o1_done"), 2 * (n + 1))
                    for b in range(2):
                        j = slice(HEADS * h + HD * b, HEADS * h + HD * b + HD)
                        v.wait_ge(sem("oi_ps"), 2 * h + b + 1)
                        v.tensor_tensor(o_rows[:, j, :], o_rows[:, j, :], bank3(6 + b), ALU.add).then_inc(sem("o_sum"), 1)
            v.wait_ge(sem("o_sum"), 4)
            v.wait_ge(sem("z_done"), 4)
            osq = Wm
            dve_link(v, v.tensor_tensor(osq[:, :, :], o_rows[:, :, :], o_rows[:, :, :], ALU.mult))
            omsf = oms.rearrange("p a b -> p (a b)")
            off = of.rearrange("p a b -> p (a b)")
            rqf = rq_s.rearrange("p a b -> p (a b)")
            dve_link(v, v.tensor_reduce(omsf, osq[:, :, :], AX.X, ALU.add))
            dve_link(v, v.tensor_tensor(omsf, omsf, rqf, ALU.mult))
            dve_link(v, v.tensor_tensor(omsf, omsf, rqf, ALU.mult))
            dve_link(v, v.tensor_scalar(omsf, omsf, 1.0 / P, NORM_EPS, ALU.mult, ALU.add))
            v.reciprocal(off, omsf).then_inc(sem("oms_inv"), 1)
            v.wait_ge(sem("of_done"), 1)
            dve_link(v, v.tensor_tensor(off, off, rqf, ALU.mult))
            for h in range(HALVES):
                o_h = o_rows[:, HEADS * h:HEADS * (h + 1), :]
                dve_link(v, v.tensor_tensor(o_h, o_h, bc(of[:, h, :], 2, P), ALU.mult))
                dve_link(v, v.tensor_tensor(o_h, o_h, bc(norm_g, 1, HEADS), ALU.mult))
                v.tensor_tensor(o_h, o_h, zs[:, h, :].rearrange("p (e d) -> p e d", e=HEADS), ALU.mult)\
                 .then_inc(sem("o_gated"), 1)
            for j in range(2):
                for h in range(HALVES):
                    v.wait_ge(sem("wout_ps"), 2 * j + h + 1)
                    xs = xres[:, h, 512 * j:512 * j + 512]
                    ins = v.scalar_tensor_tensor(xs, xs, ALPHA, bank[4 + 2 * j + h][:, :], ALU.mult, ALU.add)
            dve_link(v, ins)
            norm_vector(v, 0, xres, xres)

        def gdn_gpsimd(g):
            g.memset(raw[:, :, 0:TAPS - 1], 0.0).then_inc(sem("pad_done"), 1)
            for c in range(2 * HEADS):
                g.wait_ge(sem("silu_done"), c + 1)
                g.tensor_tensor(sq[c // HEADS][:, c % HEADS, :], qkvT[:, c, :], qkvT[:, c, :], ALU.mult)\
                 .then_inc(sem("sq_done"), 1)

        def load_norm(eng, n):
            eng.dma_start(lnp[:, 0, :], I["ln_rows"][n, 0]).then_inc(sem("lnp_loaded"), 16)
            eng.dma_start(lnp[:, 1, :], I["ln_rows"][n, 1]).then_inc(sem("lnp_loaded"), 16)

        fw = Carver(work, 0, WORK)
        bt = fw(DC, 4, P)
        y0re = fw(PAIRS, 32)
        y0im = fw(PAIRS, 32)
        y1re = fw(PAIRS, 32)
        y1im = fw(PAIRS, 32)
        k0 = fw(DC, P)
        s5_phase_at = fw.at
        cosT = fw(PAIRS, NSTEP)
        sinT = fw(PAIRS, NSTEP)
        uT = fw(DC, SEQ)
        s5_hid = fw(DC, SEQ)
        rot_r, rot_i, pw_r, pw_i, decay2 = (fw(PAIRS) for _ in range(5))
        s5_tmp_at = fw.at
        NP2 = DC * S5_STATE + PAIRS
        fp = Carver(work, s5_tmp_at, WORK)
        lam_re, lam_im, dt, lr, th, rho, kk_, sn, ar, ai, t0, t1 = (fp(NP2) for _ in range(12))
        bbar_r, bbar_i = fp(PAIRS, 32), fp(PAIRS, 32)
        cc_ = Carver(work, s5_phase_at, s5_phase_at + 2 * PAIRS * NSTEP)
        b1_re, b1_im, m1 = cc_(PAIRS, 32), cc_(PAIRS, 32), cc_(PAIRS, 32)
        b2_re, b2_im, br_, bi_, m2, abr, abi = (cc_(DC, S5_STATE) for _ in range(7))
        ff_hid = [uT[:, 4 * i:4 * i + 4, :] for i in range(2)]
        ff_silu = [s5_hid[:, i, :] for i in range(2)]
        NCH = 2 * sum(FF_BLOCKS)
        TWO_PI = 2 * np.pi
        C1 = float(np.float32(6.28125))
        C2 = float(np.float32(TWO_PI - C1))
        C2 = float(np.frombuffer((np.frombuffer(np.float32(C2).tobytes(), np.uint32) & 0xFFFFF000).tobytes(), np.float32)[0])
        C3 = float(np.float32(TWO_PI - C1 - C2))
        MAGIC = 1.5 * 2.0 ** 23
        PI_LO = float(np.nextafter(np.float32(np.pi), np.float32(0)))
        LOADS_S5 = 9

        def ffn_tensor(pe):
            f = 0
            for e in range(2):
                for b, nch in enumerate(FF_BLOCKS):
                    u = U_FFN + 9 * e + 3 * b
                    unit_ready(pe, u)
                    unit_ready(pe, u + 1)
                    w1, w3 = (slot(u + i)[:, 0:DC * nch * P].rearrange("p (k n) -> p k n", k=DC) for i in range(2))
                    for c in range(nch):
                        for k in range(DC):
                            mm(bank[4 + c][:, 0:SEQ], w1[:, k, c * P:(c + 1) * P], xT[:, k, :], k == 0, k == DC - 1)
                        for k in range(DC):
                            ins = mm(bank[4 + c][:, SEQ:], w3[:, k, c * P:(c + 1) * P], xT[:, k, :], k == 0, k == DC - 1)
                        ins.then_inc(sem("ffn_up"), 1)
                    unit_ready(pe, u + 2)
                    w2 = slot(u + 2)[:, 0:nch * D].rearrange("p (c n) -> p c n", c=nch)
                    for c in range(nch):
                        f += 1
                        pe.wait_ge(sem("ffn_hid"), f)
                        for h in range(HALVES):
                            for j in range(2):
                                ins = mm(bank[2 * h + j][:, :], ff_hid[(3 * e + b) % 2][:, c, h * P:(h + 1) * P],
                                         w2[:, c, 512 * j:512 * j + 512], f == 1, f == NCH)
                    ins.then_inc(sem("ffn_dn"), 1)

        def ffn_scalar(act):
            load_norm(act, 1)
            for name, dst in (("lam_re", lam_re), ("lam_im", lam_im), ("log_dt", dt), ("c_re", y0re), ("c_im", y0im),
                              ("b1_re", b1_re), ("b1_im", b1_im), ("b2_re", b2_re), ("b2_im", b2_im)):
                act.dma_start(dst, I[name]).then_inc(sem("s5_loaded"), 16)
            act.wait_ge(sem("s5_loaded"), 16 * LOADS_S5)
            act.activation(dt, dt, ACT.Exp).then_inc(sem("s5_dt"), 1)
            act.wait_ge(sem("s5_lr"), 1)
            act.activation(rho, lr, ACT.Exp).then_inc(sem("s5_rho"), 1)
            act.wait_ge(sem("s5_theta"), 1)
            act.activation(sn, th, ACT.Sin).then_inc(sem("s5_sin"), 1)
            act.activation(t0, th, ACT.Sin, scale=0.5).then_inc(sem("s5_sin"), 1)
            for f in range(NCH):
                b, c = ff_block(f)
                act.wait_ge(sem("ffn_up"), f + 1)
                if f >= 2:
                    act.wait_ge(sem("ffn_hid"), f - 1)
                act.activation(ff_silu[f % 2], bank[4 + c][:, 0:SEQ], ACT.Silu).then_inc(sem("ffn_silu"), 1)
            norm_scalar(act, 1)
            turn_evacuate(act, 1, None)

        def ff_block(f):
            e, r = divmod(f, sum(FF_BLOCKS))
            b = 0
            while r >= FF_BLOCKS[b]:
                r -= FF_BLOCKS[b]
                b += 1
            return 3 * e + b, r

        def ffn_vector(v):
            v.wait_ge(sem("s5_dt"), 1)
            v.tensor_tensor(lr, lam_re, dt, ALU.mult).then_inc(sem("s5_lr"), 1)
            v.tensor_scalar(y0im[:, :, :], y0im[:, :, :], -1.0, None, ALU.mult).then_inc(sem("c_negated"), 1)
            dve_link(v, v.tensor_tensor(th, lam_im, dt, ALU.mult))
            dve_link(v, v.tensor_scalar(kk_, th, 1.0 / TWO_PI, MAGIC, ALU.mult, ALU.add))
            dve_link(v, v.tensor_scalar(kk_, kk_, MAGIC, None, ALU.subtract))
            for c in (C1, C2, C3):
                dve_link(v, v.scalar_tensor_tensor(th, kk_, -c, th, ALU.mult, ALU.add))
            v.tensor_scalar(th, th, PI_LO, -PI_LO, ALU.min, ALU.max).then_inc(sem("s5_theta"), 1)
            dve_link(v, v.tensor_tensor(kk_, lam_re, lam_re, ALU.mult))
            dve_link(v, v.tensor_tensor(t1, lam_im, lam_im, ALU.mult))
            dve_link(v, v.tensor_tensor(kk_, kk_, t1, ALU.add))
            dve_link(v, v.reciprocal(kk_, kk_))
            v.wait_ge(sem("s5_sin"), 2)
            v.wait_ge(sem("s5_rho"), 1)
            dve_link(v, v.tensor_tensor(t0, t0, t0, ALU.mult))
            dve_link(v, v.tensor_scalar(t0, t0, -2.0, 1.0, ALU.mult, ALU.add))
            st = slice(DC * S5_STATE, NP2)
            dve_link(v, v.tensor_tensor(t1[:, st], t0[:, st], t0[:, st], ALU.mult))
            dve_link(v, v.tensor_tensor(rot_r, sn[:, st], sn[:, st], ALU.mult))
            dve_link(v, v.tensor_tensor(rot_r, t1[:, st], rot_r, ALU.subtract))
            dve_link(v, v.tensor_tensor(t1[:, st], t0[:, st], sn[:, st], ALU.mult))
            dve_link(v, v.tensor_scalar(rot_i, t1[:, st], 2.0, None, ALU.mult))
            dve_link(v, v.tensor_tensor(decay2, rho[:, st], rho[:, st], ALU.mult))
            dve_link(v, v.tensor_tensor(ar, rho, t0, ALU.mult))
            dve_link(v, v.tensor_tensor(ai, rho, sn, ALU.mult))
            dve_link(v, v.tensor_scalar(t0, ar, 1.0, None, ALU.subtract))
            dve_link(v, v.tensor_tensor(rho, t0, lam_re, ALU.mult))
            dve_link(v, v.tensor_tensor(t1, ai, lam_im, ALU.mult))
            dve_link(v, v.tensor_tensor(rho, rho, t1, ALU.add))
            dve_link(v, v.tensor_tensor(sn, ai, lam_re, ALU.mult))
            dve_link(v, v.tensor_tensor(t1, t0, lam_im, ALU.mult))
            dve_link(v, v.tensor_tensor(sn, sn, t1, ALU.subtract))
            v.tensor_tensor(rho, rho, kk_, ALU.mult).then_inc(sem("s5_coef"), 1)
            v.tensor_tensor(sn, sn, kk_, ALU.mult).then_inc(sem("s5_coef"), 1)
            for f in range(NCH):
                b, c = ff_block(f)
                v.wait_ge(sem("ffn_silu"), f + 1)
                if b >= 2:
                    v.wait_ge(sem("ffn_dn"), b - 1)
                v.tensor_tensor(ff_hid[b % 2][:, c, :], ff_silu[f % 2], bank[4 + c][:, SEQ:], ALU.mult)\
                 .then_inc(sem("ffn_hid"), 1)
            v.wait_ge(sem("ffn_dn"), 2 * len(FF_BLOCKS))
            for h in range(HALVES):
                for j in range(2):
                    xs = xres[:, h, 512 * j:512 * j + 512]
                    ins = v.scalar_tensor_tensor(xs, xs, ALPHA, bank[2 * h + j][:, :], ALU.mult, ALU.add)
            dve_link(v, ins)
            norm_vector(v, 1, xres, xres)

        def cmul(g, o_r, o_i, a_r, a_i, b_r, b_i, tmp, conj=False):
            g.tensor_tensor(o_r, a_r, b_r, ALU.mult)
            pool_link(g, g.tensor_tensor(tmp, a_i, b_i, ALU.mult))
            pool_link(g, g.tensor_tensor(o_r, o_r, tmp, ALU.add if conj else ALU.subtract))
            g.tensor_tensor(o_i, a_r, b_i, ALU.mult)
            pool_link(g, g.tensor_tensor(tmp, a_i, b_r, ALU.mult))
            pool_link(g, g.tensor_tensor(o_i, o_i, tmp, ALU.add))

        def ffn_gpsimd(g):
            g.wait_ge(sem("s5_coef"), 2)
            l2 = slice(0, DC * S5_STATE)
            l1 = slice(DC * S5_STATE, NP2)

            def rows2(t):
                return t[:, l2].rearrange("p (q s) -> p q s", q=DC)

            def st1(t):
                return bc(t[:, l1], 2, 32)

            cmul(g, bbar_r, bbar_i, b1_re, b1_im, st1(rho), st1(sn), m1)
            cmul(g, br_, bi_, b2_re, b2_im, rows2(rho), rows2(sn), m2)
            cmul(g, abr, abi, br_, bi_, rows2(ar), rows2(ai), m2)
            for j, t in enumerate((abr, abi, br_, bi_)):
                for g2 in range(2):
                    pool_link(g, g.tensor_tensor(
                        bt[:, :, j, S5_STATE * g2:S5_STATE * (g2 + 1)], t[:, :, :],
                        half_mask[:, g2:g2 + 1].unsqueeze(2).to_broadcast([P, DC, S5_STATE]), ALU.mult))
            g.wait_ge(sem("c_negated"), 1)
            pool_link(g, g.tensor_tensor(m1[:, :, :], y0im[:, :, :], st1(ai), ALU.mult))
            pool_link(g, g.tensor_tensor(y1re[:, :, :], y0re[:, :, :], st1(ar), ALU.mult))
            pool_link(g, g.tensor_tensor(y1re[:, :, :], y1re[:, :, :], m1[:, :, :], ALU.add))
            pool_link(g, g.tensor_tensor(m1[:, :, :], y0re[:, :, :], st1(ai), ALU.mult))
            pool_link(g, g.tensor_tensor(y1im[:, :, :], y0im[:, :, :], st1(ar), ALU.mult))
            pool_link(g, g.tensor_tensor(y1im[:, :, :], y1im[:, :, :], m1[:, :, :], ALU.subtract))
            g.memset(cosT[:, :, 0:1], 1.0)
            g.memset(sinT[:, :, 0:1], 0.0)
            g.tensor_copy(cosT[:, :, 1:2], rot_r.unsqueeze(2))
            g.tensor_copy(sinT[:, :, 1:2], rot_i.unsqueeze(2))
            g.tensor_copy(pw_r, rot_r)
            pool_link(g, g.tensor_copy(pw_i, rot_i))
            m = 2
            while m < NSTEP:
                sq_t = t0[:, 0:PAIRS]
                pool_link(g, g.tensor_tensor(sq_t, pw_i, pw_i, ALU.mult))
                pool_link(g, g.tensor_tensor(pw_i, pw_r, pw_i, ALU.mult))
                pool_link(g, g.tensor_tensor(pw_i, pw_i, pw_i, ALU.add))
                pool_link(g, g.tensor_tensor(pw_r, pw_r, pw_r, ALU.mult))
                pool_link(g, g.tensor_tensor(pw_r, pw_r, sq_t, ALU.subtract))
                tmp = work[:, s5_tmp_at:s5_tmp_at + PAIRS * m].rearrange("p (a m) -> p a m", a=PAIRS)
                cmul(g, cosT[:, :, m:2 * m], sinT[:, :, m:2 * m], cosT[:, :, 0:m], sinT[:, :, 0:m],
                     bc(pw_r, 2, m), bc(pw_i, 2, m), tmp)
                m *= 2

        ft = Carver(work, s5_tmp_at, WORK)
        rotb = [ft(8, PAIRS // DC, NSTEP) for _ in range(2)]
        s5_y = [ft(SEQ) for _ in range(2)]
        glu_s = rotb[0].rearrange("p a b c -> p (a b c)")[:, 0:1024].rearrange("p (h n) -> p h n", h=HALVES)
        glu_t = rotb[1].rearrange("p a b c -> p (a b c)")[:, 0:512]
        PQ = PAIRS // DC

        def s5_in():
            return psum[:, 2:2 + PQ, 0:2 * NSTEP].rearrange("p i (r t) -> p i r t", r=2)

        def s5_tensor(pe):
            for q in range(DC):
                o = bank[6 + q // 4][:, (q % 4) * P:(q % 4 + 1) * P]

                def flat(t):
                    return t[:, PQ * q:PQ * (q + 1), :].rearrange("p a b -> p (a b)")
                mm(o, flat(bbar_r), flat(y0re), True, False)
                ins = mm(o, flat(bbar_i), flat(y0im), False, True)
                if q % 4 == 3:
                    ins.then_inc(sem("k0_ps"), 1)
            for c in range(DC):
                if c % 4 == 0:
                    unit_ready(pe, U_S5IN + c // 4)
                if c >= 2:
                    pe.wait_ge(sem("s5_u_done"), c - 1)
                w = slot(U_S5IN + c // 4).rearrange("p (k n) -> p k n", k=DC)
                for k in range(DC):
                    ins = mm(bank[c % 2][:, 0:SEQ], w[:, k, (c % 4) * P:(c % 4 + 1) * P], xT[:, k, :], k == 0, k == DC - 1)
                ins.then_inc(sem("u_ps"), 1)
            pe.wait_ge(sem("k0_done"), 2)
            for q in range(DC + 2):
                if q < DC:
                    pe.wait_ge(sem("s5_u_done"), q + 1)
                    if q >= 1:
                        pe.wait_ge(sem("s5_pre"), q)
                    for i in range(PQ):
                        r = slice(32 * i, 32 * i + 32)
                        for ri in range(2):
                            for s in range(STEP):
                                ins = mm(s5_in()[:, i, ri, :],
                                         bt[r, q, 2 * s + ri, :], uT[r, q, s::STEP], s == 0, s == STEP - 1)
                    ins.then_inc(sem("s5_in_ps"), 1)
                if q >= 2:
                    z = q - 2
                    if z >= 2:
                        pe.wait_ge(sem("s5_y_done"), z - 1)
                    yb = bank[6 + z % 2][:, 0:SEQ].rearrange("p (n s) -> p n s", s=STEP)
                    hre, him = rotb[z % 2][:, 4, :, :], rotb[z % 2][:, 6, :, :]
                    mm(yb[:, :, 0], k0[:, z, :], uT[:, z, 0::STEP], True, False, skip_group_check=True)
                    pe.wait_ge(sem("s5_h"), 2 * (z + 1))
                    for i in range(PQ):
                        r = slice(32 * i, 32 * i + 32)
                        pr = PQ * z + i
                        for y0, y1, hh in ((y0re, y1re, hre), (y0im, y1im, him)):
                            mm(yb[r, :, 1], y0[:, pr, :], hh[:, i, :], False, False, skip_group_check=True)
                            ins = mm(yb[r, 1:, 0], y1[:, pr, :], hh[:, i, 0:NSTEP - 1], False, True, skip_group_check=True)
                    ins.then_inc(sem("s5_y_ps"), 1)
            pe.wait_ge(sem("s5_gelu"), DC)
            for j in range(4):
                unit_ready(pe, U_GLU + j)
                w = slot(U_GLU + j).rearrange("p (k n) -> p k n", k=DC)
                for h in range(HALVES):
                    for k in range(DC):
                        ins = mm(bank[2 * j + h][:, :], s5_hid[:, k, h * P:(h + 1) * P], w[:, k, :], k == 0, k == DC - 1)
                    ins.then_inc(sem("glu_ps"), 1)

        def s5_scalar(act):
            load_norm(act, 2)
            for c in range(DC):
                act.wait_ge(sem("u_ps"), c + 1)
                act.activation(uT[:, c, :], bank[c % 2][:, 0:SEQ], ACT.Copy).then_inc(sem("s5_u_done"), 1)
            for q in range(DC):
                act.wait_ge(sem("s5_y_done"), q + 1)
                act.activation(s5_hid[:, q, :], s5_y[q % 2], ACT.Gelu).then_inc(sem("s5_gelu"), 1)
            for j in range(2):
                for h in range(HALVES):
                    act.wait_ge(sem("glu_ps"), 4 * j + 2 + h + 1)
                    if j > 0:
                        act.wait_ge(sem("glu_done"), h + 1)
                    act.activation(glu_s[:, h, :], bank[4 * j + 2 + h][:, :], ACT.Sigmoid).then_inc(sem("glu_sig"), 1)
            norm_scalar(act, 2)
            turn_evacuate(act, 2, None)

        def s5_vector(v):
            for i in range(2):
                v.wait_ge(sem("k0_ps"), i + 1)
                v.tensor_tensor(k0[:, 4 * i:4 * i + 4, :], bank[6 + i][:, :].rearrange("p (q c) -> p q c", q=4),
                                bc(blk32, 1, 4), ALU.mult).then_inc(sem("k0_done"), 1)
            for q in range(DC + 1):
                if q < DC:
                    B = rotb[q % 2]
                    v_re, v_im = s5_in()[:, :, 0, :], s5_in()[:, :, 1, :]
                    cq, sq_ = cosT[:, PQ * q:PQ * (q + 1), :], sinT[:, PQ * q:PQ * (q + 1), :]
                    v.wait_ge(sem("s5_in_ps"), q + 1)
                    if q >= 2:
                        v.wait_ge(sem("s5_y_ps"), q - 1)
                    v.tensor_tensor(B[:, 0], v_re, cq, ALU.mult)
                    v.tensor_tensor(B[:, 1], v_im, sq_, ALU.mult)
                    v.tensor_tensor(B[:, 2], v_im, cq, ALU.mult)
                    v.tensor_tensor(B[:, 3], v_re, sq_, ALU.mult).then_inc(sem("s5_pre"), 1)
                if q >= 1:
                    z = q - 1
                    B = rotb[z % 2]
                    cq, sq_ = cosT[:, PQ * z:PQ * (z + 1), :], sinT[:, PQ * z:PQ * (z + 1), :]
                    v.wait_ge(sem("s5_scan"), z + 1)
                    v.tensor_tensor(B[:, 4], B[:, 1], cq, ALU.mult)
                    v.tensor_tensor(B[:, 5], B[:, 3], sq_, ALU.mult)
                    v.tensor_tensor(B[:, 6], B[:, 1], sq_, ALU.mult)
                    v.tensor_tensor(B[:, 7], B[:, 3], cq, ALU.mult).then_inc(sem("s5_post"), 1)
                if q < DC:
                    B = rotb[q % 2]
                    v.wait_ge(sem("s5_turned"), 2 * (q + 1))
                    for i in range(PQ):
                        dec = decay2[:, PQ * q + i:PQ * q + i + 1].to_broadcast([P, NSTEP])
                        v.tensor_tensor_scan(B[:, 1, i, :], dec, B[:, 0, i, :], 0.0, ALU.mult, ALU.add)
                        ins = v.tensor_tensor_scan(B[:, 3, i, :], dec, B[:, 2, i, :], 0.0, ALU.mult, ALU.add)
                    ins.then_inc(sem("s5_scan"), 1)
                if q >= 2:
                    s5_out(v, q - 2)
            s5_out(v, DC - 1)
            for j in range(2):
                for h in range(HALVES):
                    v.wait_ge(sem("glu_sig"), 2 * j + h + 1)
                    dve_link(v, v.tensor_tensor(glu_t, glu_s[:, h, :], bank[4 * j + h][:, :], ALU.mult))
                    xs = xres[:, h, 512 * j:512 * j + 512]
                    v.scalar_tensor_tensor(xs, xs, ALPHA, glu_t, ALU.mult, ALU.add).then_inc(sem("glu_done"), 1)
                    v.wait_ge(sem("glu_done"), 2 * j + h + 1)
            norm_vector(v, 2, xres, xres)

        def s5_out(v, z):
            v.wait_ge(sem("s5_y_ps"), z + 1)
            if z >= 2:
                v.wait_ge(sem("s5_gelu"), z - 1)
            v.scalar_tensor_tensor(s5_y[z % 2], uT[:, z, :], s5_d[:, z:z + 1], bank[6 + z % 2][:, 0:SEQ], ALU.mult, ALU.add)\
             .then_inc(sem("s5_y_done"), 1)

        def s5_gpsimd(g):
            for q in range(DC + 1):
                if q < DC:
                    B = rotb[q % 2]
                    g.wait_ge(sem("s5_pre"), q + 1)
                    g.tensor_tensor(B[:, 0], B[:, 0], B[:, 1], ALU.add).then_inc(sem("s5_turned"), 1)
                    g.tensor_tensor(B[:, 2], B[:, 2], B[:, 3], ALU.subtract).then_inc(sem("s5_turned"), 1)
                if q >= 1:
                    B = rotb[(q - 1) % 2]
                    g.wait_ge(sem("s5_post"), q)
                    g.tensor_tensor(B[:, 4], B[:, 4], B[:, 5], ALU.subtract).then_inc(sem("s5_h"), 1)
                    g.tensor_tensor(B[:, 6], B[:, 6], B[:, 7], ALU.add).then_inc(sem("s5_h"), 1)

        ew = Carver(work, 0, WORK)
        xeT = ew(DC, P)
        sel = ew(HALVES, P)
        selg = ew(HALVES, P)
        selT = ew(SEQ)
        e_silu = [ew(512) for _ in range(2)]
        e_hid = ew(512)
        e_hidT = ew(4, P)
        e_out = ew(D)
        yacc = ew(HALVES, D)
        xn = ew(HALVES, D)
        lg = ew(HALVES, 40)
        lgE = ew(HALVES, 8)
        top = ew(HALVES, 8)
        topi = ew(HALVES, 8)
        oh = ew(2, HALVES, 8)
        gw = ew(HALVES, 8)
        ohG = ew(HALVES, 4)
        gexp = ew(HALVES, 4)
        mask1, comb1 = ew(HALVES, EXPERTS), ew(HALVES, EXPERTS)
        rank1 = ew(EXPERTS + 1, HALVES)
        gate1 = ew(EXPERTS + 1, HALVES)
        mask2, comb2 = ew(HALVES, EXPERTS2), ew(HALVES, EXPERTS2)
        rank2 = ew(PACKS + 1, HALVES, PACK)
        gate2 = ew(PACKS + 1, HALVES, PACK)
        cnt = ew(EXPERTS2)
        w_r1, b_r1 = ew(DC, EXPERTS), ew(EXPERTS)
        w_r2, b_r2 = ew(DC, 36), ew(36)
        iota_over = ew(P)
        moe_end = ew.at
        idx_u = sb("idx_u", [P, HALVES, 8], U32)

        def rank_tensor(pe, n, mask, ne):
            pe.wait_ge(sem("mask_ready"), n + 1)
            mm(bank[0][:, 0:ne], before, mask[:, 0, :])
            mm(bank[0][:, ne:2 * ne], ones, mask[:, 0, :], True, False)
            mm(bank[0][:, ne:2 * ne], before, mask[:, 1, :], False, True)
            mm(bank[1][:, 0:ne], ones, mask[:, 0, :], True, False)
            mm(bank[1][:, 0:ne], ones, mask[:, 1, :], False, True).then_inc(sem("rank_ps"), 1)

        def top2_vector(v, n, src, k, wmul):
            for h in range(HALVES):
                dve_link(v, v.max(top[:, h, :], src[:, h, :]))
                dve_link(v, v.max_index(idx_u[:, h, :], top[:, h, :], src[:, h, :]))
            dve_link(v, v.tensor_copy(topi[:, :, :], idx_u[:, :, :]))
            v.tensor_tensor(gw[:, :, 0:1], top[:, :, 1:2], top[:, :, 0:1], ALU.subtract).then_inc(sem("top_diff"), 1)
            for i in range(2):
                for h in range(HALVES):
                    ins = v.tensor_scalar(oh[:, i, h, :], iota[:, 0:8], topi[:, h, i:i + 1], None, ALU.is_equal)
            dve_link(v, ins)
            v.wait_ge(sem("top_exp"), n + 1)
            dve_link(v, v.tensor_scalar(gw[:, :, 2:3], gw[:, :, 1:2], 1.0, None, ALU.add))
            dve_link(v, v.reciprocal(gw[:, :, 2:3], gw[:, :, 2:3]))
            if wmul is not None:
                dve_link(v, v.tensor_tensor(gw[:, :, 2:3], gw[:, :, 2:3], wmul, ALU.mult))
            dve_link(v, v.tensor_tensor(gw[:, :, 3:4], gw[:, :, 2:3], gw[:, :, 1:2], ALU.mult))

        def top2_scalar(act, n):
            act.wait_ge(sem("top_diff"), n + 1)
            act.activation(gw[:, :, 1:2], gw[:, :, 0:1], ACT.Exp).then_inc(sem("top_exp"), 1)

        def combine_tensor(pe, step, waits):
            for i in range(4):
                waits(i)
                mm(bank[6 + i % 2][:, :], selT[:, P * (i // 2):P * (i // 2) + P], e_out[:, 512 * (i % 2):512 * (i % 2) + 512])\
                    .then_inc(step, 1)

        def dispatch_tensor(pe, step, x, first, waits):
            for i in range(2):
                waits(i)
                for c in range(4):
                    for h in range(HALVES):
                        ins = mm(bank[first if i == 0 else 13 - first][:, c * P:(c + 1) * P],
                                 x[:, h, (4 * i + c) * P:(4 * i + c + 1) * P], sel[:, h, :], h == 0, h == HALVES - 1)
                ins.then_inc(step, 1)

        def seltrans_tensor(pe, step, b):
            for h in range(HALVES):
                ins = pe.transpose(bank[b][:, P * h:P * (h + 1)], selg[:, h, :], ident)
            ins.then_inc(step, 1)

        FIRST_PE, FIRST_ACT, FIRST_DVE = 2, 4, 4
        M1_PE = Order(FIRST_PE, ["g0", "c0", "c1", "c2", "c3", "u0", "g1", "t0", "d0", "u1", "g2", "t1", "d1", "u2", "st", "x0", "x1", "t2", "d2"])
        M1_ACT = Order(FIRST_ACT, ["s0", "s1", "s2", "st", "x0", "x1", "y0", "y1"])
        M1_DVE = Order(FIRST_DVE, ["sg0", "sg1", "s0", "s1", "c0", "c1", "c2", "c3", "h0", "t0", "h1", "t1", "h2", "t2"])
        M1_UNIT_STEP = ["g0", "u0", "g1", "d0", "u1", "g2", "d1", "u2", "d2"]
        PE1, ACT1, DVE1 = len(M1_PE.names), len(M1_ACT.names), len(M1_DVE.names)

        def at(order, it, name, back=0):
            return it * len(order.names) + (order.first + order.names.index(name) + 1 - back * len(order.names))

        def moe1_tensor(pe):
            for h in range(HALVES):
                for k in range(DC):
                    if h == 0 and k == 0:
                        pe.wait_ge(sem("router_loaded"), 64)
                    ins = mm(bank[0][:, EXPERTS * h:EXPERTS * (h + 1)], xT[:, k, h * P:(h + 1) * P], w_r1[:, k, :],
                             k == 0, k == DC - 1)
            ins.then_inc(sem("logits_ps"), 1)
            rank_tensor(pe, 0, mask1, EXPERTS)
            step, actd, dved = sem("m1_pe"), sem("m1_act"), sem("m1_dve")
            pe.wait_ge(dved, FIRST_DVE)
            dispatch_tensor(pe, step, xres, 7, lambda i: None)
            with pe.Fori(0, EXPERTS) as it:
                def unit(j):
                    unit_ready_it(pe, U_MOE1 + j, it, UNITS_EXPERT)
                    return slot(U_MOE1 + j)

                def up(b, j, o, name):
                    n = FF_BLOCKS[b] * P
                    w = unit(j)[:, 0:DC * n].rearrange("p (k n) -> p k n", k=DC)
                    for k in range(DC):
                        ins = mm(o[:, 0:n], xeT[:, k, :], w[:, k, :], k == 0, k == DC - 1)
                    ins.then_inc(step, 1)

                def turn(b, o):
                    pe.wait_ge(dved, at(M1_DVE, it, f"h{b}"))
                    for c in range(FF_BLOCKS[b]):
                        ins = pe.transpose(o[:, c * P:(c + 1) * P], e_hid[:, c * P:(c + 1) * P], ident)
                    ins.then_inc(step, 1)

                def down(b, j):
                    w = unit(j)[:, 0:FF_BLOCKS[b] * D].rearrange("p (c n) -> p c n", n=D)
                    pe.wait_ge(dved, at(M1_DVE, it, f"t{b}"))
                    for c in range(FF_BLOCKS[b]):
                        for n in range(2):
                            ins = mm(bank[4 + n][:, :], e_hidT[:, c, :], w[:, c, 512 * n:512 * n + 512],
                                     b == 0 and c == 0, b == 2 and c == FF_BLOCKS[2] - 1)
                    ins.then_inc(step, 1)

                pe.wait_ge(actd, at(M1_ACT, it, "x1", 1))
                up(0, 0, bank[0], "g0")

                def combine_waits(i):
                    if i == 0:
                        pe.wait_ge(actd, at(M1_ACT, it, "y1", 1))
                    if i >= 2:
                        pe.wait_ge(dved, at(M1_DVE, it, f"c{i - 2}"))
                combine_tensor(pe, step, combine_waits)
                up(0, 1, bank[1], "u0")
                up(1, 2, bank[2], "g1")
                pe.wait_ge(dved, at(M1_DVE, it, "c2"))
                turn(0, bank[6])
                down(0, 3)
                up(1, 4, bank[3], "u1")
                up(2, 5, bank[0], "g2")
                turn(1, bank[7])
                down(1, 6)
                up(2, 7, bank[1], "u2")
                pe.wait_ge(dved, at(M1_DVE, it, "sg1"))
                seltrans_tensor(pe, step, 6)
                pe.wait_ge(dved, at(M1_DVE, it, "s1"))

                def dispatch_waits(i):
                    if i == 1:
                        pe.wait_ge(actd, at(M1_ACT, it, "st"))
                dispatch_tensor(pe, step, xres, 7, dispatch_waits)
                pe.wait_ge(actd, at(M1_ACT, it, "x0"))
                turn(2, bank[7])
                down(2, 8)
            pe.wait_ge(actd, at(M1_ACT, EXPERTS, "y1", 1))

            def last_waits(i):
                if i >= 2:
                    pe.wait_ge(dved, FIRST_DVE + EXPERTS * DVE1 + i - 1)
            combine_tensor(pe, step, last_waits)

        def moe1_scalar(act):
            load_norm(act, 3)
            for name, dst in (("w_r1", w_r1), ("b_r1", b_r1), ("w_r2", w_r2), ("b_r2", b_r2)):
                act.dma_start(dst, I[name]).then_inc(sem("router_loaded"), 16)
            top2_scalar(act, 0)
            step, ped, dved = sem("m1_act"), sem("m1_pe"), sem("m1_dve")
            for i in range(2):
                act.wait_ge(ped, i + 1)
                act.activation(xeT[:, 4 * i:4 * i + 4, :], bank3(7 - i), ACT.Copy).then_inc(step, 1)
            act.wait_ge(step, 2)
            zero_scalar(act, step)
            with act.Fori(0, EXPERTS) as it:
                for b in range(3):
                    n = FF_BLOCKS[b] * P
                    act.wait_ge(ped, at(M1_PE, it, f"g{b}"))
                    act.wait_ge(dved, at(M1_DVE, it, f"h{(b - 2) % 3}", 1 if b < 2 else 0))
                    act.activation(e_silu[b % 2][:, 0:n], bank[2 * (b % 2)][:, 0:n], ACT.Silu).then_inc(step, 1)
                act.wait_ge(ped, at(M1_PE, it, "st"))
                act.activation(selT, bank[6][:, 0:SEQ], ACT.Copy).then_inc(step, 1)
                for i in range(2):
                    act.wait_ge(ped, at(M1_PE, it, f"x{i}"))
                    act.activation(xeT[:, 4 * i:4 * i + 4, :], bank3(7 - i), ACT.Copy).then_inc(step, 1)
                act.wait_ge(ped, at(M1_PE, it, "d2"))
                for i in range(2):
                    act.activation(e_out[:, 512 * i:512 * i + 512], bank[4 + i][:, :], ACT.Copy).then_inc(step, 1)

        def zero_vector(v, step):
            v.memset(selT, 0.0).then_inc(step, 1)
            v.memset(yacc[:, :, :], 0.0).then_inc(step, 1)

        def zero_scalar(act, step):
            for i in range(2):
                act.activation(e_out[:, 512 * i:512 * i + 512], xeT[:, 4 * i:4 * i + 4, :].rearrange("p c s -> p (c s)"),
                               ACT.Copy, scale=0.0).then_inc(step, 1)

        def rank_vector(v, n, ne, mask, flags):
            v.wait_ge(sem("rank_ps"), n + 1)
            r = bank[0][:, 0:2 * ne].rearrange("p (h e) -> p h e", h=HALVES)
            dve_link(v, v.tensor_copy(cnt[:, 0:ne], bank[1][:, 0:ne]))
            dve_link(v, v.tensor_reduce(cnt[:, 0:1], cnt[:, 0:ne], AX.X, ALU.max))
            for i, slots in flags:
                v.tensor_scalar(smalli[:, i:i + 1], cnt[:, 0:1], float(slots), None, ALU.is_gt).then_inc(sem("flag_ready"), 1)
            dve_link(v, v.scalar_tensor_tensor(mask[:, :, :], r, 1.0, mask[:, :, :], ALU.add, ALU.mult))

        def moe1_vector(v):
            v.wait_ge(sem("logits_ps"), 1)
            v.wait_ge(sem("router_loaded"), 64)
            for h in range(HALVES):
                ins = v.tensor_tensor(lgE[:, h, :], bank[0][:, EXPERTS * h:EXPERTS * (h + 1)], b_r1, ALU.add)
            dve_link(v, ins)
            top2_vector(v, 0, lgE, 0, None)
            for h in range(HALVES):
                dve_link(v, v.tensor_scalar(comb1[:, h, :], oh[:, 0, h, :], gw[:, h, 2:3], None, ALU.mult))
                dve_link(v, v.scalar_tensor_tensor(comb1[:, h, :], oh[:, 1, h, :], gw[:, h, 3:4], comb1[:, h, :], ALU.mult, ALU.add))
            v.tensor_tensor(mask1[:, :, :], oh[:, 0], oh[:, 1], ALU.add).then_inc(sem("mask_ready"), 1)
            v.wait_ge(sem("mask_ready"), 1)
            zero_vector(v, sem("m1_dve"))
            rank_vector(v, 0, EXPERTS, mask1, ((0, SLOTS1),))
            v.memset(rank1[:, EXPERTS, :], -1.0)
            v.memset(gate1[:, :, :], 0.0)
            dve_link(v, v.tensor_scalar(rank1[:, 0:EXPERTS, :].rearrange("p e h -> p h e"), mask1[:, :, :], 1.0, None, ALU.subtract))
            dve_link(v, v.tensor_copy(gate1[:, 0:EXPERTS, :].rearrange("p e h -> p h e"), comb1[:, :, :]))
            step, ped, actd = sem("m1_dve"), sem("m1_pe"), sem("m1_act")
            for h in range(HALVES):
                v.tensor_scalar(sel[:, h, :], iota, rank1[:, 0, h:h + 1], None, ALU.is_equal).then_inc(step, 1)
            with v.Fori(0, EXPERTS) as it:
                v.wait_ge(ped, it * PE1 + FIRST_PE)
                for h in range(HALVES):
                    v.tensor_scalar(selg[:, h, :], iota, rank1[:, it, h:h + 1], gate1[:, it, h:h + 1], ALU.is_equal, ALU.mult)\
                     .then_inc(step, 1)
                for h in range(HALVES):
                    v.tensor_scalar(sel[:, h, :], iota, rank1[:, it + 1, h:h + 1], None, ALU.is_equal).then_inc(step, 1)
                for i in range(4):
                    v.wait_ge(ped, at(M1_PE, it, f"c{i}"))
                    combine_add(v, i).then_inc(step, 1)
                for b in range(3):
                    n = FF_BLOCKS[b] * P
                    v.wait_ge(actd, at(M1_ACT, it, f"s{b}"))
                    v.wait_ge(ped, at(M1_PE, it, f"u{b}"))
                    if b > 0:
                        v.wait_ge(ped, at(M1_PE, it, f"t{b - 1}"))
                    v.tensor_tensor(e_hid[:, 0:n], e_silu[b % 2][:, 0:n], bank[2 * (b % 2) + 1][:, 0:n], ALU.mult).then_inc(step, 1)
                    v.wait_ge(ped, at(M1_PE, it, f"t{b}"))
                    v.tensor_copy(e_hidT[:, 0:FF_BLOCKS[b], :], bank3(6 if b == 0 else 7)[:, 0:FF_BLOCKS[b], :]).then_inc(step, 1)
            for i in range(4):
                v.wait_ge(ped, FIRST_PE + EXPERTS * PE1 + i + 1)
                combine_add(v, i).then_inc(step, 1)
            v.wait_ge(step, FIRST_DVE + EXPERTS * DVE1 + 4)

        def combine_add(v, i):
            y = yacc[:, i // 2, 512 * (i % 2):512 * (i % 2) + 512]
            return v.tensor_tensor(y, y, bank[6 + i % 2][:, :], ALU.add)

        def residual_vector(v, alpha):
            for h in range(HALVES):
                ins = v.scalar_tensor_tensor(xres[:, h, :], xres[:, h, :], alpha, yacc[:, h, :], ALU.mult, ALU.add)
            dve_link(v, ins)

        M2_PE = Order(FIRST_PE, ["k0", "k1", "c0", "c1", "c2", "c3"] + [f"k{i}" for i in range(2, DC)] + ["st", "x0", "x1", "t", "d0", "d1", "d2", "d3"])
        M2_ACT = Order(FIRST_ACT, ["s", "st", "x0", "x1", "y0", "y1"])
        M2_DVE = Order(FIRST_DVE, ["e0", "e1", "sg0", "sg1", "s0", "s1", "c0", "c1", "c2", "c3", "h", "t"])
        M2_UNIT_STEP = [f"k{UP_K * i + UP_K - 1}" for i in range(UP_UNITS)] + [f"d{DOWN_C * i + DOWN_C - 1}" for i in range(DOWN_UNITS)]
        PE2, ACT2, DVE2 = len(M2_PE.names), len(M2_ACT.names), len(M2_DVE.names)

        def moe2_tensor(pe):
            for h in range(HALVES):
                for k in range(DC):
                    ins = mm(bank[0][:, 36 * h:36 * (h + 1)], xT[:, k, h * P:(h + 1) * P], w_r2[:, k, :], k == 0, k == DC - 1)
            ins.then_inc(sem("logits_ps"), 1)
            rank_tensor(pe, 1, mask2, EXPERTS2)
            step, actd, dved = sem("m2_pe"), sem("m2_act"), sem("m2_dve")
            pe.wait_ge(dved, FIRST_DVE)
            dispatch_tensor(pe, step, xn, 6, lambda i: None)
            with pe.Fori(0, PACKS) as it:
                def unit(j):
                    unit_ready_it(pe, U_MOE2 + j, it, UNITS_PACK)
                    return slot(U_MOE2 + j)

                def up(k):
                    w = unit(k // UP_K).rearrange("p (e w k n) -> p e w k n", e=PACK, w=2, k=UP_K)
                    for i in range(2):
                        for e in range(PACK):
                            r = slice(SLOTS2 * e, SLOTS2 * (e + 1))
                            ins = mm(bank[i][r, :], xeT[:, k, r], w[:, e, i, k % UP_K, :], k == 0, k == DC - 1)
                    ins.then_inc(step, 1)

                pe.wait_ge(actd, at(M2_ACT, it, "x1", 1))
                up(0)
                up(1)

                def combine_waits(i):
                    if i == 0:
                        pe.wait_ge(actd, at(M2_ACT, it, "y1", 1))
                    if i >= 2:
                        pe.wait_ge(dved, at(M2_DVE, it, f"c{i - 2}"))
                combine_tensor(pe, step, combine_waits)
                for k in range(2, DC):
                    up(k)
                pe.wait_ge(dved, at(M2_DVE, it, "sg1"))
                seltrans_tensor(pe, step, 3)
                pe.wait_ge(dved, at(M2_DVE, it, "s1"))
                dispatch_tensor(pe, step, xn, 6, lambda i: pe.wait_ge(dved, at(M2_DVE, it, f"c{2 + i}")))
                pe.wait_ge(dved, at(M2_DVE, it, "h"))
                for c in range(4):
                    ins = pe.transpose(bank[2][:, c * P:(c + 1) * P], e_hid[:, c * P:(c + 1) * P], ident)
                ins.then_inc(step, 1)
                pe.wait_ge(dved, at(M2_DVE, it, "t"))
                for c in range(4):
                    w = unit(UP_UNITS + c // DOWN_C).rearrange("p (e c n) -> p e c n", e=PACK, c=DOWN_C)
                    for n in range(2):
                        for e in range(PACK):
                            r = slice(SLOTS2 * e, SLOTS2 * (e + 1))
                            ins = mm(bank[4 + n][r, :], e_hidT[:, c, r], w[:, e, c % DOWN_C, 512 * n:512 * n + 512], c == 0, c == 3)
                    ins.then_inc(step, 1)
            pe.wait_ge(actd, at(M2_ACT, PACKS, "y1", 1))

            def last_waits(i):
                if i >= 2:
                    pe.wait_ge(dved, FIRST_DVE + PACKS * DVE2 + i - 1)
            combine_tensor(pe, step, last_waits)

        def moe2_scalar(act):
            for h in range(HALVES):
                act.wait_ge(sem("group_max"), h + 1)
                act.activation(gexp[:, h, :], lg[:, h, 0:GROUPS2], ACT.Exp, bias=gw[:, h, 4:5]).then_inc(sem("group_exp"), 1)
            top2_scalar(act, 1)
            step, ped, dved = sem("m2_act"), sem("m2_pe"), sem("m2_dve")

            def gathered(i):
                for c in range(4):
                    q = 4 * i + c
                    ins = act.activation(xeT[:, q, :], bank[6 + i][:, c * P:(c + 1) * P], ACT.Copy, scale=g_cols[:, 1, q:q + 1])
                ins.then_inc(step, 1)
            for i in range(2):
                act.wait_ge(ped, i + 1)
                gathered(i)
            act.wait_ge(step, 2)
            zero_scalar(act, step)
            with act.Fori(0, PACKS) as it:
                act.wait_ge(ped, at(M2_PE, it, f"k{DC - 1}"))
                act.wait_ge(dved, at(M2_DVE, it, "h", 1))
                act.activation(e_silu[0], bank[0][:, :], ACT.Silu).then_inc(step, 1)
                act.wait_ge(ped, at(M2_PE, it, "st"))
                act.activation(selT, bank[3][:, 0:SEQ], ACT.Copy).then_inc(step, 1)
                for i in range(2):
                    act.wait_ge(ped, at(M2_PE, it, f"x{i}"))
                    gathered(i)
                act.wait_ge(ped, at(M2_PE, it, "d3"))
                for i in range(2):
                    act.activation(e_out[:, 512 * i:512 * i + 512], bank[4 + i][:, :], ACT.Copy).then_inc(step, 1)

        def moe2_vector(v):
            v.wait_ge(sem("logits_ps"), 2)
            for h in range(HALVES):
                ins = v.tensor_tensor(lg[:, h, 0:36], bank[0][:, 36 * h:36 * (h + 1)], b_r2, ALU.add)
            dve_link(v, ins)
            v.memset(lgE[:, :, 4:8], -3.0e38)
            dve_link(v, v.tensor_copy(lgE[:, :, 0:4], lg[:, :, 0:GROUPS2]))
            for h in range(HALVES):
                dve_link(v, v.max(top[:, h, :], lgE[:, h, :]))
                dve_link(v, v.max_index(idx_u[:, h, :], top[:, h, :], lgE[:, h, :]))
                v.tensor_scalar(gw[:, h, 4:5], top[:, h, 0:1], -1.0, None, ALU.mult).then_inc(sem("group_max"), 1)
            dve_link(v, v.tensor_copy(topi[:, :, :], idx_u[:, :, :]))
            for h in range(HALVES):
                ins = v.tensor_scalar(ohG[:, h, :], iota[:, 0:GROUPS2], topi[:, h, 0:1], None, ALU.is_equal)
            dve_link(v, ins)
            for h in range(HALVES):
                for g in range(GROUPS2):
                    le = lg[:, h, GROUPS2 + PER_GROUP * g:GROUPS2 + PER_GROUP * (g + 1)]
                    if g == 0:
                        dve_link(v, v.tensor_scalar(lgE[:, h, :], le, ohG[:, h, g:g + 1], None, ALU.mult))
                    else:
                        dve_link(v, v.scalar_tensor_tensor(lgE[:, h, :], le, ohG[:, h, g:g + 1], lgE[:, h, :], ALU.mult, ALU.add))
            v.wait_ge(sem("group_exp"), 2)
            dve_link(v, v.tensor_reduce(gw[:, :, 5], gexp[:, :, :], AX.X, ALU.add))
            dve_link(v, v.reciprocal(gw[:, :, 5:6], gw[:, :, 5:6]))
            top2_vector(v, 1, lgE, 1, gw[:, :, 5:6])
            for h in range(HALVES):
                dve_link(v, v.tensor_scalar(top[:, h, :], oh[:, 0, h, :], gw[:, h, 2:3], None, ALU.mult))
                dve_link(v, v.scalar_tensor_tensor(top[:, h, :], oh[:, 1, h, :], gw[:, h, 3:4], top[:, h, :], ALU.mult, ALU.add))
            dve_link(v, v.tensor_tensor(topi[:, :, :], oh[:, 0], oh[:, 1], ALU.add))
            for h in range(HALVES):
                for g in range(GROUPS2):
                    e = slice(PER_GROUP * g, PER_GROUP * (g + 1))
                    v.tensor_scalar(comb2[:, h, e], top[:, h, :], ohG[:, h, g:g + 1], None, ALU.mult)
                    ins = v.tensor_scalar(mask2[:, h, e], topi[:, h, :], ohG[:, h, g:g + 1], None, ALU.mult)
            ins.then_inc(sem("mask_ready"), 1)
            v.wait_ge(sem("mask_ready"), 2)
            zero_vector(v, sem("m2_dve"))
            rank_vector(v, 1, EXPERTS2, mask2, ((1, SLOTS2), (2, SLOTS2 + P)))
            v.memset(rank2[:, PACKS], -1.0)
            v.memset(gate2[:, PACKS], 0.0)
            for h in range(HALVES):
                v.tensor_copy(gate2[:, 0:PACKS, h, :], comb2[:, h, :].rearrange("p (g e) -> p g e", e=PACK))
                ins = v.tensor_scalar(rank2[:, 0:PACKS, h, :], mask2[:, h, :].rearrange("p (g e) -> p g e", e=PACK), 1.0, None, ALU.subtract)
            dve_link(v, ins)
            step, ped, actd = sem("m2_dve"), sem("m2_pe"), sem("m2_act")

            def onehot(dst, h, g):
                return v.tensor_tensor(dst[:, h, :].rearrange("p (e s) -> p e s", e=PACK), bc(iota[:, 0:SLOTS2], 1, PACK),
                                       bc(rank2[:, g, h, :], 2, SLOTS2), ALU.is_equal)
            for h in range(HALVES):
                onehot(sel, h, 0).then_inc(step, 1)
            with v.Fori(0, PACKS) as it:
                v.wait_ge(ped, it * PE2 + FIRST_PE)
                for h in range(HALVES):
                    onehot(selg, h, it).then_inc(step, 1)
                v.wait_ge(step, at(M2_DVE, it, "e1"))
                for h in range(HALVES):
                    sg = selg[:, h, :].rearrange("p (e s) -> p e s", e=PACK)
                    v.tensor_tensor(sg, sg, bc(gate2[:, it, h, :], 2, SLOTS2), ALU.mult).then_inc(step, 1)
                for h in range(HALVES):
                    onehot(sel, h, it + 1).then_inc(step, 1)
                for i in range(4):
                    v.wait_ge(ped, at(M2_PE, it, f"c{i}"))
                    combine_add(v, i).then_inc(step, 1)
                v.wait_ge(actd, at(M2_ACT, it, "s"))
                v.tensor_tensor(e_hid, e_silu[0], bank[1][:, :], ALU.mult).then_inc(step, 1)
                v.wait_ge(ped, at(M2_PE, it, "t"))
                v.tensor_copy(e_hidT[:, :, :], bank3(2)).then_inc(step, 1)
            for i in range(4):
                v.wait_ge(ped, FIRST_PE + PACKS * PE2 + i + 1)
                combine_add(v, i).then_inc(step, 1)
            v.wait_ge(step, FIRST_DVE + PACKS * DVE2 + 4)

        OVER_EXPERTS = (EXPERTS, EXPERTS2, EXPERTS2)
        OVER_BLOCKS = (FF_BLOCKS, (FF2 // P,), (FF2 // P,))
        OVER_FIRST = (SLOTS1, SLOTS2, SLOTS2 + P)
        OVER_X = (xres, xn, xn)

        def over_steps(n):
            return 6 * len(OVER_BLOCKS[n]) + 6

        def over_flag(eng, n):
            eng.wait_ge(sem("flag_ready"), n + 1)
            return eng.value_load(smalli[0:1, n:n + 1], min_val=0, max_val=1)

        def over_wait(eng, n, it, s):
            eng.wait_ge(sem(f"over_step{n}"), it * over_steps(n) + (1 + s))

        def overflow_sync(sp, n):
            with sp.If(over_flag(sp, n) == 1):
                loaded = sem(f"over_loaded{n}")
                if n == 0:
                    with sp.Fori(0, EXPERTS) as it:
                        for b in range(len(FF_BLOCKS)):
                            over_wait(sp, n, it, 3 + 6 * b if b > 0 else 1)
                            for i in range(3):
                                if b < 2:
                                    sp.dma_start(ring[:, i, :], I["moe1_wide"][it, ((0, 1, 3), (2, 4, 5))[b][i]]).then_inc(loaded, 16)
                                else:
                                    sp.dma_start(ring[:, i, 0:3 * D], I["moe1_last"][it, i]).then_inc(loaded, 16)
                else:
                    with sp.Fori(0, PACKS) as g:
                        for e in range(PACK):
                            over_wait(sp, n, g * PACK + e, 1)
                            for i in range(2):
                                sp.dma_start(ring[:, i, :].rearrange("p (u r) -> p u r", u=UP_UNITS),
                                             I["moe2_up"][g].rearrange("u d (e w r) -> d e w u r", e=PACK, w=2)[:, e, i])\
                                    .then_inc(loaded, 16)
                            sp.dma_start(ring[:, 2, :].rearrange("p (u r) -> p u r", u=DOWN_UNITS),
                                         I["moe2_down"][g].rearrange("u f (e r) -> f e u r", e=PACK)[:, e])\
                                .then_inc(loaded, 16)
                over_wait(sp, n, OVER_EXPERTS[n], 0)

        def overflow_tensor(pe, n):
            nb, x = len(OVER_BLOCKS[n]), OVER_X[n]
            step = sem(f"over_step{n}")
            with pe.If(over_flag(pe, n) == 1):
                with pe.Fori(0, OVER_EXPERTS[n]) as it:
                    over_wait(pe, n, it, 1)
                    for c in range(DC):
                        for h in range(HALVES):
                            mm(bank[7 - c // 4][:, (c % 4) * P:(c % 4 + 1) * P], x[:, h, c * P:(c + 1) * P], sel[:, h, :],
                               h == 0, h == HALVES - 1)
                    for h in range(HALVES):
                        ins = pe.transpose(bank[3][:, P * h:P * (h + 1)], selg[:, h, :], ident)
                    ins.then_inc(step, 1)
                    for b, nch in enumerate(OVER_BLOCKS[n]):
                        over_wait(pe, n, it, 3 + 6 * b)
                        pe.wait_ge(sem(f"over_loaded{n}"), it * (48 * nb) + 48 * (b + 1))
                        w1, w3 = (ring[:, i, 0:DC * nch * P].rearrange("p (k n) -> p k n", k=DC) for i in range(2))
                        for k in range(DC):
                            mm(bank[0][:, 0:nch * P], xeT[:, k, :], w1[:, k, :], k == 0, k == DC - 1)
                        for k in range(DC):
                            ins = mm(bank[1][:, 0:nch * P], xeT[:, k, :], w3[:, k, :], k == 0, k == DC - 1)
                        ins.then_inc(step, 1)
                        over_wait(pe, n, it, 6 + 6 * b)
                        for c in range(nch):
                            ins = pe.transpose(bank[2][:, c * P:(c + 1) * P], e_hid[:, c * P:(c + 1) * P], ident)
                        ins.then_inc(step, 1)
                        over_wait(pe, n, it, 8 + 6 * b)
                        w2 = ring[:, 2, 0:nch * D].rearrange("p (c n) -> p c n", n=D)
                        for c in range(nch):
                            for j in range(2):
                                ins = mm(bank[4 + j][:, :], e_hidT[:, c, :], w2[:, c, 512 * j:512 * j + 512],
                                         b == 0 and c == 0, b == nb - 1 and c == nch - 1)
                        ins.then_inc(step, 1)
                    over_wait(pe, n, it, 4 + 6 * nb)
                    for i in range(4):
                        ins = mm(bank[i][:, :], selT[:, P * (i // 2):P * (i // 2) + P], e_out[:, 512 * (i % 2):512 * (i % 2) + 512])
                    ins.then_inc(step, 1)

        def overflow_scalar(act, n):
            nb = len(OVER_BLOCKS[n])
            step = sem(f"over_step{n}")
            with act.If(over_flag(act, n) == 1):
                with act.Fori(0, OVER_EXPERTS[n]) as it:
                    over_wait(act, n, it, 2)
                    for c in range(DC):
                        src = bank[7 - c // 4][:, (c % 4) * P:(c % 4 + 1) * P]
                        if n == 0:
                            act.activation(xeT[:, c, :], src, ACT.Copy)
                        else:
                            act.activation(xeT[:, c, :], src, ACT.Copy, scale=g_cols[:, 1, c:c + 1])
                    act.activation(selT, bank[3][:, 0:SEQ], ACT.Copy).then_inc(step, 1)
                    for b, nch in enumerate(OVER_BLOCKS[n]):
                        over_wait(act, n, it, 4 + 6 * b)
                        act.activation(e_silu[0][:, 0:nch * P], bank[0][:, 0:nch * P], ACT.Silu).then_inc(step, 1)
                    over_wait(act, n, it, 3 + 6 * nb)
                    for i in range(2):
                        ins = act.activation(e_out[:, 512 * i:512 * i + 512], bank[4 + i][:, :], ACT.Copy)
                    ins.then_inc(step, 1)

        def overflow_vector(v, n):
            nb = len(OVER_BLOCKS[n])
            step = sem(f"over_step{n}")
            rank, gate = ((mask1, comb1), (mask2, comb2), (mask2, comb2))[n]
            with v.If(over_flag(v, n) == 1):
                v.tensor_scalar(iota_over, iota, float(OVER_FIRST[n] + 1), None, ALU.add).then_inc(step, 1)
                with v.Fori(0, OVER_EXPERTS[n]) as it:
                    over_wait(v, n, it, 0)
                    for h in range(HALVES):
                        v.tensor_scalar(sel[:, h, :], iota_over, rank[:, h, it].unsqueeze(1), None, ALU.is_equal)
                    for h in range(HALVES):
                        ins = v.tensor_scalar(selg[:, h, :], iota_over, rank[:, h, it].unsqueeze(1), gate[:, h, it].unsqueeze(1),
                                              ALU.is_equal, ALU.mult)
                    ins.then_inc(step, 1)
                    for b, nch in enumerate(OVER_BLOCKS[n]):
                        over_wait(v, n, it, 5 + 6 * b)
                        v.tensor_tensor(e_hid[:, 0:nch * P], e_silu[0][:, 0:nch * P], bank[1][:, 0:nch * P], ALU.mult)\
                         .then_inc(step, 1)
                        over_wait(v, n, it, 7 + 6 * b)
                        v.tensor_copy(e_hidT[:, 0:nch, :], bank3(2)[:, 0:nch, :]).then_inc(step, 1)
                    over_wait(v, n, it, 5 + 6 * nb)
                    for i in range(4):
                        y = yacc[:, i // 2, 512 * (i % 2):512 * (i % 2) + 512]
                        ins = v.tensor_tensor(y, y, bank[i][:, :], ALU.add)
                    ins.then_inc(step, 1)
                over_wait(v, n, OVER_EXPERTS[n], 0)

        mw = Carver(work, moe_end, WORK)
        NC2 = CW // P
        zT = mw(NC2, SEQ + CONV2_TAPS - 1)
        cT = mw(NC2, SEQ)
        ycT = mw(NC2, SEQ)
        ug = mw(HALVES, CW)
        vg = mw(HALVES, CW)
        ysT = mw(NC2, SEQ)
        wsT = mw(SGU_HEADS, P)
        g_sgu = mw(CW)
        vst = mw(HALVES, 6)
        vmv = mw(HALVES, 2)
        vrs = mw(HALVES, 1)
        SD = CW // SGU_HEADS
        pT = mw(2, SEQ)
        ple_g = ug.rearrange("p a b -> p (a b)")[:, 0:512]
        ple_t = vg.rearrange("p a b -> p (a b)")[:, 0:512]

        def mix2_tensor(pe):
            for j in range(3):
                unit_ready(pe, U_WIN2 + j)
                w = slot(U_WIN2 + j).rearrange("p (k n) -> p k n", k=DC)
                for c in range(NC2):
                    for k in range(DC):
                        ins = mm(bank[2 * j + c // 2][:, SEQ * (c % 2):SEQ * (c % 2) + SEQ], w[:, k, c * P:(c + 1) * P],
                                 xT[:, k, :], k == 0, k == DC - 1)
                    ins.then_inc(sem("cxb_ps"), 1)
            for j in range(2):
                unit_ready(pe, U_WIN2 + 3 + j)
                w = slot(U_WIN2 + 3 + j).rearrange("p (k n) -> p k n", k=DC)
                if j == 1:
                    pe.wait_ge(sem("c_done"), NC2)
                for h in range(HALVES):
                    for k in range(DC):
                        ins = mm(bank[6 + h if j == 0 else h][:, :], xT[:, k, h * P:(h + 1) * P], w[:, k, :], k == 0, k == DC - 1)
                    ins.then_inc(sem("uv_ps"), 1)
            pe.wait_ge(sem("z2_done"), NC2)
            pe.wait_ge(sem("ws_masked"), 1)
            for h in range(HALVES):
                pe.wait_ge(sem("v_normed"), h + 1)
                for e in range(SGU_HEADS):
                    ins = mm(bank[2 + h][:, SD * e:SD * (e + 1)], wsT[:, e, :], vg[:, h, SD * e:SD * (e + 1)])
                ins.then_inc(sem("mixed_ps"), 1)
            for h in range(HALVES):
                pe.wait_ge(sem("ysgu_done"), h + 1)
                for c in range(NC2):
                    ins = pe.transpose(bank[h][:, c * P:(c + 1) * P], vg[:, h, c * P:(c + 1) * P], ident)
                ins.then_inc(sem("ys_ps"), 1)
            pe.wait_ge(sem("conv2_done"), NC2)
            pe.wait_ge(sem("ys_done"), HALVES)
            pe.wait_ge(sem("gelu2_done"), 2 * HALVES)
            for j in range(2):
                unit_ready(pe, U_WOUT2 + j)
                w = slot(U_WOUT2 + j).rearrange("p (k n) -> p k n", k=DC)
                for h in range(HALVES):
                    for k in range(DC):
                        src = ycT if k < NC2 else ysT
                        ins = mm(bank[4 + 2 * j + h][:, :], src[:, k % NC2, h * P:(h + 1) * P], w[:, k, :], k == 0, k == DC - 1)
                    ins.then_inc(sem("wout2_ps"), 1)
            turn_tensor(pe, 5, xn)

        def mix2_loads(act):
            for name, dst in (("wsT", wsT), ("g_sgu", g_sgu), ("pT", pT)):
                act.dma_start(dst, I[name]).then_inc(sem("mix2_loaded"), 16)

        def mix2_scalar(act):
            act.wait_ge(sem("lnp_used"), 1)
            act.dma_start(lnp[:, 0, :], I["g_final"]).then_inc(sem("lnp_loaded"), 16)
            for c in range(NC2):
                act.wait_ge(sem("cxb_ps"), 2 * (c // 2) + 2)
                act.activation(cT[:, c, :], bank[c // 2][:, SEQ * (c % 2):SEQ * (c % 2) + SEQ], ACT.Copy).then_inc(sem("c_done"), 1)
            for j in range(2):
                for h in range(HALVES):
                    act.wait_ge(sem("uv_ps"), 2 * j + h + 1)
                    act.activation((ug, vg)[j][:, h, :], bank[6 + h if j == 0 else h][:, :], ACT.Gelu_apprx_tanh)\
                       .then_inc(sem("gelu2_done"), 1)
            for h in range(HALVES):
                act.wait_ge(sem("v_var"), h + 1)
                act.activation(vrs[:, h, :], vrs[:, h, :], ACT.Sqrt).then_inc(sem("v_rstd"), 1)
            for h in range(HALVES):
                act.wait_ge(sem("ys_ps"), h + 1)
                act.activation(ysT[:, :, h * P:(h + 1) * P], bank3(h), ACT.Copy).then_inc(sem("ys_done"), 1)
            norm_scalar(act, 5)

        def mix2_vector(v):
            v.wait_ge(sem("mix2_loaded"), 48)
            v.memset(zT[:, :, 0:CONV2_TAPS - 1], 0.0)
            v.tensor_tensor(wsT[:, :, :], wsT[:, :, :], bc(upto_t, 1, SGU_HEADS), ALU.mult).then_inc(sem("ws_masked"), 1)
            for c in range(NC2):
                v.wait_ge(sem("cxb_ps"), NC2 + 2 * (c // 2) + 2)
                v.wait_ge(sem("c_done"), c + 1)
                v.tensor_tensor(zT[:, c, CONV2_TAPS - 1:], cT[:, c, :], bank[2 + c // 2][:, SEQ * (c % 2):SEQ * (c % 2) + SEQ],
                                ALU.mult).then_inc(sem("z2_done"), 1)
            v.wait_ge(sem("z2_done"), NC2)
            for c in range(NC2):
                dve_link(v, v.tensor_scalar(ycT[:, c, :], zT[:, c, 0:SEQ], conv2_w[:, c, 0:1], None, ALU.mult))
                for k in range(1, CONV2_TAPS):
                    dve_link(v, v.scalar_tensor_tensor(ycT[:, c, :], zT[:, c, k:k + SEQ], conv2_w[:, c, k:k + 1], ycT[:, c, :],
                                                       ALU.mult, ALU.add))
                v.wait_ge(sem("cxb_ps"), 2 * NC2 + 2 * (c // 2) + 2)
                v.tensor_tensor(ycT[:, c, :], ycT[:, c, :], bank[4 + c // 2][:, SEQ * (c % 2):SEQ * (c % 2) + SEQ], ALU.mult)\
                 .then_inc(sem("conv2_done"), 1)
            for h in range(HALVES):
                v.wait_ge(sem("gelu2_done"), HALVES + h + 1)
                dve_link(v, v.bn_stats(vst[:, h, :], vg[:, h, :]))
                dve_link(v, v.bn_aggr(vmv[:, h, :], vst[:, h, :]))
                dve_link(v, v.tensor_scalar(vrs[:, h, :], vmv[:, h, 1:2], NORM_EPS, None, ALU.add))
                v.reciprocal(vrs[:, h, :], vrs[:, h, :]).then_inc(sem("v_var"), 1)
            for h in range(HALVES):
                v.wait_ge(sem("v_rstd"), h + 1)
                dve_link(v, v.tensor_scalar(vg[:, h, :], vg[:, h, :], vmv[:, h, 0:1], vrs[:, h, :], ALU.subtract, ALU.mult))
                v.tensor_tensor(vg[:, h, :], vg[:, h, :], g_sgu, ALU.mult).then_inc(sem("v_normed"), 1)
            for h in range(HALVES):
                v.wait_ge(sem("mixed_ps"), h + 1)
                o = vg[:, h, :].rearrange("p (e d) -> p e d", e=SGU_HEADS)
                dve_link(v, v.tensor_tensor(o, bank[2 + h][:, :].rearrange("p (e d) -> p e d", e=SGU_HEADS), bc(b_sp, 2, SD), ALU.add))
                v.tensor_tensor(vg[:, h, :], vg[:, h, :], ug[:, h, :], ALU.mult).then_inc(sem("ysgu_done"), 1)
            for j in range(2):
                for h in range(HALVES):
                    v.wait_ge(sem("wout2_ps"), 2 * j + h + 1)
                    xs = xres[:, h, 512 * j:512 * j + 512]
                    ins = v.tensor_tensor(xs, xs, bank[4 + 2 * j + h][:, :], ALU.add)
            dve_link(v, ins)
            norm_vector(v, 5, xres, xn)
            turn_evacuate(v, 5, g_cols[:, 1, :])

        def ple_tensor(pe):
            for j in range(2):
                unit_ready(pe, U_PLE + j)
                w = slot(U_PLE + j).rearrange("p (k n) -> p k n", k=DC)
                for h in range(HALVES):
                    for k in range(DC):
                        ins = mm(bank[2 * j + h][:, :], xT[:, k, h * P:(h + 1) * P], w[:, k, :], k == 0, k == DC - 1)
                    ins.then_inc(sem("ple_ps"), 1)
            unit_ready(pe, U_PLE + 2)
            w = slot(U_PLE + 2)[:, 0:2 * D].rearrange("p (k n) -> p k n", k=2)
            for j in range(2):
                for h in range(HALVES):
                    for k in range(2):
                        ins = mm(bank[4 + 2 * j + h][:, :], pT[:, k, h * P:(h + 1) * P], w[:, k, 512 * j:512 * j + 512], k == 0, k == 1)
                    ins.then_inc(sem("ple_ps"), 1)

        def ple_scalar(act):
            for i in range(4):
                act.wait_ge(sem("ple_ps"), i + 1)
                if i >= 1:
                    act.wait_ge(sem("ple_done"), i)
                act.activation(ple_g, bank[i][:, :], ACT.Sigmoid).then_inc(sem("ple_sig"), 1)
            norm_scalar(act, 7)

        def ple_vector(v):
            for i in range(4):
                j, h = i // 2, i % 2
                v.wait_ge(sem("ple_ps"), 4 + i + 1)
                v.wait_ge(sem("ple_sig"), i + 1)
                dve_link(v, v.tensor_tensor(ple_t, ple_g, bank[4 + i][:, :], ALU.mult))
                xs = xres[:, h, 512 * j:512 * j + 512]
                v.tensor_tensor(xs, xs, ple_t, ALU.add).then_inc(sem("ple_done"), 1)
                v.wait_ge(sem("ple_done"), i + 1)
            v.wait_ge(sem("lnp_loaded"), 32 * 4 + 16)
            norm_vector(v, 7, xres, xn)

        LAST = {"gdn": 1, "ffn": 2, "s5": 3, "moe1": 4, "mix2": 5, "moe2": 6, "all": 7}[upto]
        STORES = HALVES

        block = ctx.enter_context(nc.Block())

        @block.sync
        def _(sp):
            sp.dma_start(xT[:, :, :], I["x_cols"]).then_inc(sem("xT_loaded"), 16)

            def load(u, src, n=UNIT):
                sp.dma_start(slot(u)[:, 0:n], src).then_inc(sem(f"unit_loaded{u % RING}"), 16)

            def dense(u, first):
                load(u, I["w_dense"][DENSE_AT[first] + u - first])

            def released(u):
                if u < 0:
                    return
                if u < U_Z:
                    sp.wait_ge(sem("qkv_ps"), 4 * (u + 1))
                elif u < U_WOUT:
                    sp.wait_ge(sem("z_ps"), 2 * (u - U_Z + 1))
                elif u < U_FFN:
                    sp.wait_ge(sem("wout_ps"), 2 * (u - U_WOUT + 1))
                elif u < U_S5IN:
                    b, i = divmod(u - U_FFN, 3)
                    if i < 2:
                        sp.wait_ge(sem("ffn_up"), sum((FF_BLOCKS * 2)[:b + 1]))
                    else:
                        sp.wait_ge(sem("ffn_dn"), b + 1)
                elif u < U_GLU:
                    sp.wait_ge(sem("u_ps"), 4 * (u - U_S5IN + 1))
                elif u < U_MOE1:
                    sp.wait_ge(sem("glu_ps"), 2 * (u - U_GLU + 1))
                elif u < U_WIN2:
                    e, i = divmod(u - U_MOE1, UNITS_EXPERT)
                    sp.wait_ge(sem("m1_pe"), at(M1_PE, e, M1_UNIT_STEP[i]))
                elif u < U_WIN2 + 3:
                    sp.wait_ge(sem("cxb_ps"), NC2 * (u - U_WIN2 + 1))
                elif u < U_WOUT2:
                    sp.wait_ge(sem("uv_ps"), HALVES * (u - U_WIN2 - 2))
                elif u < U_MOE2:
                    sp.wait_ge(sem("wout2_ps"), 2 * (u - U_WOUT2 + 1))
                elif u < U_PLE:
                    g, i = divmod(u - U_MOE2, UNITS_PACK)
                    sp.wait_ge(sem("m2_pe"), at(M2_PE, g, M2_UNIT_STEP[i]))

            def dense_phase(first, n):
                for u in range(first, first + n):
                    released(u - RING)
                    dense(u, first)

            dense_phase(U_QKV, 6)
            dense_phase(U_Z, 2)
            dense_phase(U_WOUT, 2)
            if LAST >= 2:
                for u in range(U_FFN, U_S5IN):
                    e, i = divmod(u - U_FFN, 9)
                    released(u - RING)
                    if i < 6:
                        load(u, I["ffn_wide"][e, i])
                    else:
                        load(u, I["ffn_last"][e, i - 6], 3 * D)
            if LAST >= 3:
                dense_phase(U_S5IN, 2)
                dense_phase(U_GLU, 4)
            if LAST >= 4:
                WIDE = {0: 0, 1: 1, 2: 2, 3: 3, 4: 4, 6: 5}
                NARROW = {5: 0, 7: 1, 8: 2}

                def expert_load(e, j):
                    if j in WIDE:
                        load(U_MOE1 + j, I["moe1_wide"][e, WIDE[j]])
                    else:
                        load(U_MOE1 + j, I["moe1_last"][e, NARROW[j]], 3 * D)
                for j in range(UNITS_EXPERT):
                    released(U_MOE1 + j - RING)
                    expert_load(0, j)
                with sp.Fori(1, EXPERTS) as it:
                    for j in range(UNITS_EXPERT):
                        i = j - RING
                        sp.wait_ge(sem("m1_pe"), at(M1_PE, it, M1_UNIT_STEP[i % UNITS_EXPERT], 1 if i < 0 else 0))
                        expert_load(it, j)
                overflow_sync(sp, 0)
            if LAST >= 5:
                dense_phase(U_WIN2, 5)
                dense_phase(U_WOUT2, 2)
            if LAST >= 6:
                def pack_load(g, j):
                    load(U_MOE2 + j, I["moe2_up"][g, j] if j < UP_UNITS else I["moe2_down"][g, j - UP_UNITS])
                for j in range(UNITS_PACK):
                    released(U_MOE2 + j - RING)
                    pack_load(0, j)
                with sp.Fori(1, PACKS) as it:
                    for j in range(UNITS_PACK):
                        i = j - RING
                        sp.wait_ge(sem("m2_pe"), at(M2_PE, it, M2_UNIT_STEP[i % UNITS_PACK], 1 if i < 0 else 0))
                        pack_load(it, j)
                for n in (1, 2):
                    overflow_sync(sp, n)
            if LAST >= 7:
                dense_phase(U_PLE, 2)
                released(U_PLE + 2 - RING)
                load(U_PLE + 2, I["w_ple"], 2 * D)
            nst = {1: 0, 2: 1, 3: 2, 4: 4, 5: 5, 6: 6, 7: 7}[LAST]
            src = xn if LAST == 7 else xres
            for h in range(HALVES):
                sp.wait_ge(sem("rows_normed"), 2 * nst + h + 1)
                sp.dma_start(out[h], src[:, h, :]).then_inc(sem("stored"), 16)
            sp.wait_ge(sem("stored"), 16 * STORES)

        @block.tensor
        def _(pe):
            gdn_tensor(pe)
            turn_tensor(pe, 0, xres)
            phase_end(pe, 1)
            if LAST >= 2:
                ffn_tensor(pe)
                turn_tensor(pe, 1, xres)
                phase_end(pe, 2)
            if LAST >= 3:
                s5_tensor(pe)
                turn_tensor(pe, 2, xres)
                phase_end(pe, 3)
            if LAST >= 4:
                moe1_tensor(pe)
                overflow_tensor(pe, 0)
                turn_tensor(pe, 4, xn)
                phase_end(pe, 4)
            if LAST >= 5:
                mix2_tensor(pe)
                phase_end(pe, 5)
            if LAST >= 6:
                moe2_tensor(pe)
                for n in (1, 2):
                    overflow_tensor(pe, n)
                turn_tensor(pe, 6, xn)
                phase_end(pe, 6)
            if LAST >= 7:
                ple_tensor(pe)

        @block.scalar
        def _(act):
            gdn_scalar(act)
            phase_end(act, 1)
            if LAST >= 2:
                ffn_scalar(act)
                phase_end(act, 2)
            if LAST >= 3:
                s5_scalar(act)
                phase_end(act, 3)
            if LAST >= 4:
                mix2_loads(act)
                moe1_scalar(act)
                overflow_scalar(act, 0)
                norm_scalar(act, 3)
                norm_scalar(act, 4)
                phase_end(act, 4)
            if LAST >= 5:
                mix2_scalar(act)
                phase_end(act, 5)
            if LAST >= 6:
                moe2_scalar(act)
                for n in (1, 2):
                    overflow_scalar(act, n)
                norm_scalar(act, 6)
                phase_end(act, 6)
            if LAST >= 7:
                ple_scalar(act)

        @block.vector
        def _(v):
            gdn_vector(v)
            phase_end(v, 1)
            if LAST >= 2:
                ffn_vector(v)
                phase_end(v, 2)
            if LAST >= 3:
                s5_vector(v)
                phase_end(v, 3)
            if LAST >= 4:
                moe1_vector(v)
                overflow_vector(v, 0)
                residual_vector(v, ALPHA)
                norm_vector(v, 3, xres, xres)
                v.drain().then_inc(sem("lnp_used"), 1)
                norm_vector(v, 4, xres, xn)
                turn_evacuate(v, 4, g_cols[:, 0, :])
                phase_end(v, 4)
            if LAST >= 5:
                mix2_vector(v)
                phase_end(v, 5)
            if LAST >= 6:
                moe2_vector(v)
                for n in (1, 2):
                    overflow_vector(v, n)
                residual_vector(v, 1.0)
                norm_vector(v, 6, xres, xn)
                turn_evacuate(v, 6, g_cols[:, 2, :])
                phase_end(v, 6)
            if LAST >= 7:
                ple_vector(v)

        @block.gpsimd
        def _(g):
            gdn_gpsimd(g)
            phase_end(g, 1)
            if LAST >= 2:
                ffn_gpsimd(g)
                phase_end(g, 2)
            if LAST >= 3:
                s5_gpsimd(g)
                phase_end(g, 3)
            for n in range(4, min(LAST, 6) + 1):
                phase_end(g, n)


def kernel(**inputs):
    import concourse.bacc as _bacc
    from concourse.bass_utils import run_bass_kernel_spmd as _run

    arrays = layouts(inputs)
    nc = _bacc.Bacc("TRN2", target_bir_lowering=False, num_devices=1)
    I = {name: nc.dram_tensor(name, a.shape, F32, kind="ExternalInput").ap() for name, a in arrays.items()}
    out = nc.dram_tensor("out", (HALVES, P, D), F32, kind="ExternalOutput").ap()
    program(nc, I, out)
    r = _run(nc, [arrays], core_ids=[0])
    return np.asarray(r.results[0]["out"]).reshape(1, SEQ, D)


def constants():
    k, m = np.arange(P)[:, None], np.arange(P)[None, :]
    same = (k // CHUNK) == (m // CHUNK)
    t = [k == m, same & (k <= m), np.where(same & (k <= m), 0.0, NEG)]
    for i in range(6):
        s = 1 << i
        t.append((k // (2 * s) == m // (2 * s)) & (m % (2 * s) >= s) & (k % (2 * s) < s))
    t += [same, (k < CHUNK) & (m >= 0), (k >= CHUNK) & (m >= 0), k < m, (k >= 0) & (m >= 0), m + 0 * k, k <= m,
          k // 32 == m // 32]
    half = np.zeros((P, P))
    half[:, 0] = (np.arange(P) // S5_CH) % 2 == 0
    half[:, 1] = (np.arange(P) // S5_CH) % 2 == 1
    t.append(half)
    return np.ascontiguousarray(np.stack([np.asarray(a, np.float32) for a in t], axis=1))


def layouts(inp):
    inp = {k: np.asarray(v) for k, v in inp.items()}
    f32 = np.float32
    A = {}

    def rep(row):
        return np.broadcast_to(row.reshape(1, -1), (P, row.size))

    def kchunks(w):
        return w.reshape(-1, P, w.shape[-1]).transpose(1, 0, 2)

    def chunkcols(vec):
        return vec.reshape(-1, P).T

    x = inp["x"].reshape(SEQ, D)
    A["x_rows"] = x.reshape(HALVES, P, D).transpose(1, 0, 2)
    A["x_cols"] = x.reshape(SEQ, DC, P).transpose(2, 1, 0)
    w_in = inp["gdn_w_in"][0]
    A["w_ba"] = kchunks(w_in[:, 4 * D:])
    A["conv_w"] = inp["gdn_conv_w"][0].reshape(TAPS, QKV, P).transpose(2, 1, 0)
    A["a_log"], A["dt_bias"] = rep(inp["gdn_a_log"][0]), rep(inp["gdn_dt_bias"][0])
    A["norm_g"] = rep(inp["gdn_norm_g"][0])
    A["consts"] = constants()
    A["g_cols"] = np.stack([chunkcols(inp[n][0]) for n in ("g_mix_2", "g_ffn_2", "g_ple_2")], axis=1)
    A["conv2_w"] = inp["w_conv_2"][0].reshape(CONV2_TAPS, CW // P, P).transpose(2, 1, 0)
    A["b_sp"] = inp["b_spatial_2"][0].T
    A["s5_d"] = chunkcols(inp["s5_d"][0])
    A["ln_rows"] = np.stack([np.stack([rep(inp[n][i, j]) for n in ("ln_g", "ln_b")]) for i in range(2) for j in range(2)])
    chan = 8 * np.arange(DC)[None, :] + (np.arange(P) // 32 * 2 + np.arange(P) // 16 % 2)[:, None]
    pair = 2 * np.arange(PAIRS)[None, :] + (np.arange(P) // S5_STATE)[:, None]
    state = np.arange(P)[:, None] % S5_STATE

    def both(lam):
        return np.concatenate([lam[chan].reshape(P, -1), lam[pair, state]], axis=1)
    A["lam_re"], A["lam_im"] = both(inp["s5_lam_re"][0]), both(inp["s5_lam_im"][0])
    A["log_dt"] = both(np.repeat(inp["s5_log_dt"][0][:, None], S5_STATE, axis=1))

    def paired(t):
        o = np.zeros((2, S5_STATE, PAIRS, 2, S5_CH), f32)
        t = t.reshape(PAIRS, 2, S5_STATE, S5_CH)
        for g in range(2):
            o[g, :, :, g, :] = t[:, g].transpose(1, 0, 2)
        return o.reshape(P, PAIRS, 32)
    for part in ("re", "im"):
        b, c = inp["s5_b_" + part][0], inp["s5_c_" + part][0]
        A["c_" + part] = paired(c.transpose(0, 2, 1))
        A["b1_" + part] = paired(b)
        A["b2_" + part] = b[chan, :, (np.arange(P) % S5_CH)[:, None]]
    A["w_r1"], A["b_r1"] = kchunks(inp["moe_w_router"][0]), rep(inp["moe_b_router"][0])
    A["w_r2"] = kchunks(np.concatenate([inp["w_group_2"][0], inp["w_router_2"][0].transpose(1, 0, 2).reshape(D, -1)], axis=1))
    A["b_r2"] = rep(np.concatenate([inp["b_group_2"][0], inp["b_router_2"][0].reshape(-1)]))
    A["wsT"] = inp["w_spatial_2"][0].transpose(2, 0, 1)
    A["g_sgu"] = rep(inp["g_sgu_2"][0])
    A["pT"] = inp["p_2"][0, 0].reshape(SEQ, 2, P).transpose(2, 1, 0)
    A["g_final"] = rep(inp["g_final_2"])

    def cols(w, at, n=1):
        return [kchunks(w[:, at + 512 * i:at + 512 * i + 512]).reshape(P, UNIT) for i in range(n)]
    glu, w2in = inp["s5_w_glu"][0], inp["w_in_2"][0]
    units = cols(w_in, 0, 8) + cols(inp["gdn_w_out"][0], 0, 2) + cols(inp["s5_w_in"][0], 0, 2)
    units += cols(glu, 0) + cols(glu, D) + cols(glu, 512) + cols(glu, D + 512)
    units += cols(w2in, CW) + cols(w2in, 2 * CW) + cols(w2in, 0) + cols(w2in, 3 * CW, 2)
    units += cols(inp["w_out_2"][0], 0, 2) + cols(inp["w_ple_gate_2"][0], 0, 2)
    A["w_dense"] = np.stack(units)
    A["w_ple"] = kchunks(inp["w_ple_proj_2"][0]).reshape(P, 2 * D)

    def blocks(w1, w3, w2):
        u = []
        at = 0
        for nch in FF_BLOCKS:
            n = nch * P
            u.append([kchunks(w1[:, at:at + n]).reshape(P, -1), kchunks(w3[:, at:at + n]).reshape(P, -1),
                      kchunks(w2[at:at + n]).reshape(P, -1)])
            at += n
        return u
    halves = [blocks(inp["ffn_w1"][0][:, s], inp["ffn_w3"][0][:, s], inp["ffn_w2"][0][s])
              for s in (slice(0, FF_E), slice(FF_E, 2 * FF_E))]
    A["ffn_wide"] = np.stack([np.stack(h[0] + h[1]) for h in halves])
    A["ffn_last"] = np.stack([np.stack(h[2]) for h in halves])
    exps = [blocks(inp["moe_w1"][0, e], inp["moe_w3"][0, e], inp["moe_w2"][0, e]) for e in range(EXPERTS)]
    A["moe1_wide"] = np.stack([np.stack([b0[0], b0[1], b1[0], b0[2], b1[1], b1[2]]) for b0, b1, _ in exps])
    A["moe1_last"] = np.stack([np.stack(b2) for _, _, b2 in exps])
    gate_up = np.stack([inp["w_gate_2"][0], inp["w_up_2"][0]], axis=3)
    A["moe2_up"] = gate_up.reshape(PACKS, PACK, UP_UNITS, UP_K, P, 2, FF2).transpose(0, 2, 4, 1, 5, 3, 6)\
        .reshape(PACKS, UP_UNITS, P, -1)
    A["moe2_down"] = inp["w_down_2"][0].reshape(PACKS, PACK, DOWN_UNITS, DOWN_C, P, D).transpose(0, 2, 4, 1, 3, 5)\
        .reshape(PACKS, DOWN_UNITS, P, -1)
    return {k: np.ascontiguousarray(v, dtype=f32) for k, v in A.items()}
```

```python
from contextlib import ExitStack
from typing import NamedTuple

import numpy as np
import concourse.bass as bass
from concourse import mybir

F32 = mybir.dt.float32
F32R = mybir.dt.float32r
I32 = mybir.dt.int32
U32 = mybir.dt.uint32
ALU = mybir.AluOpType
ACT = mybir.ActivationFunctionType
AX = mybir.AxisListType

P = 128
SEQ, D = 256, 1024
HALVES, DC = SEQ // P, D // P
HEADS, CHUNK = 8, 64
QKV = 3 * HEADS
TAPS = 4
S5_GROUPS, S5_STATE, S5_CH = 64, 64, 16
PAIRS = S5_GROUPS // 2
STEP = 2
NSTEP = SEQ // STEP
FF_E = 1408
FF_BLOCKS = (4, 4, 3)
EXPERTS, SLOTS1 = 8, 128
GROUPS2, PER_GROUP = 4, 8
EXPERTS2 = GROUPS2 * PER_GROUP
PACK, SLOTS2, FF2 = 2, 64, 512
PACKS = EXPERTS2 // PACK
CONV2_TAPS, CW, SGU_HEADS = 3, 512, 8
ALPHA = 4.0 ** 0.25
LN_EPS, NORM_EPS = 1e-5, 1e-6
UNIT = 4096
RING = 3
NEG = -1e30

U_QKV, U_Z, U_WOUT, U_FFN, U_S5IN, U_GLU, U_MOE1, U_WIN2, U_WOUT2, U_MOE2, U_PLE = (
    0, 6, 8, 10, 28, 30, 34, 106, 111, 113, 161)
DENSE_AT = {U_QKV: 0, U_Z: 6, U_WOUT: 8, U_S5IN: 10, U_GLU: 12, U_WIN2: 16, U_WOUT2: 21, U_PLE: 22}
UP_K, DOWN_C = UNIT // (PACK * 2 * FF2), UNIT // (PACK * D)
UP_UNITS, DOWN_UNITS = DC // UP_K, FF2 // P // DOWN_C
UNITS_EXPERT, UNITS_PACK = 9, UP_UNITS + DOWN_UNITS


class Order(NamedTuple):
    first: int
    names: list


class Chain:

    def __init__(self, sem):
        self.sem, self.n = sem, 0

    def __call__(self, eng, ins):
        self.n += 1
        ins.then_inc(self.sem, 1)
        eng.wait_ge(self.sem, self.n)


def program(nc, I, out, upto="all"):
    ctx = ExitStack()
    with ctx:
        def sb(name, shape, dt=F32):
            return ctx.enter_context(nc.sbuf_tensor("sb_" + name, shape, dt))

        sems = {}

        def sem(name):
            if name not in sems:
                sems[name] = ctx.enter_context(nc.semaphore(name))
            return sems[name]

        xres = sb("xres", [P, HALVES, D])
        consts = sb("consts", [P, 18, P])
        (ident, cum, negm, lvl0, lvl1, lvl2, lvl3, lvl4, lvl5, blk, first64, last64,
         before, ones, iota, upto_t, blk32, half_mask) = (consts[:, i, :] for i in range(18))
        lvl = (lvl0, lvl1, lvl2, lvl3, lvl4, lvl5)
        small = sb("small", [P, 1400])
        smalli = sb("smalli", [P, 32], I32)
        psum = ctx.enter_context(nc.psum_tensor("psum", [P, 8, 512], F32))
        bank = [psum[:, i, :] for i in range(8)]

        class Carver:
            def __init__(self, tile, at, end):
                self.tile, self.at, self.end = tile, at, end

            def __call__(self, *shape):
                n = int(np.prod(shape))
                a = self.tile[:, self.at:self.at + n]
                self.at += n
                assert self.at <= self.end, (self.at, self.end)
                if len(shape) == 2:
                    a = a.rearrange("p (a b) -> p a b", a=shape[0])
                if len(shape) == 3:
                    a = a.rearrange("p (a b c) -> p a b c", a=shape[0], b=shape[1])
                if len(shape) == 4:
                    a = a.rearrange("p (a b c d) -> p a b c d", a=shape[0], b=shape[1], c=shape[2])
                return a

        cs = Carver(small, 0, 1400)
        stats = cs(HALVES, 2, 6)
        mv = cs(HALVES, 2)
        rstd = cs(HALVES, 1)
        rtmp = cs(HALVES, 1)
        w_ba = cs(DC, 16)
        conv_w = cs(QKV, TAPS)
        a_log, dt_bias = cs(HEADS), cs(HEADS)
        norm_g = cs(P)
        ba = cs(HALVES, 16)
        g_t, beta, sp_t, sp_a = (cs(HALVES, HEADS) for _ in range(4))
        rn = cs(HALVES, 2 * HEADS)
        gc, eg, kd_s, kb_s, kbg_s, rq_s = (cs(HALVES, HEADS) for _ in range(6))
        s_scale = cs(2 * HALVES, HEADS)
        oms, of = cs(HALVES, HEADS), cs(HALVES, HEADS)
        g_cols = cs(3, DC)
        conv2_w = cs(CW // P, CONV2_TAPS)
        b_sp = cs(SGU_HEADS)
        s5_d = cs(DC)

        idx_u = sb("idx_u", [P, HALVES, 8], U32)
        cr = Carver(sb("router", [P, 396]), 0, 396)
        w_r1, b_r1 = cr(DC, EXPERTS), cr(EXPERTS)
        w_r2, b_r2 = cr(DC, GROUPS2 + EXPERTS2), cr(GROUPS2 + EXPERTS2)
        WORK, FFN_R_AT, K0_AT, SPLIT_AT, SPLIT = 30400, 17408, 8192, 9664, 4 * D + 3 * UNIT
        GX_AT = QKV * (2 * SEQ + TAPS - 1) + 2 * D
        GW_AT = GX_AT + 5 * 2 * D
        with nc.sbuf_tensor("sb_ring", [P, RING, UNIT], F32) as ring, \
                nc.sbuf_tensor("sb_xT", [P, DC, SEQ], F32) as xT, \
                nc.sbuf_tensor("sb_lnp", [P, 2, D], F32) as lnp, \
                nc.sbuf_tensor("sb_work", [P, WORK], F32) as work:
            pass
        ring_r = sb("ring_r", [P, RING, UNIT], F32R)
        xT_r = sb("xT_r", [P, DC, SEQ], F32R)
        lnp_r = sb("lnp_r", [P, 2, D], F32R)
        with nc.sbuf_tensor("sb_below_k0", [P, K0_AT], F32), \
                nc.sbuf_tensor("sb_k0_r", [P, D], F32R) as k0_r, \
                nc.sbuf_tensor("sb_below_ffn", [P, FFN_R_AT - K0_AT - D], F32), \
                nc.sbuf_tensor("sb_ffn_r", [P, 3 * D + 2 * SEQ], F32R) as ffn_r:
            pass
        with nc.sbuf_tensor("sb_below_gx", [P, GX_AT], F32), \
                nc.sbuf_tensor("sb_gx_r", [P, 4 * D], F32R) as gx_r, \
                nc.sbuf_tensor("sb_below_gw", [P, GW_AT - GX_AT - 4 * D], F32), \
                nc.sbuf_tensor("sb_gw_r", [P, 3, D], F32R) as gw_r:
            pass
        sb("below_split", [P, SPLIT_AT])
        split = sb("split", [P, SPLIT], F32R)

        def bc(ap, axis, n):
            a = ap.unsqueeze(axis)
            shape = list(a.shape)
            shape[axis] = n
            return a.to_broadcast(shape)

        def slot(u):
            return ring[:, u % RING, :]

        def unit_ready(pe, u):
            pe.wait_ge(sem(f"unit_loaded{u % RING}"), 16 * (u // RING + 1))

        def unit_ready_it(pe, u, it, per):
            pe.wait_ge(sem(f"unit_loaded{u % RING}"), it * (16 * (per // RING)) + 16 * (u // RING + 1))

        act_link = Chain(sem("act_link"))
        dve_link = Chain(sem("dve_link"))
        pool_link = Chain(sem("pool_link"))
        NLOADS = 10

        def phase_end(eng, n):
            eng.drain().then_inc(sem("phase_done"), 1)
            eng.wait_ge(sem("phase_done"), 4 * n)

        def mm(o, lhsT, rhs, start=True, stop=True, **kw):
            return nc.tensor.matmul(o, lhsT, rhs, start=start, stop=stop, **kw)

        TSTAGE = {0: 0, 1: 1, 2: 2, 4: 3, 5: 4, 6: 5}

        def norm_stats(v, n, y, h, j, ins):
            dve_link(v, ins)
            ins = v.bn_stats(stats[:, h, j, :], y[:, h, 512 * j:512 * j + 512])
            if j == 0:
                return
            dve_link(v, ins)
            dve_link(v, v.bn_aggr(mv[:, h, :], stats[:, h, :, :].rearrange("p a b -> p (a b)")))
            eps = LN_EPS if n < 4 else NORM_EPS
            if n >= 4:
                dve_link(v, v.scalar_tensor_tensor(mv[:, h, 1:2], mv[:, h, 0:1], mv[:, h, 0:1], mv[:, h, 1:2], ALU.mult, ALU.add))
            dve_link(v, v.tensor_scalar(rtmp[:, h, :], mv[:, h, 1:2], eps, None, ALU.add))
            v.reciprocal(rtmp[:, h, :], rtmp[:, h, :]).then_inc(sem("var_inv"), 1)

        def norm_vector(v, n, y, xn):
            for h in range(HALVES):
                v.wait_ge(sem("rstd_ready"), 2 * n + h + 1)
                if n < 4:
                    dve_link(v, v.tensor_scalar(xn[:, h, :], y[:, h, :], mv[:, h, 0:1], rstd[:, h, :],
                                                ALU.subtract, ALU.mult))
                    if h == 0:
                        v.wait_ge(sem("lnp_loaded"), 32 * (n + 1))
                    dve_link(v, v.tensor_tensor(xn[:, h, :], xn[:, h, :], lnp[:, 0, :], ALU.mult))
                    v.tensor_tensor(xn[:, h, :], xn[:, h, :], lnp[:, 1, :], ALU.add).then_inc(sem("rows_normed"), 1)
                elif n < 7:
                    v.tensor_scalar(xn[:, h, :], y[:, h, :], rstd[:, h, :], None, ALU.mult).then_inc(sem("rows_normed"), 1)
                else:
                    dve_link(v, v.tensor_scalar(xn[:, h, :], y[:, h, :], rstd[:, h, :], None, ALU.mult))
                    v.tensor_tensor(xn[:, h, :], xn[:, h, :], lnp[:, 0, :], ALU.mult).then_inc(sem("rows_normed"), 1)
            v.wait_ge(sem("rows_normed"), 2 * n + 2)

        def norm_scalar(act, n):
            for h in range(HALVES):
                act.wait_ge(sem("var_inv"), 2 * n + h + 1)
                act.activation(rstd[:, h, :], rtmp[:, h, :], ACT.Sqrt).then_inc(sem("rstd_ready"), 1)

        def turn_tensor(pe, n, xn):
            t = TSTAGE[n]
            for h in range(HALVES):
                pe.wait_ge(sem("rows_normed"), 2 * n + h + 1)
                for q in range(2):
                    for c in range(4):
                        ins = pe.transpose(bank[4 + 2 * h + q][:, c * P:(c + 1) * P],
                                           xn[:, h, (4 * q + c) * P:(4 * q + c + 1) * P], ident)
                    ins.then_inc(sem("turned"), 1)
            pe.wait_ge(sem("xT_ready"), 4 * (t + 1))
            if n == 0:
                pe.wait_ge(sem("xl_ready"), 4)

        def turn_evacuate(eng, n, gain, dst=None):
            t = TSTAGE[n]
            for h in range(HALVES):
                for q in range(2):
                    eng.wait_ge(sem("turned"), 4 * t + 2 * h + q + 1)
                    o = (xT if dst is None else dst)[:, 4 * q:4 * q + 4, h * P:(h + 1) * P]
                    i = bank[4 + 2 * h + q][:, :].rearrange("p (c t) -> p c t", c=4)
                    if gain is None:
                        ins = eng.activation(o, i, ACT.Copy)
                    else:
                        ins = eng.tensor_tensor(o, i, bc(gain[:, 4 * q:4 * q + 4], 2, P), ALU.mult)
                    ins.then_inc(sem("xT_ready"), 1)

        cw = Carver(work, 0, WORK)
        raw = cw(QKV, SEQ + TAPS - 1)
        qkvT = cw(QKV, SEQ)
        zs = cw(HALVES, D)
        IDX = HALVES * HEADS
        DT = cw(IDX, P)
        LT = cw(IDX, P)
        Ut = cw(IDX, P)
        Wm = cw(IDX, P)
        gB = cw(IDX, P)
        kbB = cw(IDX, P)
        S = cw(HEADS, P)
        c2 = Carver(work, 0, QKV * (SEQ + TAPS - 1))
        vb, kd, kbg = c2(IDX, P), c2(IDX, P), c2(IDX, P)
        qT, kT, vT = (qkvT[:, HEADS * i:HEADS * (i + 1), :] for i in range(3))
        Tm = kT.rearrange("p h t -> p (h t)").rearrange("p (i c) -> p i c", i=IDX)
        Am = vT.rearrange("p h t -> p (h t)").rearrange("p (i c) -> p i c", i=IDX)
        sq = [t.rearrange("p i c -> p (i c)").rearrange("p (h t) -> p h t", h=HEADS) for t in (Wm, gB)]
        uu, wT, vnew, o_rows = LT, Am, Tm, gB
        oT = kbB.rearrange("p i c -> p (i c)").rearrange("p (h t) -> p h t", h=HEADS)
        HD = HEADS // 2

        def grp(t, G):
            return t[:, HD * G:HD * (G + 1), :]

        def bank3(b):
            return bank[b][:, :].rearrange("p (i c) -> p i c", i=HD)

        NGRP = IDX // HD

        gxh, gxl = (gx_r[:, 2 * D * n:2 * D * (n + 1)].rearrange("p (k t) -> p k t", k=DC) for n in range(2))
        GD_PIECES = QKV + 8

        def gd_unit(s):
            return U_QKV + s // 4

        def gd_piece(tile, s):
            w = tile[:, gd_unit(s) % RING, :].rearrange("p (k n) -> p k n", k=DC)
            return w[:, :, (s % 4) * P:(s % 4 + 1) * P] if s < QKV else w[:, 2 * (s % 4):2 * (s % 4) + 2, :]

        def gd_buffer(s):
            return gw_r[:, s % 3, :].rearrange("p (k n) -> p k n", k=DC if s < QKV else 2)

        def gd_on_vector(s):
            return s < QKV and s % 3 == 2

        def gd_high(act, s):
            unit_ready(act, gd_unit(s))
            r = s - 3
            if 0 <= r < QKV:
                act.wait_ge(sem("qkv_ps"), r + 1)
            elif r >= QKV:
                j, i = divmod(r - QKV, 4)
                if i < 3:
                    act.wait_ge(sem("z_used"), 3 * j + i + 1)
                else:
                    act.wait_ge(sem("z_ps"), 2 * (j + 1))
            act.activation(gd_buffer(s), gd_piece(ring, s), ACT.Copy).then_inc(sem("gdn_high"), 1)

        def gd_low(eng, s):
            eng.wait_ge(sem("gdn_high"), 1 + s + 1)
            eng.tensor_tensor(gd_piece(ring_r, s), gd_piece(ring, s), gd_buffer(s).bitcast(F32), ALU.subtract)\
               .then_inc(sem("gdn_low_vector" if gd_on_vector(s) else "gdn_low_pool"), 1)

        def gd_split(pe, s):
            n = sum(gd_on_vector(i) == gd_on_vector(s) for i in range(s + 1))
            if gd_on_vector(s):
                pe.wait_ge(sem("gdn_low_vector"), 1 + n)
            else:
                pe.wait_ge(sem("gdn_low_pool"), n)

        def gdn_tensor(pe):
            pe.wait_ge(sem("gdn_low_vector"), 1)
            for c in range(QKV):
                if c >= 4:
                    pe.wait_ge(sem("qkv_evac"), c - 3)
                gd_split(pe, c)
                wh_, wl_, o = gd_buffer(c), gd_piece(ring_r, c), bank[c % 4][:, 0:SEQ]
                for k in range(DC):
                    mm(o, wh_[:, k, :], gxh[:, k, :], k == 0, False)
                    mm(o, wl_[:, k, :], gxh[:, k, :], False, False)
                    ins = mm(o, wh_[:, k, :], gxl[:, k, :], False, k == DC - 1)
                ins.then_inc(sem("qkv_ps"), 1)
            pe.wait_ge(sem("small_loaded"), 16 * NLOADS)
            pe.wait_ge(sem("qkv_evac"), QKV - 3)
            for h in range(HALVES):
                for k in range(DC):
                    ins = mm(bank[0][:, 16 * h:16 * h + 16], xT[:, k, h * P:(h + 1) * P], w_ba[:, k, :],
                             k == 0, k == DC - 1)
            ins.then_inc(sem("ba_ps"), 1)
            pe.wait_ge(sem("qkv_evac"), QKV - 2)
            for c in range(2 * HEADS):
                pe.wait_ge(sem("sq_done"), c + 1)
                for h in range(HALVES):
                    ins = mm(bank[1][:, 2 * HEADS * h + c:2 * HEADS * h + c + 1],
                             sq[c // HEADS][:, c % HEADS, h * P:(h + 1) * P], ones[:, 0:1])
            ins.then_inc(sem("l2_ps"), 1)
            for j in range(2):
                for i in range(4):
                    s = QKV + 4 * j + i
                    gd_split(pe, s)
                    wh_, wl_ = gd_buffer(s), gd_piece(ring_r, s)
                    for h in range(HALVES):
                        o, t = bank[4 + 2 * j + h][:, :], slice(h * P, (h + 1) * P)
                        for k in range(2):
                            kk = 2 * i + k
                            mm(o, gxh[:, kk, t], wh_[:, k, :], kk == 0, False)
                            mm(o, gxl[:, kk, t], wh_[:, k, :], False, False)
                            ins = mm(o, gxh[:, kk, t], wl_[:, k, :], False, kk == DC - 1)
                        if i == 3:
                            ins.then_inc(sem("z_ps"), 1)
                    if i < 3:
                        ins.then_inc(sem("z_used"), 1)
            pe.wait_ge(sem("qkv_evac"), QKV)
            pe.wait_ge(sem("silu_done"), QKV)
            pe.wait_ge(sem("z_done"), 4)
            pe.wait_ge(sem("g_ready"), 1)
            for h in range(HALVES):
                mm(bank[0][:, 32 + 8 * h:40 + 8 * h], cum, g_t[:, h, :])
                mm(bank[0][:, 48 + 8 * h:56 + 8 * h], blk, g_t[:, h, :])
                mm(bank[0][:, 64 + 16 * h:72 + 16 * h], first64, g_t[:, h, :])
                ins = mm(bank[0][:, 72 + 16 * h:80 + 16 * h], last64, g_t[:, h, :])
            ins.then_inc(sem("gsum_ps"), 1)
            for G in range(NGRP):
                h, h0 = G // 2, HD * (G % 2)
                if G >= 2:
                    pe.wait_ge(sem("kd_done"), G - 1)
                    pe.wait_ge(sem("kbg_done"), G - 1)
                    pe.wait_ge(sem("vrows_done"), G - 1)
                for i in range(HD):
                    ins = pe.transpose(bank[4 + G % 2][:, i * P:(i + 1) * P], kT[:, h0 + i, h * P:(h + 1) * P], ident)
                ins.then_inc(sem("krows_ps"), 1)
                for i in range(HD):
                    ins = pe.transpose(bank[6 + G % 2][:, i * P:(i + 1) * P], vT[:, h0 + i, h * P:(h + 1) * P], ident)
                ins.then_inc(sem("vrows_ps"), 1)
            pe.wait_ge(sem("bcast_done"), 2)
            for G in range(NGRP):
                h, h0 = G // 2, HD * (G % 2)
                if G >= 1:
                    pe.wait_ge(sem("decay_arg"), HD * G)
                    pe.wait_ge(sem("lt_done"), G)
                for i in range(HD):
                    ins = mm(bank[2][:, i * P:(i + 1) * P], gB[:, HD * G + i, :], cum)
                ins.then_inc(sem("decay_ps"), 1)
                for i in range(HD):
                    mm(bank[3][:, i * P:(i + 1) * P], kbB[:, HD * G + i, :], ident)
                if G < 2:
                    pe.wait_ge(sem("kd_done"), G + 3)
                    pe.wait_ge(sem("kbg_done"), G + 3)
                    pe.wait_ge(sem("vrows_done"), G + 3)
                else:
                    pe.wait_ge(sem("at_done"), G - 1)
                for i in range(HD):
                    kk = kT[:, h0 + i, h * P:(h + 1) * P]
                    ins = mm(bank[4 + G % 2][:, i * P:(i + 1) * P], kk, kk)
                ins.then_inc(sem("kk_ps"), 1)
                for i in range(HD):
                    ins = mm(bank[6 + G % 2][:, i * P:(i + 1) * P], kT[:, h0 + i, h * P:(h + 1) * P],
                             qT[:, h0 + i, h * P:(h + 1) * P])
                ins.then_inc(sem("kq_ps"), 1)
            for m in range(6):
                for G in range(NGRP + 1):
                    if G < NGRP:
                        g = NGRP * m + G
                        pe.wait_ge(sem("a_done"), g + 1)
                        if m > 0:
                            pe.wait_ge(sem("t_done"), g - NGRP + 1)
                            pe.wait_ge(sem("u_done"), g - NGRP + 1)
                        if g >= 2:
                            pe.wait_ge(sem("w_evac"), g - 1)
                        for i in range(HD):
                            j = HD * G + i
                            ins = mm(bank[g % 2][:, i * P:(i + 1) * P], Am[:, j, :], ident if m == 0 else Tm[:, j, :])
                        ins.then_inc(sem("w_ps"), 1)
                    if G > 0 and m > 0:
                        g = NGRP * m + G - 1
                        pe.wait_ge(sem("w_evac"), g + 1)
                        if g >= NGRP + 2:
                            pe.wait_ge(sem("t_done"), min(g - 1, 5 * NGRP))
                            pe.wait_ge(sem("u_done"), g - 1)
                        if m < 5:
                            for i in range(HD):
                                j = HD * (G - 1) + i
                                ins = mm(bank[2 + g % 2][:, i * P:(i + 1) * P], Ut[:, j, :], Wm[:, j, :])
                        for i in range(HD):
                            j = HD * (G - 1) + i
                            ins = mm(bank[4 + g % 2][:, i * P:(i + 1) * P], Wm[:, j, :], Ut[:, j, :])
                        ins.then_inc(sem("wu_ps"), 1)
            pe.wait_ge(sem("w_evac"), 6 * NGRP)
            pe.wait_ge(sem("t_done"), 5 * NGRP)
            for G in range(NGRP):
                pe.wait_ge(sem("u_done"), 5 * NGRP + G + 1)
                if G >= 2:
                    pe.wait_ge(sem("uu_done"), G - 1)
                    pe.wait_ge(sem("wt_done"), G - 1)
                for i in range(HD):
                    j = HD * G + i
                    ins = mm(bank[G % 2][:, i * P:(i + 1) * P], Ut[:, j, :], vb[:, j, :])
                ins.then_inc(sem("uu_ps"), 1)
                for i in range(HD):
                    j = HD * G + i
                    ins = mm(bank[2 + G % 2][:, i * P:(i + 1) * P], kbg[:, j, :], Ut[:, j, :])
                ins.then_inc(sem("wt_ps"), 1)
            pe.wait_ge(sem("uu_done"), NGRP)
            pe.wait_ge(sem("wt_done"), NGRP)
            for n in range(2 * HALVES):
                h, r = n // 2, CHUNK * (n % 2)
                rows = slice(r, r + CHUNK)
                if n > 0:
                    for e in range(HEADS):
                        j = HEADS * h + e
                        pe.wait_ge(sem("state_done"), HEADS * (n - 1) + e + 1)
                        ins = mm(bank[e // HD][rows, (e % HD) * P:(e % HD + 1) * P], wT[:, j, rows], S[:, e, :])
                        if e % HD == HD - 1:
                            ins.then_inc(sem("ws_ps"), 1)
                    for e in range(HEADS):
                        ins = mm(bank[2 + e // HD][rows, (e % HD) * P:(e % HD + 1) * P],
                                 qT[:, e, h * P + r:h * P + r + CHUNK], S[:, e, :])
                        if e % HD == HD - 1:
                            ins.then_inc(sem("qs_ps"), 1)
                for b in range(2):
                    pe.wait_ge(sem("vnew_done"), 2 * n + b + 1)
                    if n < 2 * HALVES - 1:
                        for i in range(HD):
                            j = HEADS * h + HD * b + i
                            ins = mm(bank[4 + b][:, i * P:(i + 1) * P], kd[rows, j, :], vnew[rows, j, :])
                        ins.then_inc(sem("ds_ps"), 1)
                if n % 2 == 1:
                    for b in range(2):
                        if h > 0:
                            pe.wait_ge(sem("o_sum"), b + 1)
                        for i in range(HD):
                            j = HEADS * h + HD * b + i
                            ins = mm(bank[6 + b][:, i * P:(i + 1) * P], DT[:, j, :], vnew[:, j, :])
                        ins.then_inc(sem("oi_ps"), 1)
            for G in range(NGRP):
                h, h0 = G // 2, HD * (G % 2)
                pe.wait_ge(sem("o_gated"), h + 1)
                for i in range(HD):
                    ins = pe.transpose(bank[G][:, i * P:(i + 1) * P], o_rows[:, HD * G + i, :], ident)
                ins.then_inc(sem("ot_ps"), 1)
            pe.wait_ge(sem("ot_done"), NGRP)
            for j in range(2):
                unit_ready(pe, U_WOUT + j)
                w = slot(U_WOUT + j).rearrange("p (k n) -> p k n", k=DC)
                for h in range(HALVES):
                    for k in range(DC):
                        ins = mm(bank[4 + 2 * j + h][:, :], oT[:, k, h * P:(h + 1) * P], w[:, k, :], k == 0, k == DC - 1)
                    ins.then_inc(sem("wout_ps"), 1)

        def gdn_scalar(act):
            act.dma_start(conv_w, I["conv_w"]).then_inc(sem("first_loaded"), 16)
            act.wait_ge(sem("first_loaded"), 32)
            act.activation(gxh[:, :, :], xT[:, :, :], ACT.Copy).then_inc(sem("gdn_high"), 1)
            for s in range(3):
                gd_high(act, s)
            for c in range(QKV + 2):
                if c < QKV:
                    gd_high(act, c + 3)
                    act.wait_ge(sem("qkv_ps"), c + 1)
                    act.activation(raw[:, c, TAPS - 1:], bank[c % 4][:, 0:SEQ], ACT.Copy).then_inc(sem("qkv_evac"), 1)
                if c >= 2:
                    act.wait_ge(sem("conv_done"), c - 1)
                    act.activation(qkvT[:, c - 2, :], qkvT[:, c - 2, :], ACT.Silu).then_inc(sem("silu_done"), 1)
            act.wait_ge(sem("gate_in"), 1)
            act.activation(beta[:, :, :], ba[:, :, 0:HEADS], ACT.Sigmoid).then_inc(sem("beta_done"), 1)
            act_link(act, act.activation(sp_a[:, :, :], sp_a[:, :, :], ACT.Exp, scale=-1.0))
            act.activation(a_log, a_log, ACT.Exp).then_inc(sem("sp_done"), 1)
            act.activation(sp_a[:, :, :], sp_a[:, :, :], ACT.Ln, bias=1.0).then_inc(sem("sp_done"), 1)
            act.wait_ge(sem("rn_inv"), 1)
            act.activation(rn[:, :, :], rn[:, :, :], ACT.Sqrt).then_inc(sem("rn_done"), 1)
            for s in range(QKV + 3, GD_PIECES):
                gd_high(act, s)
            for j in range(2):
                for h in range(HALVES):
                    act.wait_ge(sem("z_ps"), 2 * j + h + 1)
                    act.activation(zs[:, h, 512 * j:512 * j + 512], bank[4 + 2 * j + h][:, :], ACT.Silu).then_inc(sem("z_done"), 1)
            act.wait_ge(sem("gsum_done"), 2)
            act.activation(eg[:, :, :], gc[:, :, :], ACT.Exp).then_inc(sem("eg_done"), 1)
            act.activation(kd_s[:, :, :], kd_s[:, :, :], ACT.Exp).then_inc(sem("eg_done"), 1)
            act.activation(s_scale[:, :, :], bank[0][:, 64:96].rearrange("p (n h) -> p n h", n=2 * HALVES),
                           ACT.Exp).then_inc(sem("eg_done"), 1)
            act.wait_ge(sem("scalars_done"), 1)
            for G in range(NGRP):
                act.wait_ge(sem("krows_ps"), G + 1)
                for i in range(HD):
                    h, e = G // 2, HD * (G % 2) + i
                    ins = act.activation(kd[:, HD * G + i, :], bank[4 + G % 2][:, i * P:(i + 1) * P], ACT.Copy,
                                         scale=kd_s[:, h, e:e + 1])
                ins.then_inc(sem("kd_done"), 1)
                act.wait_ge(sem("vrows_ps"), G + 1)
                for i in range(HD):
                    h, e = G // 2, HD * (G % 2) + i
                    ins = act.activation(vb[:, HD * G + i, :], bank[6 + G % 2][:, i * P:(i + 1) * P], ACT.Copy,
                                         scale=beta[:, h, e:e + 1])
                ins.then_inc(sem("vrows_done"), 1)
            for G in range(NGRP):
                act.wait_ge(sem("decay_arg"), HD * (G + 1))
                act.activation(grp(DT, G), grp(DT, G), ACT.Exp).then_inc(sem("decay_done"), 1)
            for g in range(6 * NGRP):
                act.wait_ge(sem("w_ps"), g + 1)
                if g >= 2 * NGRP:
                    act.wait_ge(sem("wu_ps"), g - 2 * NGRP + 1)
                act.activation(grp(Wm, g % NGRP), bank3(g % 2), ACT.Copy).then_inc(sem("w_evac"), 1)
            for G in range(NGRP):
                act.wait_ge(sem("wt_ps"), G + 1)
                act.activation(grp(wT, G), bank3(2 + G % 2), ACT.Copy).then_inc(sem("wt_done"), 1)
            act.wait_ge(sem("oms_inv"), 1)
            act.activation(of[:, :, :], of[:, :, :], ACT.Sqrt).then_inc(sem("of_done"), 1)
            for G in range(NGRP):
                h, h0 = G // 2, HD * (G % 2)
                act.wait_ge(sem("ot_ps"), G + 1)
                act.activation(oT[:, h0:h0 + HD, h * P:(h + 1) * P], bank3(G), ACT.Copy).then_inc(sem("ot_done"), 1)
            norm_scalar(act, 0)
            turn_evacuate(act, 0, None, xT_r)

        def gdn_vector(v):
            v.wait_ge(sem("gdn_high"), 1)
            v.tensor_tensor(gxl[:, :, :], xT[:, :, :], gxh[:, :, :].bitcast(F32), ALU.subtract).then_inc(sem("gdn_low_vector"), 1)
            gd_low(v, 2)
            v.wait_ge(sem("pad_done"), 1)
            for c in range(QKV):
                if c + 3 < QKV and gd_on_vector(c + 3):
                    gd_low(v, c + 3)
                v.wait_ge(sem("qkv_evac"), c + 1)
                acc = qkvT[:, c, :]
                dve_link(v, v.tensor_scalar(acc, raw[:, c, 0:SEQ], conv_w[:, c, 0:1], None, ALU.mult))
                for k in range(1, TAPS):
                    ins = v.scalar_tensor_tensor(acc, raw[:, c, k:k + SEQ], conv_w[:, c, k:k + 1], acc, ALU.mult, ALU.add)
                    if k < TAPS - 1:
                        dve_link(v, ins)
                ins.then_inc(sem("conv_done"), 1)
            v.wait_ge(sem("ba_ps"), 1)
            v.wait_ge(sem("small_loaded"), 16 * NLOADS)
            dve_link(v, v.tensor_copy(ba[:, :, :], bank[0][:, 0:32].rearrange("p (h n) -> p h n", h=HALVES)))
            dve_link(v, v.tensor_tensor(sp_t[:, :, :], ba[:, :, HEADS:], bc(dt_bias, 1, HALVES), ALU.add))
            dve_link(v, v.tensor_scalar(sp_a[:, :, :], sp_t[:, :, :], -1.0, None, ALU.mult))
            v.tensor_tensor(sp_a[:, :, :], sp_a[:, :, :], sp_t[:, :, :], ALU.max).then_inc(sem("gate_in"), 1)
            v.wait_ge(sem("gate_in"), 1)
            dve_link(v, v.tensor_scalar(sp_t[:, :, :], sp_t[:, :, :], 0.0, None, ALU.max))
            v.wait_ge(sem("l2_ps"), 1)
            dve_link(v, v.tensor_scalar(rn[:, :, :], bank[1][:, 0:4 * HEADS].rearrange("p (h n) -> p h n", h=HALVES),
                                        NORM_EPS, None, ALU.add))
            v.reciprocal(rn[:, :, :], rn[:, :, :]).then_inc(sem("rn_inv"), 1)
            v.wait_ge(sem("sp_done"), 2)
            dve_link(v, v.tensor_tensor(sp_t[:, :, :], sp_t[:, :, :], sp_a[:, :, :], ALU.add))
            v.scalar_tensor_tensor(g_t[:, :, :], sp_t[:, :, :], -1.0, bc(a_log, 1, HALVES), ALU.mult, ALU.mult)\
             .then_inc(sem("g_ready"), 1)
            v.wait_ge(sem("gsum_ps"), 1)
            v.tensor_copy(gc[:, :, :], bank[0][:, 32:48].rearrange("p (h n) -> p h n", h=HALVES)).then_inc(sem("gsum_done"), 1)
            v.wait_ge(sem("gsum_done"), 1)
            v.tensor_tensor(kd_s[:, :, :], bank[0][:, 48:64].rearrange("p (h n) -> p h n", h=HALVES), gc[:, :, :],
                            ALU.subtract).then_inc(sem("gsum_done"), 1)
            v.wait_ge(sem("eg_done"), 3)
            v.wait_ge(sem("rn_done"), 1)
            v.wait_ge(sem("beta_done"), 1)
            dve_link(v, v.tensor_tensor(kb_s[:, :, :], rn[:, :, HEADS:], beta[:, :, :], ALU.mult))
            v.tensor_scalar(rq_s[:, :, :], rn[:, :, 0:HEADS], float(P) ** -0.5, None, ALU.mult)
            v.tensor_tensor(kbg_s[:, :, :], kb_s[:, :, :], eg[:, :, :], ALU.mult)
            v.tensor_tensor(kd_s[:, :, :], kd_s[:, :, :], rn[:, :, HEADS:], ALU.mult).then_inc(sem("scalars_done"), 1)
            v.wait_ge(sem("scalars_done"), 1)
            v.wait_ge(sem("l2_ps"), 1)
            v.tensor_copy(gB[:, :, :], bc(g_t.rearrange("p a b -> p (a b)"), 2, P)).then_inc(sem("bcast_done"), 1)
            v.tensor_copy(kbB[:, :, :], bc(kb_s.rearrange("p a b -> p (a b)"), 2, P)).then_inc(sem("bcast_done"), 1)
            for G in range(NGRP):
                v.wait_ge(sem("kd_done"), G + 1)
                for i in range(HD):
                    h, e = G // 2, HD * (G % 2) + i
                    ins = v.tensor_scalar(kbg[:, HD * G + i, :], bank[4 + G % 2][:, i * P:(i + 1) * P],
                                          kbg_s[:, h, e:e + 1], None, ALU.mult)
                ins.then_inc(sem("kbg_done"), 1)
            for G in range(NGRP):
                h, h0 = G // 2, HD * (G % 2)
                v.wait_ge(sem("decay_ps"), G + 1)
                for i in range(HD):
                    v.scalar_tensor_tensor(DT[:, HD * G + i, :], bank[2][:, i * P:(i + 1) * P], gc[:, h, h0 + i:h0 + i + 1],
                                           negm, ALU.subtract, ALU.add).then_inc(sem("decay_arg"), 1)
                v.wait_ge(sem("kk_ps"), G + 1)
                v.wait_ge(sem("decay_done"), G + 1)
                for i in range(HD):
                    ins = v.scalar_tensor_tensor(LT[:, HD * G + i, :], bank[4 + G % 2][:, i * P:(i + 1) * P],
                                                 rn[:, h, HEADS + h0 + i:HEADS + h0 + i + 1], DT[:, HD * G + i, :],
                                                 ALU.mult, ALU.mult)
                dve_link(v, ins)
                v.tensor_tensor(grp(LT, G), grp(LT, G), bank3(3), ALU.mult).then_inc(sem("lt_done"), 1)
                v.wait_ge(sem("kq_ps"), G + 1)
                for i in range(HD):
                    ins = v.scalar_tensor_tensor(DT[:, HD * G + i, :], bank[6 + G % 2][:, i * P:(i + 1) * P],
                                                 rn[:, h, HEADS + h0 + i:HEADS + h0 + i + 1], DT[:, HD * G + i, :],
                                                 ALU.mult, ALU.mult)
                ins.then_inc(sem("at_done"), 1)
            v.wait_ge(sem("at_done"), NGRP)
            for m in range(6):
                for G in range(NGRP):
                    g = NGRP * m + G
                    if m > 0:
                        v.wait_ge(sem("w_ps"), g - NGRP + 1)
                    if m == 1:
                        v.wait_ge(sem("u_done"), G + 1)
                    v.wait_ge(sem("lt_done"), G + 1)
                    v.tensor_tensor(grp(Am, G), grp(LT, G), bc(lvl[m], 1, HD), ALU.mult).then_inc(sem("a_done"), 1)
                for G in range(NGRP):
                    g = NGRP * m + G
                    idb = bc(ident, 1, HD)
                    if m == 0:
                        v.wait_ge(sem("w_evac"), g + 1)
                        v.tensor_tensor(grp(Tm, G), idb, grp(Wm, G), ALU.subtract).then_inc(sem("t_done"), 1)
                        v.wait_ge(sem("a_done"), g + 1)
                        v.tensor_tensor(grp(Ut, G), idb, grp(Am, G), ALU.subtract).then_inc(sem("u_done"), 1)
                        continue
                    v.wait_ge(sem("wu_ps"), g - NGRP + 1)
                    if m < 5:
                        v.wait_ge(sem("t_done"), g - NGRP + 1)
                        v.tensor_tensor(grp(Tm, G), grp(Tm, G), bank3(2 + g % 2), ALU.subtract).then_inc(sem("t_done"), 1)
                    v.wait_ge(sem("u_done"), g - NGRP + 1)
                    v.tensor_tensor(grp(Ut, G), grp(Ut, G), bank3(4 + g % 2), ALU.subtract).then_inc(sem("u_done"), 1)
            for G in range(NGRP):
                v.wait_ge(sem("uu_ps"), G + 1)
                v.tensor_copy(grp(uu, G), bank3(G % 2)).then_inc(sem("uu_done"), 1)
            v.wait_ge(sem("uu_done"), NGRP)
            v.wait_ge(sem("t_done"), 5 * NGRP)
            for n in range(2 * HALVES):
                h, r = n // 2, CHUNK * (n % 2)
                rows = slice(r, r + CHUNK)
                for b in range(2):
                    j = slice(HEADS * h + HD * b, HEADS * h + HD * b + HD)
                    if n == 0:
                        v.tensor_copy(vnew[rows, j, :], uu[rows, j, :]).then_inc(sem("vnew_done"), 1)
                    else:
                        v.wait_ge(sem("ws_ps"), 2 * (n - 1) + b + 1)
                        v.tensor_tensor(vnew[rows, j, :], uu[rows, j, :], bank3(b)[rows], ALU.subtract).then_inc(sem("vnew_done"), 1)
                for b in range(2):
                    j = slice(HEADS * h + HD * b, HEADS * h + HD * b + HD)
                    if n == 0:
                        v.memset(o_rows[rows, j, :], 0.0).then_inc(sem("o1_done"), 1)
                    else:
                        v.wait_ge(sem("qs_ps"), 2 * (n - 1) + b + 1)
                        v.tensor_tensor(o_rows[rows, j, :], bank3(2 + b)[rows], bc(eg[rows, h, HD * b:HD * b + HD], 2, P),
                                        ALU.mult).then_inc(sem("o1_done"), 1)
                if n < 2 * HALVES - 1:
                    for e in range(HEADS):
                        if e % HD == 0:
                            v.wait_ge(sem("ds_ps"), 2 * n + e // HD + 1)
                        src = bank[4 + e // HD][:, (e % HD) * P:(e % HD + 1) * P]
                        if n == 0:
                            ins = v.tensor_copy(S[:, e, :], src)
                        else:
                            v.wait_ge(sem("state_done"), HEADS * (n - 1) + e + 1)
                            ins = v.scalar_tensor_tensor(S[:, e, :], S[:, e, :], s_scale[:, n, e:e + 1], src, ALU.mult, ALU.add)
                        ins.then_inc(sem("state_done"), 1)
                if n % 2 == 1:
                    v.wait_ge(sem("o1_done"), 2 * (n + 1))
                    for b in range(2):
                        j = slice(HEADS * h + HD * b, HEADS * h + HD * b + HD)
                        v.wait_ge(sem("oi_ps"), 2 * h + b + 1)
                        v.tensor_tensor(o_rows[:, j, :], o_rows[:, j, :], bank3(6 + b), ALU.add).then_inc(sem("o_sum"), 1)
            v.wait_ge(sem("o_sum"), 4)
            osq = Wm
            dve_link(v, v.tensor_tensor(osq[:, :, :], o_rows[:, :, :], o_rows[:, :, :], ALU.mult))
            omsf = oms.rearrange("p a b -> p (a b)")
            off = of.rearrange("p a b -> p (a b)")
            rqf = rq_s.rearrange("p a b -> p (a b)")
            dve_link(v, v.tensor_reduce(omsf, osq[:, :, :], AX.X, ALU.add))
            dve_link(v, v.tensor_tensor(omsf, omsf, rqf, ALU.mult))
            dve_link(v, v.tensor_tensor(omsf, omsf, rqf, ALU.mult))
            dve_link(v, v.tensor_scalar(omsf, omsf, 1.0 / P, NORM_EPS, ALU.mult, ALU.add))
            v.reciprocal(off, omsf).then_inc(sem("oms_inv"), 1)
            v.wait_ge(sem("of_done"), 1)
            dve_link(v, v.tensor_tensor(off, off, rqf, ALU.mult))
            v.wait_ge(sem("zg_done"), HALVES)
            for h in range(HALVES):
                for e in range(HEADS):
                    o_h = o_rows[:, HEADS * h + e, :]
                    ins = v.scalar_tensor_tensor(o_h, o_h, of[:, h, e:e + 1], zs[:, h, P * e:P * (e + 1)], ALU.mult, ALU.mult)
                ins.then_inc(sem("o_gated"), 1)
            for j in range(2):
                for h in range(HALVES):
                    v.wait_ge(sem("wout_ps"), 2 * j + h + 1)
                    xs = xres[:, h, 512 * j:512 * j + 512]
                    ins = v.scalar_tensor_tensor(xs, xs, ALPHA, bank[4 + 2 * j + h][:, :], ALU.mult, ALU.add)
                    norm_stats(v, 0, xres, h, j, ins)
            norm_vector(v, 0, xres, xres)
            for h in range(HALVES):
                for q in range(2):
                    o = (slice(None), slice(4 * q, 4 * q + 4), slice(h * P, (h + 1) * P))
                    v.wait_ge(sem("xT_ready"), 2 * h + q + 1)
                    v.tensor_tensor(xl[o], bank3(4 + 2 * h + q), xT_r[o].bitcast(F32), ALU.subtract).then_inc(sem("xl_ready"), 1)

        def gdn_gpsimd(g):
            g.memset(raw[:, :, 0:TAPS - 1], 0.0).then_inc(sem("pad_done"), 1)
            for s in range(GD_PIECES):
                if not gd_on_vector(s):
                    gd_low(g, s)
                c = s - 5
                if 0 <= c < 2 * HEADS:
                    g.wait_ge(sem("silu_done"), c + 1)
                    g.tensor_tensor(sq[c // HEADS][:, c % HEADS, :], qkvT[:, c, :], qkvT[:, c, :], ALU.mult)\
                     .then_inc(sem("sq_done"), 1)
            g.wait_ge(sem("z_done"), 4)
            g.wait_ge(sem("small_loaded"), 16 * NLOADS)
            for h in range(HALVES):
                z_h = zs[:, h, :].rearrange("p (e d) -> p e d", e=HEADS)
                g.tensor_tensor(z_h, z_h, bc(norm_g, 1, HEADS), ALU.mult).then_inc(sem("zg_done"), 1)

        def load_norm(eng, n):
            eng.dma_start(lnp[:, 0, :], I["ln_rows"][n, 0]).then_inc(sem("lnp_loaded"), 16)
            eng.dma_start(lnp[:, 1, :], I["ln_rows"][n, 1]).then_inc(sem("lnp_loaded"), 16)

        fw = Carver(work, 0, WORK)
        bt = fw(DC, 4, P)
        y0re = fw(PAIRS, 32)
        y0im = fw(PAIRS, 32)
        y1re = fw(PAIRS, 32)
        y1im = fw(PAIRS, 32)
        k0 = fw(DC, P)
        s5_phase_at = fw.at
        cosT = fw(PAIRS, NSTEP)
        sinT = fw(PAIRS, NSTEP)
        uT = fw(DC, SEQ)
        s5_hid = fw(DC, SEQ)
        rot_r, rot_i, pw_r, pw_i, decay2 = (fw(PAIRS) for _ in range(5))
        s5_tmp_at = fw.at
        NP2 = DC * S5_STATE + PAIRS
        fp = Carver(work, s5_tmp_at, WORK)
        lam_re, lam_im, dt, lr, th, rho, kk_, sn, ar, ai, t0, t1 = (fp(NP2) for _ in range(12))
        bbar_r, bbar_i = fp(PAIRS, 32), fp(PAIRS, 32)
        cc_ = Carver(work, s5_phase_at, s5_phase_at + 2 * PAIRS * NSTEP)
        b1_re, b1_im, m1 = cc_(PAIRS, 32), cc_(PAIRS, 32), cc_(PAIRS, 32)
        b2_re, b2_im, br_, bi_, m2, abr, abi = (cc_(DC, S5_STATE) for _ in range(7))
        assert K0_AT == DC * 4 * P + 4 * PAIRS * 32 and FFN_R_AT == K0_AT + D + 2 * PAIRS * NSTEP
        fr = Carver(ffn_r, 0, 3 * D + 2 * SEQ)
        xl = fr(DC, SEQ)
        ff_hh, ff_hl = fr(3, SEQ), fr(3, SEQ)
        ff_high = [lnp_r[:, 0, :], lnp_r[:, 1, :], k0_r[:, :]]
        ff_silu = [s5_hid[:, 6 + i, :] for i in range(2)]
        FF_ORDER = []
        for b, nch in enumerate(FF_BLOCKS * 2):
            for c in range(nch):
                FF_ORDER += [("g", b, c), ("u", b, c)] + ([("d", b, c - 2)] if c >= 2 else [])
            FF_ORDER += [("d", b, nch - 2), ("d", b, nch - 1)]
        FF_PIECES = len(FF_ORDER)
        NCH = 2 * sum(FF_BLOCKS)
        TWO_PI = 2 * np.pi
        C1 = float(np.float32(6.28125))
        C2 = float(np.float32(TWO_PI - C1))
        C2 = float(np.frombuffer((np.frombuffer(np.float32(C2).tobytes(), np.uint32) & 0xFFFFF000).tobytes(), np.float32)[0])
        C3 = float(np.float32(TWO_PI - C1 - C2))
        MAGIC = 1.5 * 2.0 ** 23
        PI_LO = float(np.nextafter(np.float32(np.pi), np.float32(0)))
        LOADS_S5 = 9

        def ff_unit(s):
            kind, b, c = FF_ORDER[s]
            return U_FFN + 3 * b + "gud".index(kind)

        def ff_piece(tile, s):
            kind, b, c = FF_ORDER[s]
            nch = FF_BLOCKS[b % 3]
            w = tile[:, ff_unit(s) % RING, 0:D * nch]
            if kind == "d":
                return w[:, D * c:D * (c + 1)]
            return w.rearrange("p (k n) -> p k n", k=DC)[:, :, c * P:(c + 1) * P]

        def ff_buffer(s):
            o = ff_high[s % 3]
            return o if FF_ORDER[s][0] == "d" else o.rearrange("p (k n) -> p k n", k=DC)

        def ff_chunk(b, c):
            return sum((FF_BLOCKS * 2)[:b]) + c

        def ffn_tensor(pe):
            for s, (kind, b, c) in enumerate(FF_ORDER):
                pe.wait_ge(sem("ffn_split"), s + 1)
                wh_, wl_ = ff_buffer(s), ff_piece(ring_r, s)
                f = ff_chunk(b, c)
                if kind == "d":
                    pe.wait_ge(sem("ffn_hid"), f + 1)
                    hh, hl = ff_hh[:, f % 3, :], ff_hl[:, f % 3, :]
                    for h in range(HALVES):
                        t = slice(h * P, (h + 1) * P)
                        for j in range(2):
                            n = slice(512 * j, 512 * j + 512)
                            o = bank[2 * h + j][:, :]
                            mm(o, hh[:, t], wh_[:, n], f == 0, False)
                            mm(o, hl[:, t], wh_[:, n], False, False)
                            ins = mm(o, hh[:, t], wl_[:, n], False, f == NCH - 1)
                else:
                    o = bank[4 + c][:, 0:SEQ] if kind == "g" else bank[4 + c][:, SEQ:]
                    if kind == "g" and b > 0:
                        pe.wait_ge(sem("ffn_hid"), ff_chunk(b - 1, min(c, FF_BLOCKS[(b - 1) % 3] - 1)) + 1)
                    for k in range(DC):
                        mm(o, wh_[:, k, :], xT_r[:, k, :], k == 0, False)
                        mm(o, wl_[:, k, :], xT_r[:, k, :], False, False)
                        ins = mm(o, wh_[:, k, :], xl[:, k, :], False, k == DC - 1)
                ins.then_inc(sem("ffn_used"), 1)

        def ffn_scalar(act):
            for name, dst in (("lam_re", lam_re), ("lam_im", lam_im), ("log_dt", dt), ("c_re", y0re), ("c_im", y0im),
                              ("b1_re", b1_re), ("b1_im", b1_im), ("b2_re", b2_re), ("b2_im", b2_im)):
                act.dma_start(dst, I[name]).then_inc(sem("s5_loaded"), 16)
            for s in range(FF_PIECES + 5):
                if s < FF_PIECES:
                    unit_ready(act, ff_unit(s))
                    if s >= 3:
                        act.wait_ge(sem("ffn_used"), s - 2)
                    act.activation(ff_buffer(s), ff_piece(ring, s), ACT.Copy).then_inc(sem("ffn_high"), 1)
                if 0 <= s - 3 < FF_PIECES and FF_ORDER[s - 3][0] == "g":
                    kind, b, c = FF_ORDER[s - 3]
                    f = ff_chunk(b, c)
                    act.wait_ge(sem("ffn_used"), s - 1)
                    if f >= 2:
                        act.wait_ge(sem("ffn_hid"), f - 1)
                    act.activation(ff_silu[f % 2], bank[4 + c][:, 0:SEQ], ACT.Silu).then_inc(sem("ffn_silu"), 1)
                if 0 <= s - 4 < FF_PIECES and FF_ORDER[s - 4][0] == "g":
                    kind, b, c = FF_ORDER[s - 4]
                    f = ff_chunk(b, c)
                    act.wait_ge(sem("ffn_mul"), f + 1)
                    if f >= 3:
                        act.wait_ge(sem("ffn_used"), FF_ORDER.index(("d",) + ff_bc(f - 3)) + 1)
                    act.activation(ff_hh[:, f % 3, :], ff_silu[f % 2], ACT.Copy).then_inc(sem("ffn_hh"), 1)
                if s == 3:
                    act.wait_ge(sem("s5_loaded"), 16 * LOADS_S5)
                    act.activation(dt, dt, ACT.Exp).then_inc(sem("s5_dt"), 1)
                if s == 6:
                    act.wait_ge(sem("s5_lr"), 1)
                    act.activation(rho, lr, ACT.Exp).then_inc(sem("s5_polar"), 1)
                if s == 8:
                    act.wait_ge(sem("s5_theta"), 1)
                    act.activation(sn, th, ACT.Sin).then_inc(sem("s5_polar"), 1)
                    act.activation(t0, th, ACT.Sin, scale=0.5).then_inc(sem("s5_polar"), 1)
            assert FF_PIECES % 3 == 0
            for i in range(2):
                act.wait_ge(sem("ffn_used"), FF_PIECES - 2 + i)
                act.dma_start(lnp[:, i, :], I["ln_rows"][1, i]).then_inc(sem("lnp_loaded"), 16)
            norm_scalar(act, 1)
            turn_evacuate(act, 1, None)

        def ff_bc(f):
            b = 0
            while f >= FF_BLOCKS[b % 3]:
                f -= FF_BLOCKS[b % 3]
                b += 1
            return b, f

        def ffn_vector(v):
            for s in range(FF_PIECES + 5):
                if 0 <= s - 4 < FF_PIECES and FF_ORDER[s - 4][0] == "g":
                    kind, b, c = FF_ORDER[s - 4]
                    f = ff_chunk(b, c)
                    v.wait_ge(sem("ffn_silu"), f + 1)
                    v.tensor_tensor(ff_silu[f % 2], ff_silu[f % 2], bank[4 + c][:, SEQ:], ALU.mult).then_inc(sem("ffn_mul"), 1)
                if s < FF_PIECES:
                    v.wait_ge(sem("ffn_high"), s + 1)
                    v.tensor_tensor(ff_piece(ring_r, s), ff_piece(ring, s), ff_buffer(s).bitcast(F32), ALU.subtract)\
                     .then_inc(sem("ffn_split"), 1)
                if 0 <= s - 4 < FF_PIECES and FF_ORDER[s - 4][0] == "g":
                    f = ff_chunk(*FF_ORDER[s - 4][1:])
                    v.wait_ge(sem("ffn_hh"), f + 1)
                    v.tensor_tensor(ff_hl[:, f % 3, :], ff_silu[f % 2], ff_hh[:, f % 3, :].bitcast(F32), ALU.subtract)\
                     .then_inc(sem("ffn_hid"), 1)
                if s == 4:
                    v.wait_ge(sem("s5_dt"), 1)
                    v.tensor_tensor(lr, lam_re, dt, ALU.mult).then_inc(sem("s5_lr"), 1)
                    v.tensor_scalar(y0im[:, :, :], y0im[:, :, :], -1.0, None, ALU.mult).then_inc(sem("c_negated"), 1)
                    dve_link(v, v.tensor_tensor(th, lam_im, dt, ALU.mult))
                if s == 6:
                    dve_link(v, v.tensor_scalar(kk_, th, 1.0 / TWO_PI, MAGIC, ALU.mult, ALU.add))
                    dve_link(v, v.tensor_scalar(kk_, kk_, MAGIC, None, ALU.subtract))
                    for c in (C1, C2, C3):
                        dve_link(v, v.scalar_tensor_tensor(th, kk_, -c, th, ALU.mult, ALU.add))
                    v.tensor_scalar(th, th, PI_LO, -PI_LO, ALU.min, ALU.max).then_inc(sem("s5_theta"), 1)
                if s == 10:
                    v.wait_ge(sem("s5_polar"), 3)
                    dve_link(v, v.tensor_tensor(t0, t0, t0, ALU.mult))
                    dve_link(v, v.tensor_scalar(t0, t0, -2.0, 1.0, ALU.mult, ALU.add))
                    st = slice(DC * S5_STATE, NP2)
                    dve_link(v, v.tensor_tensor(t1[:, st], t0[:, st], t0[:, st], ALU.mult))
                    dve_link(v, v.tensor_tensor(rot_r, sn[:, st], sn[:, st], ALU.mult))
                    dve_link(v, v.tensor_tensor(rot_r, t1[:, st], rot_r, ALU.subtract))
                    dve_link(v, v.tensor_tensor(t1[:, st], t0[:, st], sn[:, st], ALU.mult))
                    dve_link(v, v.tensor_scalar(rot_i, t1[:, st], 2.0, None, ALU.mult))
                if s == 12:
                    dve_link(v, v.tensor_tensor(ar, rho, t0, ALU.mult))
                    dve_link(v, v.tensor_tensor(ai, rho, sn, ALU.mult))
                    v.tensor_tensor(decay2, rho[:, st], rho[:, st], ALU.mult).then_inc(sem("s5_a"), 1)
                    v.wait_ge(sem("s5_a"), 1)
                    dve_link(v, v.tensor_scalar(t0, ar, 1.0, None, ALU.subtract))
                if s == 14:
                    dve_link(v, v.tensor_tensor(kk_, lam_re, lam_re, ALU.mult))
                    dve_link(v, v.tensor_tensor(t1, lam_im, lam_im, ALU.mult))
                    dve_link(v, v.tensor_tensor(kk_, kk_, t1, ALU.add))
                    dve_link(v, v.reciprocal(kk_, kk_))
                if s == 17:
                    dve_link(v, v.tensor_tensor(rho, t0, lam_re, ALU.mult))
                    dve_link(v, v.tensor_tensor(t1, ai, lam_im, ALU.mult))
                    dve_link(v, v.tensor_tensor(rho, rho, t1, ALU.add))
                    dve_link(v, v.tensor_tensor(sn, ai, lam_re, ALU.mult))
                    dve_link(v, v.tensor_tensor(t1, t0, lam_im, ALU.mult))
                    dve_link(v, v.tensor_tensor(sn, sn, t1, ALU.subtract))
                if s == 19:
                    v.tensor_tensor(rho, rho, kk_, ALU.mult).then_inc(sem("s5_coef"), 1)
                    v.tensor_tensor(sn, sn, kk_, ALU.mult).then_inc(sem("s5_coef"), 1)
            v.wait_ge(sem("ffn_used"), FF_PIECES)
            for h in range(HALVES):
                for j in range(2):
                    xs = xres[:, h, 512 * j:512 * j + 512]
                    ins = v.scalar_tensor_tensor(xs, xs, ALPHA, bank[2 * h + j][:, :], ALU.mult, ALU.add)
                    norm_stats(v, 1, xres, h, j, ins)
            norm_vector(v, 1, xres, xres)

        def cmul(g, o_r, o_i, a_r, a_i, b_r, b_i, tmp, conj=False):
            g.tensor_tensor(o_r, a_r, b_r, ALU.mult)
            pool_link(g, g.tensor_tensor(tmp, a_i, b_i, ALU.mult))
            pool_link(g, g.tensor_tensor(o_r, o_r, tmp, ALU.add if conj else ALU.subtract))
            g.tensor_tensor(o_i, a_r, b_i, ALU.mult)
            pool_link(g, g.tensor_tensor(tmp, a_i, b_r, ALU.mult))
            pool_link(g, g.tensor_tensor(o_i, o_i, tmp, ALU.add))

        def ffn_gpsimd(g):
            g.wait_ge(sem("s5_a"), 1)
            l2 = slice(0, DC * S5_STATE)
            l1 = slice(DC * S5_STATE, NP2)

            def rows2(t):
                return t[:, l2].rearrange("p (q s) -> p q s", q=DC)

            def st1(t):
                return bc(t[:, l1], 2, 32)

            g.wait_ge(sem("c_negated"), 1)
            pool_link(g, g.tensor_tensor(m1[:, :, :], y0im[:, :, :], st1(ai), ALU.mult))
            pool_link(g, g.tensor_tensor(y1re[:, :, :], y0re[:, :, :], st1(ar), ALU.mult))
            pool_link(g, g.tensor_tensor(y1re[:, :, :], y1re[:, :, :], m1[:, :, :], ALU.add))
            pool_link(g, g.tensor_tensor(m1[:, :, :], y0re[:, :, :], st1(ai), ALU.mult))
            pool_link(g, g.tensor_tensor(y1im[:, :, :], y0im[:, :, :], st1(ar), ALU.mult))
            pool_link(g, g.tensor_tensor(y1im[:, :, :], y1im[:, :, :], m1[:, :, :], ALU.subtract))
            g.wait_ge(sem("s5_coef"), 2)
            cmul(g, bbar_r, bbar_i, b1_re, b1_im, st1(rho), st1(sn), m1)
            cmul(g, br_, bi_, b2_re, b2_im, rows2(rho), rows2(sn), m2)
            cmul(g, abr, abi, br_, bi_, rows2(ar), rows2(ai), m2)
            for j, t in enumerate((abr, abi, br_, bi_)):
                for g2 in range(2):
                    pool_link(g, g.tensor_tensor(
                        bt[:, :, j, S5_STATE * g2:S5_STATE * (g2 + 1)], t[:, :, :],
                        half_mask[:, g2:g2 + 1].unsqueeze(2).to_broadcast([P, DC, S5_STATE]), ALU.mult))
            g.memset(cosT[:, :, 0:1], 1.0)
            g.memset(sinT[:, :, 0:1], 0.0)
            g.tensor_copy(cosT[:, :, 1:2], rot_r.unsqueeze(2))
            g.tensor_copy(sinT[:, :, 1:2], rot_i.unsqueeze(2))
            g.tensor_copy(pw_r, rot_r)
            pool_link(g, g.tensor_copy(pw_i, rot_i))
            m = 2
            while m < NSTEP:
                sq_t = t0[:, 0:PAIRS]
                pool_link(g, g.tensor_tensor(sq_t, pw_i, pw_i, ALU.mult))
                pool_link(g, g.tensor_tensor(pw_i, pw_r, pw_i, ALU.mult))
                pool_link(g, g.tensor_tensor(pw_i, pw_i, pw_i, ALU.add))
                pool_link(g, g.tensor_tensor(pw_r, pw_r, pw_r, ALU.mult))
                pool_link(g, g.tensor_tensor(pw_r, pw_r, sq_t, ALU.subtract))
                tmp = work[:, s5_tmp_at:s5_tmp_at + PAIRS * m].rearrange("p (a m) -> p a m", a=PAIRS)
                cmul(g, cosT[:, :, m:2 * m], sinT[:, :, m:2 * m], cosT[:, :, 0:m], sinT[:, :, 0:m],
                     bc(pw_r, 2, m), bc(pw_i, 2, m), tmp)
                m *= 2

        ft = Carver(work, s5_tmp_at, WORK)
        rotb = [ft(8, PAIRS // DC, NSTEP) for _ in range(2)]
        s5_y = [ft(SEQ) for _ in range(2)]
        glu_s = rotb[0].rearrange("p a b c -> p (a b c)")[:, 0:1024].rearrange("p (h n) -> p h n", h=HALVES)
        glu_t = rotb[1].rearrange("p a b c -> p (a b c)")[:, 0:512]
        PQ = PAIRS // DC

        def s5_in():
            return psum[:, 2:2 + PQ, 0:2 * NSTEP].rearrange("p i (r t) -> p i r t", r=2)

        def s5_tensor(pe):
            for q in range(DC):
                o = bank[6 + q // 4][:, (q % 4) * P:(q % 4 + 1) * P]

                def flat(t):
                    return t[:, PQ * q:PQ * (q + 1), :].rearrange("p a b -> p (a b)")
                mm(o, flat(bbar_r), flat(y0re), True, False)
                ins = mm(o, flat(bbar_i), flat(y0im), False, True)
                if q % 4 == 3:
                    ins.then_inc(sem("k0_ps"), 1)
            for c in range(DC):
                if c % 4 == 0:
                    unit_ready(pe, U_S5IN + c // 4)
                if c >= 2:
                    pe.wait_ge(sem("s5_u_done"), c - 1)
                w = slot(U_S5IN + c // 4).rearrange("p (k n) -> p k n", k=DC)
                for k in range(DC):
                    ins = mm(bank[c % 2][:, 0:SEQ], w[:, k, (c % 4) * P:(c % 4 + 1) * P], xT[:, k, :], k == 0, k == DC - 1)
                ins.then_inc(sem("u_ps"), 1)
            pe.wait_ge(sem("k0_done"), 2)
            for q in range(DC + 2):
                if q < DC:
                    pe.wait_ge(sem("s5_u_done"), q + 1)
                    if q >= 1:
                        pe.wait_ge(sem("s5_pre"), q)
                    for ri in range(2):
                        for s in range(STEP):
                            for i in range(PQ):
                                r = slice(32 * i, 32 * i + 32)
                                ins = mm(s5_in()[:, i, ri, :],
                                         bt[r, q, 2 * s + ri, :], uT[r, q, s::STEP], s == 0, s == STEP - 1)
                    ins.then_inc(sem("s5_in_ps"), 1)
                if q >= 2:
                    z = q - 2
                    if z >= 2:
                        pe.wait_ge(sem("s5_y_done"), z - 1)
                    yb = bank[6 + z % 2][:, 0:SEQ].rearrange("p (n s) -> p n s", s=STEP)
                    hre, him = rotb[z % 2][:, 4, :, :], rotb[z % 2][:, 6, :, :]
                    mm(yb[:, :, 0], k0[:, z, :], uT[:, z, 0::STEP], True, False, skip_group_check=True)
                    pe.wait_ge(sem("s5_h"), 2 * (z + 1))
                    for y0, y1, hh in ((y0re, y1re, hre), (y0im, y1im, him)):
                        for i in range(PQ):
                            mm(yb[32 * i:32 * i + 32, :, 1], y0[:, PQ * z + i, :], hh[:, i, :], False, False, skip_group_check=True)
                        for i in range(PQ):
                            ins = mm(yb[32 * i:32 * i + 32, 1:, 0], y1[:, PQ * z + i, :], hh[:, i, 0:NSTEP - 1], False, True,
                                     skip_group_check=True)
                    ins.then_inc(sem("s5_y_ps"), 1)
            pe.wait_ge(sem("s5_gelu"), DC)
            for j in range(4):
                unit_ready(pe, U_GLU + j)
                w = slot(U_GLU + j).rearrange("p (k n) -> p k n", k=DC)
                for h in range(HALVES):
                    for k in range(DC):
                        ins = mm(bank[2 * j + h][:, :], s5_hid[:, k, h * P:(h + 1) * P], w[:, k, :], k == 0, k == DC - 1)
                    ins.then_inc(sem("glu_ps"), 1)

        def s5_scalar(act):
            load_norm(act, 2)
            for c in range(DC):
                act.wait_ge(sem("u_ps"), c + 1)
                act.activation(uT[:, c, :], bank[c % 2][:, 0:SEQ], ACT.Copy).then_inc(sem("s5_u_done"), 1)
            for q in range(DC):
                act.wait_ge(sem("s5_y_done"), q + 1)
                act.activation(s5_hid[:, q, :], s5_y[q % 2], ACT.Gelu).then_inc(sem("s5_gelu"), 1)
            for j in range(2):
                for h in range(HALVES):
                    act.wait_ge(sem("glu_ps"), 4 * j + 2 + h + 1)
                    if j > 0:
                        act.wait_ge(sem("glu_done"), h + 1)
                    act.activation(glu_s[:, h, :], bank[4 * j + 2 + h][:, :], ACT.Sigmoid).then_inc(sem("glu_sig"), 1)
            norm_scalar(act, 2)
            turn_evacuate(act, 2, None)

        def s5_vector(v):
            for i in range(2):
                v.wait_ge(sem("k0_ps"), i + 1)
                v.tensor_tensor(k0[:, 4 * i:4 * i + 4, :], bank[6 + i][:, :].rearrange("p (q c) -> p q c", q=4),
                                bc(blk32, 1, 4), ALU.mult).then_inc(sem("k0_done"), 1)
            for q in range(DC + 1):
                if q < DC:
                    B = rotb[q % 2]
                    v_re, v_im = s5_in()[:, :, 0, :], s5_in()[:, :, 1, :]
                    cq, sq_ = cosT[:, PQ * q:PQ * (q + 1), :], sinT[:, PQ * q:PQ * (q + 1), :]
                    v.wait_ge(sem("s5_in_ps"), q + 1)
                    if q >= 2:
                        v.wait_ge(sem("s5_post"), q - 1)
                    v.tensor_tensor(B[:, 0], v_re, cq, ALU.mult)
                    v.tensor_tensor(B[:, 1], v_im, sq_, ALU.mult)
                    v.tensor_tensor(B[:, 2], v_im, cq, ALU.mult)
                    v.tensor_tensor(B[:, 3], v_re, sq_, ALU.mult).then_inc(sem("s5_pre"), 1)
                if q >= 1:
                    z = q - 1
                    B = rotb[z % 2]
                    cq, sq_ = cosT[:, PQ * z:PQ * (z + 1), :], sinT[:, PQ * z:PQ * (z + 1), :]
                    v.wait_ge(sem("s5_scan"), z + 1)
                    if z >= 2:
                        v.wait_ge(sem("s5_y_ps"), z - 1)
                    v.tensor_tensor(B[:, 4], B[:, 1], cq, ALU.mult)
                    v.tensor_tensor(B[:, 5], B[:, 3], sq_, ALU.mult)
                    v.tensor_tensor(B[:, 6], B[:, 1], sq_, ALU.mult)
                    v.tensor_tensor(B[:, 7], B[:, 3], cq, ALU.mult).then_inc(sem("s5_post"), 1)
                if q < DC:
                    B = rotb[q % 2]
                    v.wait_ge(sem("s5_turned"), 2 * (q + 1))
                    for i in range(PQ):
                        dec = decay2[:, PQ * q + i:PQ * q + i + 1].to_broadcast([P, NSTEP])
                        v.tensor_tensor_scan(B[:, 1, i, :], dec, B[:, 0, i, :], 0.0, ALU.mult, ALU.add)
                        ins = v.tensor_tensor_scan(B[:, 3, i, :], dec, B[:, 2, i, :], 0.0, ALU.mult, ALU.add)
                    ins.then_inc(sem("s5_scan"), 1)
                if q >= 2:
                    s5_out(v, q - 2)
            s5_out(v, DC - 1)
            for j in range(2):
                for h in range(HALVES):
                    v.wait_ge(sem("glu_sig"), 2 * j + h + 1)
                    v.tensor_tensor(glu_t, glu_s[:, h, :], bank[4 * j + h][:, :], ALU.mult).then_inc(sem("glu_done"), 1)
                    v.wait_ge(sem("glu_done"), 2 * j + h + 1)
                    xs = xres[:, h, 512 * j:512 * j + 512]
                    norm_stats(v, 2, xres, h, j, v.scalar_tensor_tensor(xs, xs, ALPHA, glu_t, ALU.mult, ALU.add))
            norm_vector(v, 2, xres, xres)

        def s5_out(v, z):
            v.wait_ge(sem("s5_y_ps"), z + 1)
            if z >= 2:
                v.wait_ge(sem("s5_gelu"), z - 1)
            v.scalar_tensor_tensor(s5_y[z % 2], uT[:, z, :], s5_d[:, z:z + 1], bank[6 + z % 2][:, 0:SEQ], ALU.mult, ALU.add)\
             .then_inc(sem("s5_y_done"), 1)

        def s5_gpsimd(g):
            for q in range(DC + 1):
                if q < DC:
                    B = rotb[q % 2]
                    g.wait_ge(sem("s5_pre"), q + 1)
                    g.tensor_tensor(B[:, 0], B[:, 0], B[:, 1], ALU.add).then_inc(sem("s5_turned"), 1)
                    g.tensor_tensor(B[:, 2], B[:, 2], B[:, 3], ALU.subtract).then_inc(sem("s5_turned"), 1)
                if q >= 1:
                    B = rotb[(q - 1) % 2]
                    g.wait_ge(sem("s5_post"), q)
                    g.tensor_tensor(B[:, 4], B[:, 4], B[:, 5], ALU.subtract).then_inc(sem("s5_h"), 1)
                    g.tensor_tensor(B[:, 6], B[:, 6], B[:, 7], ALU.add).then_inc(sem("s5_h"), 1)

        ew = Carver(work, 0, WORK)
        xeT = ew(DC, P)
        sel = ew(HALVES, P)
        selg = ew(HALVES, P)
        selT = ew(SEQ)
        e_silu = [ew(512) for _ in range(2)]
        e_hid = ew(512)
        e_hidT = ew(4, P)
        e_out = ew(D)
        yacc = ew(HALVES, D)
        xn = ew(HALVES, D)
        lg = ew(HALVES, 40)
        lgE = ew(HALVES, 8)
        top = ew(HALVES, 8)
        topi = ew(HALVES, 8)
        oh = ew(2, HALVES, 8)
        gw = ew(HALVES, 8)
        ohG = ew(HALVES, 4)
        gexp = ew(HALVES, 4)
        mask1, comb1 = ew(HALVES, EXPERTS), ew(HALVES, EXPERTS)
        rank1 = ew(EXPERTS + 1, HALVES)
        gate1 = ew(EXPERTS + 1, HALVES)
        mask2, comb2 = ew(HALVES, EXPERTS2), ew(HALVES, EXPERTS2)
        rank2 = ew(PACKS + 1, HALVES, PACK)
        gate2 = ew(PACKS + 1, HALVES, PACK)
        cnt = ew(EXPERTS2)

        def rank_tensor(pe, n, mask, ne):
            pe.wait_ge(sem("mask_ready"), n + 1)
            mm(bank[0][:, 0:ne], before, mask[:, 0, :])
            mm(bank[0][:, ne:2 * ne], ones, mask[:, 0, :], True, False)
            mm(bank[0][:, ne:2 * ne], before, mask[:, 1, :], False, True)
            mm(bank[1][:, 0:ne], ones, mask[:, 0, :], True, False)
            mm(bank[1][:, 0:ne], ones, mask[:, 1, :], False, True).then_inc(sem("rank_ps"), 1)

        def top2_vector(v, n, src, k, wmul):
            for h in range(HALVES):
                dve_link(v, v.max(top[:, h, :], src[:, h, :]))
                dve_link(v, v.max_index(idx_u[:, h, :], top[:, h, :], src[:, h, :]))
            dve_link(v, v.tensor_copy(topi[:, :, :], idx_u[:, :, :]))
            v.tensor_tensor(gw[:, :, 0:1], top[:, :, 1:2], top[:, :, 0:1], ALU.subtract).then_inc(sem("top_diff"), 1)
            for i in range(2):
                for h in range(HALVES):
                    ins = v.tensor_scalar(oh[:, i, h, :], iota[:, 0:8], topi[:, h, i:i + 1], None, ALU.is_equal)
            dve_link(v, ins)
            v.wait_ge(sem("top_exp"), n + 1)
            dve_link(v, v.tensor_scalar(gw[:, :, 2:3], gw[:, :, 1:2], 1.0, None, ALU.add))
            dve_link(v, v.reciprocal(gw[:, :, 2:3], gw[:, :, 2:3]))
            if wmul is not None:
                dve_link(v, v.tensor_tensor(gw[:, :, 2:3], gw[:, :, 2:3], wmul, ALU.mult))
            dve_link(v, v.tensor_tensor(gw[:, :, 3:4], gw[:, :, 2:3], gw[:, :, 1:2], ALU.mult))

        def top2_scalar(act, n):
            act.wait_ge(sem("top_diff"), n + 1)
            act.activation(gw[:, :, 1:2], gw[:, :, 0:1], ACT.Exp).then_inc(sem("top_exp"), 1)

        def combine_tensor(pe, step):
            for i in range(4):
                mm(combine_bank(i), selT[:, P * (i // 2):P * (i // 2) + P], e_out[:, 512 * (i % 2):512 * (i % 2) + 512])\
                    .then_inc(step, 1)

        def combine_bank(i):
            return bank[6 + i if i < 2 else 2 + i][:, :]

        def dispatch_tensor(pe, step, x, *banks):
            for i in range(2):
                for c in range(4):
                    for h in range(HALVES):
                        ins = mm(bank[banks[i]][:, c * P:(c + 1) * P],
                                 x[:, h, (4 * i + c) * P:(4 * i + c + 1) * P], sel[:, h, :], h == 0, h == HALVES - 1)
                ins.then_inc(step, 1)

        def seltrans_tensor(pe, step, b):
            for h in range(HALVES):
                ins = pe.transpose(bank[b][:, P * h:P * (h + 1)], selg[:, h, :], ident)
            ins.then_inc(step, 1)

        iota_over = ew(P)
        moe_end = ew.at

        SPLITS = 3
        HALF = UNIT // 2
        assert moe_end <= SPLIT_AT
        sw = Carver(split, 0, SPLIT)
        xeh, xel = sw(DC, P), sw(DC, P)
        hth, htl = sw(2, 4, P), sw(2, 4, P)
        wh = [sw(HALF) for _ in range(SPLITS)]
        wl = [sw(HALF) for _ in range(SPLITS)]

        M1_PE = Order(3, ["g0a", "g0b", "c0", "c1", "c2", "c3", "u0a", "u0b", "g1a", "g1b", "t0", "u1a", "u1b", "d0a", "d0b",
                          "g2a", "g2b", "t1", "u2a", "u2b", "st", "x0", "x1", "t2", "d1a", "d1b", "d2a", "d2b"])
        M1_ACT = Order(2, ["y0", "y1", "s0", "s1", "th0", "s2", "th1", "st", "xh0", "xh1", "th2"])
        M1_DVE = Order(6, ["c0", "c1", "c2", "c3", "h0", "tl0", "sg0", "sg1", "s0", "s1", "h1", "tl1", "h2", "xl0", "xl1", "tl2"])
        M1_STREAM = ["g0", "u0", "g1", "u1", "d0", "g2", "u2", "d1", "d2"]
        M1_HALVES = [s + ab for s in M1_STREAM for ab in "ab"]
        NH = len(M1_HALVES)
        PE1, ACT1, DVE1 = len(M1_PE.names), len(M1_ACT.names), len(M1_DVE.names)

        def at(order, it, name, back=0):
            return it * len(order.names) + (order.first + order.names.index(name) + 1 - back * len(order.names))

        def half_size(i):
            s = M1_STREAM[i // 2]
            b = int(s[1])
            if s[0] != "d":
                return DC // 2 * FF_BLOCKS[b] * P
            return D * min(2, FF_BLOCKS[b] - 2 * (i % 2))

        def half_raw(i):
            s = M1_STREAM[i // 2]
            first = half_size(i - 1) if i % 2 else 0
            return slot(U_MOE1 + i // 2)[:, first:first + half_size(i)]

        def split_high(act, it, i):
            if i % 2 == 0:
                unit_ready_it(act, U_MOE1 + i // 2, it, UNITS_EXPERT)
            act.wait_ge(sem("m1_pe"), at(M1_PE, it, M1_HALVES[i - SPLITS], 1 if i < SPLITS else 0))
            act.activation(wh[i % SPLITS][:, 0:half_size(i)], half_raw(i), ACT.Copy).then_inc(sem("m1_high"), 1)

        def split_low(v, it, i):
            v.wait_ge(sem("m1_high"), it * NH + (i + 1))
            v.tensor_tensor(wl[i % SPLITS][:, 0:half_size(i)], half_raw(i), wh[i % SPLITS][:, 0:half_size(i)].bitcast(F32),
                            ALU.subtract).then_inc(sem("m1_split"), 1)

        def moe1_tensor(pe):
            pe.wait_ge(sem("router_loaded"), 64)
            for h in range(HALVES):
                for k in range(DC):
                    ins = mm(bank[0][:, EXPERTS * h:EXPERTS * (h + 1)], xT[:, k, h * P:(h + 1) * P], w_r1[:, k, :],
                             k == 0, k == DC - 1)
            ins.then_inc(sem("logits_ps"), 1)
            rank_tensor(pe, 0, mask1, EXPERTS)
            step, actd, dved = sem("m1_pe"), sem("m1_act"), sem("m1_dve")
            pe.drain().then_inc(step, 1)
            pe.wait_ge(dved, 4)
            dispatch_tensor(pe, step, xres, 2, 3)
            with pe.Fori(0, EXPERTS) as it:
                def three(o, ah, al, i, cols, first, last):
                    h, l = wh[i % SPLITS][:, cols], wl[i % SPLITS][:, cols]
                    mm(o, ah, h, first, False)
                    mm(o, al, h, False, False)
                    return mm(o, ah, l, False, last)

                def weights(i):
                    pe.wait_ge(sem("m1_split"), it * NH + (i + 1))

                def up(name, o):
                    n = FF_BLOCKS[int(name[1])] * P
                    for ab in range(2):
                        i = 2 * M1_STREAM.index(name) + ab
                        weights(i)
                        for k in range(DC // 2):
                            kk = DC // 2 * ab + k
                            ins = three(o[:, 0:n], xeh[:, kk, :], xel[:, kk, :], i, slice(n * k, n * k + n), kk == 0, kk == DC - 1)
                        ins.then_inc(step, 1)

                def turn(b, o):
                    pe.wait_ge(dved, at(M1_DVE, it, f"h{b}"))
                    for c in range(FF_BLOCKS[b]):
                        ins = pe.transpose(o[:, c * P:(c + 1) * P], e_hid[:, c * P:(c + 1) * P], ident)
                    ins.then_inc(step, 1)

                def down(b):
                    pe.wait_ge(dved, at(M1_DVE, it, f"tl{b}"))
                    for ab in range(2):
                        i = 2 * M1_STREAM.index(f"d{b}") + ab
                        weights(i)
                        for c in range(half_size(i) // D):
                            cc = 2 * ab + c
                            for n in range(2):
                                ins = three(bank[4 + n][:, :], hth[:, b % 2, cc, :], htl[:, b % 2, cc, :], i,
                                            slice(D * c + 512 * n, D * c + 512 * n + 512),
                                            b == 0 and cc == 0, b == 2 and cc == FF_BLOCKS[2] - 1)
                        ins.then_inc(step, 1)

                pe.wait_ge(dved, at(M1_DVE, it, "tl2", 1))
                up("g0", bank[0])
                pe.wait_ge(actd, at(M1_ACT, it, "y1"))
                combine_tensor(pe, step)
                up("u0", bank[1])
                up("g1", bank[2])
                pe.wait_ge(dved, at(M1_DVE, it, "c3"))
                turn(0, bank[6])
                up("u1", bank[3])
                down(0)
                up("g2", bank[0])
                turn(1, bank[7])
                up("u2", bank[1])
                pe.wait_ge(dved, at(M1_DVE, it, "s1"))
                seltrans_tensor(pe, step, 6)
                dispatch_tensor(pe, step, xres, 2, 3)
                pe.wait_ge(dved, at(M1_DVE, it, "tl1"))
                turn(2, bank[7])
                down(1)
                down(2)
            pe.wait_ge(actd, M1_ACT.first + EXPERTS * ACT1 + 2)
            combine_tensor(pe, step)

        def moe1_scalar(act):
            load_norm(act, 3)
            top2_scalar(act, 0)
            step, ped, dved = sem("m1_act"), sem("m1_pe"), sem("m1_dve")

            def gathered(i):
                act.activation(xeh[:, 4 * i:4 * i + 4, :], bank3(2 + i), ACT.Copy).then_inc(step, 1)

            def outputs():
                for i in range(2):
                    act.activation(e_out[:, 512 * i:512 * i + 512], bank[4 + i][:, :], ACT.Copy).then_inc(step, 1)
            for i in range(2):
                act.wait_ge(ped, 1 + i + 1)
                gathered(i)
            with act.Fori(0, EXPERTS) as it:
                def silu(b):
                    n = FF_BLOCKS[b] * P
                    act.wait_ge(ped, at(M1_PE, it, f"g{b}b"))
                    act.wait_ge(dved, at(M1_DVE, it, f"h{(b - 2) % 3}", 1 if b < 2 else 0))
                    act.activation(e_silu[b % 2][:, 0:n], bank[2 * (b % 2)][:, 0:n], ACT.Silu).then_inc(step, 1)

                def turned(b):
                    act.wait_ge(ped, at(M1_PE, it, f"t{b}"))
                    act.activation(hth[:, b % 2, 0:FF_BLOCKS[b], :], bank3(6 if b == 0 else 7)[:, 0:FF_BLOCKS[b], :], ACT.Copy)\
                       .then_inc(step, 1)

                def high(*halves):
                    for i in halves:
                        split_high(act, it, i)
                high(0, 1, 2)
                act.wait_ge(ped, at(M1_PE, it, "d2b", 1))
                outputs()
                high(3, 4)
                silu(0)
                high(5, 6, 7, 8)
                silu(1)
                turned(0)
                high(9, 10, 11, 12, 13, 14)
                silu(2)
                turned(1)
                high(15, 16)
                act.wait_ge(ped, at(M1_PE, it, "st"))
                act.activation(selT, bank[6][:, 0:SEQ], ACT.Copy).then_inc(step, 1)
                for i in range(2):
                    act.wait_ge(ped, at(M1_PE, it, f"x{i}"))
                    gathered(i)
                turned(2)
                high(17)
            act.wait_ge(ped, M1_PE.first + EXPERTS * PE1)
            outputs()

        def zero_vector(v, step):
            v.memset(selT, 0.0).then_inc(step, 1)
            v.memset(yacc[:, :, :], 0.0).then_inc(step, 1)

        def zero_scalar(act, step):
            for i in range(2):
                act.activation(e_out[:, 512 * i:512 * i + 512], xeT[:, 4 * i:4 * i + 4, :].rearrange("p c s -> p (c s)"),
                               ACT.Copy, scale=0.0).then_inc(step, 1)

        def rank_vector(v, n, ne, mask, flags):
            v.wait_ge(sem("rank_ps"), n + 1)
            r = bank[0][:, 0:2 * ne].rearrange("p (h e) -> p h e", h=HALVES)
            dve_link(v, v.tensor_copy(cnt[:, 0:ne], bank[1][:, 0:ne]))
            dve_link(v, v.tensor_reduce(cnt[:, 0:1], cnt[:, 0:ne], AX.X, ALU.max))
            for i, slots in flags:
                v.tensor_scalar(smalli[:, i:i + 1], cnt[:, 0:1], float(slots), None, ALU.is_gt).then_inc(sem("flag_ready"), 1)
            dve_link(v, v.scalar_tensor_tensor(mask[:, :, :], r, 1.0, mask[:, :, :], ALU.add, ALU.mult))

        def moe1_vector(v):
            v.memset(psum[:, 4:6, :], 0.0)
            zero_vector(v, sem("m1_dve"))
            v.wait_ge(sem("logits_ps"), 1)
            v.wait_ge(sem("router_loaded"), 64)
            for h in range(HALVES):
                ins = v.tensor_tensor(lgE[:, h, :], bank[0][:, EXPERTS * h:EXPERTS * (h + 1)], b_r1, ALU.add)
            dve_link(v, ins)
            top2_vector(v, 0, lgE, 0, None)
            for h in range(HALVES):
                dve_link(v, v.tensor_scalar(comb1[:, h, :], oh[:, 0, h, :], gw[:, h, 2:3], None, ALU.mult))
                dve_link(v, v.scalar_tensor_tensor(comb1[:, h, :], oh[:, 1, h, :], gw[:, h, 3:4], comb1[:, h, :], ALU.mult, ALU.add))
            v.tensor_tensor(mask1[:, :, :], oh[:, 0], oh[:, 1], ALU.add).then_inc(sem("mask_ready"), 1)
            v.wait_ge(sem("mask_ready"), 1)
            rank_vector(v, 0, EXPERTS, mask1, ((0, SLOTS1),))
            v.memset(rank1[:, EXPERTS, :], -1.0)
            v.memset(gate1[:, :, :], 0.0)
            dve_link(v, v.tensor_scalar(rank1[:, 0:EXPERTS, :].rearrange("p e h -> p h e"), mask1[:, :, :], 1.0, None, ALU.subtract))
            dve_link(v, v.tensor_copy(gate1[:, 0:EXPERTS, :].rearrange("p e h -> p h e"), comb1[:, :, :]))
            step, ped, actd = sem("m1_dve"), sem("m1_pe"), sem("m1_act")

            def gathered(i):
                v.tensor_tensor(xel[:, 4 * i:4 * i + 4, :], bank3(2 + i), xeh[:, 4 * i:4 * i + 4, :].bitcast(F32), ALU.subtract)\
                 .then_inc(step, 1)
            for h in range(HALVES):
                v.tensor_scalar(sel[:, h, :], iota, rank1[:, 0, h:h + 1], None, ALU.is_equal).then_inc(step, 1)
            for i in range(2):
                v.wait_ge(actd, i + 1)
                gathered(i)
            with v.Fori(0, EXPERTS) as it:
                def low(*halves):
                    for i in halves:
                        split_low(v, it, i)

                def combined(*parts):
                    for i in parts:
                        v.wait_ge(ped, at(M1_PE, it, f"c{i}"))
                        combine_add(v, i).then_inc(step, 1)

                def hidden(b):
                    n = FF_BLOCKS[b] * P
                    v.wait_ge(actd, at(M1_ACT, it, f"s{b}"))
                    v.wait_ge(ped, at(M1_PE, it, f"u{b}b"))
                    if b > 0:
                        v.wait_ge(ped, at(M1_PE, it, f"t{b - 1}"))
                    v.tensor_tensor(e_hid[:, 0:n], e_silu[b % 2][:, 0:n], bank[2 * (b % 2) + 1][:, 0:n], ALU.mult).then_inc(step, 1)

                def turned(b):
                    n = FF_BLOCKS[b]
                    v.wait_ge(actd, at(M1_ACT, it, f"th{b}"))
                    v.tensor_tensor(htl[:, b % 2, 0:n, :], bank3(6 if b == 0 else 7)[:, 0:n, :],
                                    hth[:, b % 2, 0:n, :].bitcast(F32), ALU.subtract).then_inc(step, 1)
                low(0, 1, 2, 3)
                combined(0, 1)
                low(4)
                combined(2, 3)
                low(5, 6)
                hidden(0)
                low(7, 8)
                turned(0)
                for h in range(HALVES):
                    v.tensor_scalar(selg[:, h, :], iota, rank1[:, it, h:h + 1], gate1[:, it, h:h + 1], ALU.is_equal, ALU.mult)\
                     .then_inc(step, 1)
                for h in range(HALVES):
                    v.tensor_scalar(sel[:, h, :], iota, rank1[:, it + 1, h:h + 1], None, ALU.is_equal).then_inc(step, 1)
                low(9, 10)
                hidden(1)
                low(11, 12, 13, 14)
                turned(1)
                low(15)
                hidden(2)
                low(16)
                for i in range(2):
                    v.wait_ge(actd, at(M1_ACT, it, f"xh{i}"))
                    gathered(i)
                turned(2)
                low(17)
            for i in range(4):
                v.wait_ge(ped, M1_PE.first + EXPERTS * PE1 + i + 1)
                combine_add(v, i).then_inc(step, 1)
            v.wait_ge(step, M1_DVE.first + EXPERTS * DVE1 + 4)

        def combine_add(v, i):
            y = yacc[:, i // 2, 512 * (i % 2):512 * (i % 2) + 512]
            return v.tensor_tensor(y, y, combine_bank(i), ALU.add)

        def residual_vector(v, n, alpha):
            for h in range(HALVES):
                for j in range(2):
                    f = slice(512 * j, 512 * j + 512)
                    ins = v.scalar_tensor_tensor(xres[:, h, f], xres[:, h, f], alpha, yacc[:, h, f], ALU.mult, ALU.add)
                    norm_stats(v, n, xres, h, j, ins)

        M2_PE = Order(2, ["k0", "k1", "c0", "c1", "c2", "c3"] + [f"k{i}" for i in range(2, DC)] + ["st", "x0", "x1", "t", "d0", "d1", "d2", "d3"])
        M2_ACT = Order(4, ["s", "st", "x0", "x1", "y0", "y1"])
        M2_DVE = Order(4, ["e0", "e1", "sg0", "sg1", "s0", "s1", "c0", "c1", "c2", "c3", "h", "t"])
        M2_UNIT_STEP = [f"k{UP_K * i + UP_K - 1}" for i in range(UP_UNITS)] + [f"d{DOWN_C * i + DOWN_C - 1}" for i in range(DOWN_UNITS)]
        PE2, ACT2, DVE2 = len(M2_PE.names), len(M2_ACT.names), len(M2_DVE.names)

        def moe2_tensor(pe):
            for h in range(HALVES):
                for k in range(DC):
                    ins = mm(bank[0][:, 36 * h:36 * (h + 1)], xT[:, k, h * P:(h + 1) * P], w_r2[:, k, :], k == 0, k == DC - 1)
            ins.then_inc(sem("logits_ps"), 1)
            rank_tensor(pe, 1, mask2, EXPERTS2)
            step, actd, dved = sem("m2_pe"), sem("m2_act"), sem("m2_dve")
            pe.wait_ge(dved, M2_DVE.first)
            dispatch_tensor(pe, step, xn, 6, 7)
            with pe.Fori(0, PACKS) as it:
                def unit(j):
                    if j < RING:
                        unit_ready_it(pe, U_MOE2 + j, it, RING)
                        return slot(U_MOE2 + j)
                    pe.wait_ge(sem(f"extra_loaded{j - RING}"), it * 16 + 16)
                    return extra[:, j - RING, :]

                def up(k):
                    w = unit(k // UP_K).rearrange("p (e w k n) -> p e w k n", e=PACK, w=2, k=UP_K)
                    for i in range(2):
                        for e in range(PACK):
                            r = slice(SLOTS2 * e, SLOTS2 * (e + 1))
                            ins = mm(bank[i][r, :], xeT[:, k, r], w[:, e, i, k % UP_K, :], k == 0, k == DC - 1)
                    ins.then_inc(step, 1)

                pe.wait_ge(actd, at(M2_ACT, it, "x1", 1))
                up(0)
                up(1)

                pe.wait_ge(actd, at(M2_ACT, it, "y1", 1))
                combine_tensor(pe, step)
                for k in range(2, DC):
                    up(k)
                pe.wait_ge(dved, at(M2_DVE, it, "sg1"))
                seltrans_tensor(pe, step, 3)
                pe.wait_ge(dved, at(M2_DVE, it, "s1"))
                pe.wait_ge(dved, at(M2_DVE, it, "c3"))
                dispatch_tensor(pe, step, xn, 6, 7)
                pe.wait_ge(dved, at(M2_DVE, it, "h"))
                for c in range(4):
                    ins = pe.transpose(bank[2][:, c * P:(c + 1) * P], e_hid[:, c * P:(c + 1) * P], ident)
                ins.then_inc(step, 1)
                pe.wait_ge(dved, at(M2_DVE, it, "t"))
                for c in range(4):
                    w = unit(UP_UNITS + c // DOWN_C).rearrange("p (e c n) -> p e c n", e=PACK, c=DOWN_C)
                    for n in range(2):
                        for e in range(PACK):
                            r = slice(SLOTS2 * e, SLOTS2 * (e + 1))
                            ins = mm(bank[4 + n][r, :], e_hidT[:, c, r], w[:, e, c % DOWN_C, 512 * n:512 * n + 512], c == 0, c == 3)
                    ins.then_inc(step, 1)
            pe.wait_ge(actd, at(M2_ACT, PACKS, "y1", 1))
            combine_tensor(pe, step)

        def moe2_scalar(act):
            for h in range(HALVES):
                act.wait_ge(sem("group_max"), h + 1)
                act.activation(gexp[:, h, :], lg[:, h, 0:GROUPS2], ACT.Exp, bias=gw[:, h, 4:5]).then_inc(sem("group_exp"), 1)
            top2_scalar(act, 1)
            step, ped, dved = sem("m2_act"), sem("m2_pe"), sem("m2_dve")

            def gathered(i):
                for c in range(4):
                    q = 4 * i + c
                    ins = act.activation(xeT[:, q, :], bank[6 + i][:, c * P:(c + 1) * P], ACT.Copy, scale=g_cols[:, 1, q:q + 1])
                ins.then_inc(step, 1)
            for i in range(2):
                act.wait_ge(ped, i + 1)
                gathered(i)
            act.wait_ge(step, 2)
            zero_scalar(act, step)
            with act.Fori(0, PACKS) as it:
                act.wait_ge(ped, at(M2_PE, it, f"k{DC - 1}"))
                act.wait_ge(dved, at(M2_DVE, it, "h", 1))
                act.activation(e_silu[0], bank[0][:, :], ACT.Silu).then_inc(step, 1)
                act.wait_ge(ped, at(M2_PE, it, "st"))
                act.activation(selT, bank[3][:, 0:SEQ], ACT.Copy).then_inc(step, 1)
                for i in range(2):
                    act.wait_ge(ped, at(M2_PE, it, f"x{i}"))
                    gathered(i)
                act.wait_ge(ped, at(M2_PE, it, "d3"))
                for i in range(2):
                    act.activation(e_out[:, 512 * i:512 * i + 512], bank[4 + i][:, :], ACT.Copy).then_inc(step, 1)

        def moe2_vector(v):
            zero_vector(v, sem("m2_dve"))
            v.wait_ge(sem("logits_ps"), 2)
            for h in range(HALVES):
                ins = v.tensor_tensor(lg[:, h, 0:36], bank[0][:, 36 * h:36 * (h + 1)], b_r2, ALU.add)
            dve_link(v, ins)
            v.memset(lgE[:, :, 4:8], -3.0e38)
            dve_link(v, v.tensor_copy(lgE[:, :, 0:4], lg[:, :, 0:GROUPS2]))
            for h in range(HALVES):
                dve_link(v, v.max(top[:, h, :], lgE[:, h, :]))
                dve_link(v, v.max_index(idx_u[:, h, :], top[:, h, :], lgE[:, h, :]))
                v.tensor_scalar(gw[:, h, 4:5], top[:, h, 0:1], -1.0, None, ALU.mult).then_inc(sem("group_max"), 1)
            dve_link(v, v.tensor_copy(topi[:, :, :], idx_u[:, :, :]))
            for h in range(HALVES):
                ins = v.tensor_scalar(ohG[:, h, :], iota[:, 0:GROUPS2], topi[:, h, 0:1], None, ALU.is_equal)
            dve_link(v, ins)
            for h in range(HALVES):
                for g in range(GROUPS2):
                    le = lg[:, h, GROUPS2 + PER_GROUP * g:GROUPS2 + PER_GROUP * (g + 1)]
                    if g == 0:
                        dve_link(v, v.tensor_scalar(lgE[:, h, :], le, ohG[:, h, g:g + 1], None, ALU.mult))
                    else:
                        dve_link(v, v.scalar_tensor_tensor(lgE[:, h, :], le, ohG[:, h, g:g + 1], lgE[:, h, :], ALU.mult, ALU.add))
            v.wait_ge(sem("group_exp"), 2)
            dve_link(v, v.tensor_reduce(gw[:, :, 5], gexp[:, :, :], AX.X, ALU.add))
            dve_link(v, v.reciprocal(gw[:, :, 5:6], gw[:, :, 5:6]))
            top2_vector(v, 1, lgE, 1, gw[:, :, 5:6])
            for h in range(HALVES):
                dve_link(v, v.tensor_scalar(top[:, h, :], oh[:, 0, h, :], gw[:, h, 2:3], None, ALU.mult))
                dve_link(v, v.scalar_tensor_tensor(top[:, h, :], oh[:, 1, h, :], gw[:, h, 3:4], top[:, h, :], ALU.mult, ALU.add))
            dve_link(v, v.tensor_tensor(topi[:, :, :], oh[:, 0], oh[:, 1], ALU.add))
            for h in range(HALVES):
                for g in range(GROUPS2):
                    e = slice(PER_GROUP * g, PER_GROUP * (g + 1))
                    v.tensor_scalar(comb2[:, h, e], top[:, h, :], ohG[:, h, g:g + 1], None, ALU.mult)
                    ins = v.tensor_scalar(mask2[:, h, e], topi[:, h, :], ohG[:, h, g:g + 1], None, ALU.mult)
            ins.then_inc(sem("mask_ready"), 1)
            v.wait_ge(sem("mask_ready"), 2)
            rank_vector(v, 1, EXPERTS2, mask2, ((1, SLOTS2), (2, SLOTS2 + P)))
            v.memset(rank2[:, PACKS], -1.0)
            v.memset(gate2[:, PACKS], 0.0)
            for h in range(HALVES):
                v.tensor_copy(gate2[:, 0:PACKS, h, :], comb2[:, h, :].rearrange("p (g e) -> p g e", e=PACK))
                ins = v.tensor_scalar(rank2[:, 0:PACKS, h, :], mask2[:, h, :].rearrange("p (g e) -> p g e", e=PACK), 1.0, None, ALU.subtract)
            dve_link(v, ins)
            step, ped, actd = sem("m2_dve"), sem("m2_pe"), sem("m2_act")

            def onehot(dst, h, g):
                return v.tensor_tensor(dst[:, h, :].rearrange("p (e s) -> p e s", e=PACK), bc(iota[:, 0:SLOTS2], 1, PACK),
                                       bc(rank2[:, g, h, :], 2, SLOTS2), ALU.is_equal)
            for h in range(HALVES):
                onehot(sel, h, 0).then_inc(step, 1)
            with v.Fori(0, PACKS) as it:
                v.wait_ge(ped, it * PE2 + M2_PE.first)
                for h in range(HALVES):
                    onehot(selg, h, it).then_inc(step, 1)
                v.wait_ge(step, at(M2_DVE, it, "e1"))
                for h in range(HALVES):
                    sg = selg[:, h, :].rearrange("p (e s) -> p e s", e=PACK)
                    v.tensor_tensor(sg, sg, bc(gate2[:, it, h, :], 2, SLOTS2), ALU.mult).then_inc(step, 1)
                for h in range(HALVES):
                    onehot(sel, h, it + 1).then_inc(step, 1)
                for i in range(4):
                    v.wait_ge(ped, at(M2_PE, it, f"c{i}"))
                    combine_add(v, i).then_inc(step, 1)
                v.wait_ge(actd, at(M2_ACT, it, "s"))
                v.tensor_tensor(e_hid, e_silu[0], bank[1][:, :], ALU.mult).then_inc(step, 1)
                v.wait_ge(ped, at(M2_PE, it, "t"))
                v.tensor_copy(e_hidT[:, :, :], bank3(2)).then_inc(step, 1)
            for i in range(4):
                v.wait_ge(ped, M2_PE.first + PACKS * PE2 + i + 1)
                combine_add(v, i).then_inc(step, 1)
            v.wait_ge(step, M2_DVE.first + PACKS * DVE2 + 4)

        OVER_EXPERTS = (EXPERTS, EXPERTS2, EXPERTS2)
        OVER_BLOCKS = (FF_BLOCKS, (FF2 // P,), (FF2 // P,))
        OVER_FIRST = (SLOTS1, SLOTS2, SLOTS2 + P)
        OVER_X = (xres, xn, xn)

        def over_steps(n):
            return 6 * len(OVER_BLOCKS[n]) + 6

        def over_flag(eng, n):
            eng.wait_ge(sem("flag_ready"), n + 1)
            return eng.value_load(smalli[0:1, n:n + 1], min_val=0, max_val=1)

        def over_wait(eng, n, it, s):
            eng.wait_ge(sem(f"over_step{n}"), it * over_steps(n) + (1 + s))

        def overflow_sync(sp, n):
            with sp.If(over_flag(sp, n) == 1):
                loaded = sem(f"over_loaded{n}")
                if n == 0:
                    with sp.Fori(0, EXPERTS) as it:
                        for b in range(len(FF_BLOCKS)):
                            over_wait(sp, n, it, 3 + 6 * b if b > 0 else 1)
                            for i in range(3):
                                if b < 2:
                                    sp.dma_start(ring[:, i, :], I["moe1_wide"][it, ((0, 1, 4), (2, 3, 5))[b][i]]).then_inc(loaded, 16)
                                else:
                                    sp.dma_start(ring[:, i, 0:3 * D], I["moe1_last"][it, i]).then_inc(loaded, 16)
                else:
                    with sp.Fori(0, PACKS) as g:
                        for e in range(PACK):
                            over_wait(sp, n, g * PACK + e, 1)
                            for i in range(2):
                                sp.dma_start(ring[:, i, :].rearrange("p (u r) -> p u r", u=UP_UNITS),
                                             I["moe2_up"][g].rearrange("u d (e w r) -> d e w u r", e=PACK, w=2)[:, e, i])\
                                    .then_inc(loaded, 16)
                            sp.dma_start(ring[:, 2, :].rearrange("p (u r) -> p u r", u=DOWN_UNITS),
                                         I["moe2_down"][g].rearrange("u f (e r) -> f e u r", e=PACK)[:, e])\
                                .then_inc(loaded, 16)
                over_wait(sp, n, OVER_EXPERTS[n], 0)

        def overflow_tensor(pe, n):
            nb, x = len(OVER_BLOCKS[n]), OVER_X[n]
            step = sem(f"over_step{n}")
            with pe.If(over_flag(pe, n) == 1):
                with pe.Fori(0, OVER_EXPERTS[n]) as it:
                    over_wait(pe, n, it, 1)
                    for c in range(DC):
                        for h in range(HALVES):
                            mm(bank[7 - c // 4][:, (c % 4) * P:(c % 4 + 1) * P], x[:, h, c * P:(c + 1) * P], sel[:, h, :],
                               h == 0, h == HALVES - 1)
                    for h in range(HALVES):
                        ins = pe.transpose(bank[3][:, P * h:P * (h + 1)], selg[:, h, :], ident)
                    ins.then_inc(step, 1)
                    for b, nch in enumerate(OVER_BLOCKS[n]):
                        over_wait(pe, n, it, 3 + 6 * b)
                        pe.wait_ge(sem(f"over_loaded{n}"), it * (48 * nb) + 48 * (b + 1))
                        w1, w3 = (ring[:, i, 0:DC * nch * P].rearrange("p (k n) -> p k n", k=DC) for i in range(2))
                        for k in range(DC):
                            mm(bank[0][:, 0:nch * P], xeT[:, k, :], w1[:, k, :], k == 0, k == DC - 1)
                        for k in range(DC):
                            ins = mm(bank[1][:, 0:nch * P], xeT[:, k, :], w3[:, k, :], k == 0, k == DC - 1)
                        ins.then_inc(step, 1)
                        over_wait(pe, n, it, 6 + 6 * b)
                        for c in range(nch):
                            ins = pe.transpose(bank[2][:, c * P:(c + 1) * P], e_hid[:, c * P:(c + 1) * P], ident)
                        ins.then_inc(step, 1)
                        over_wait(pe, n, it, 8 + 6 * b)
                        w2 = ring[:, 2, 0:nch * D].rearrange("p (c n) -> p c n", n=D)
                        for c in range(nch):
                            for j in range(2):
                                ins = mm(bank[4 + j][:, :], e_hidT[:, c, :], w2[:, c, 512 * j:512 * j + 512],
                                         b == 0 and c == 0, b == nb - 1 and c == nch - 1)
                        ins.then_inc(step, 1)
                    over_wait(pe, n, it, 4 + 6 * nb)
                    for i in range(4):
                        ins = mm(bank[i][:, :], selT[:, P * (i // 2):P * (i // 2) + P], e_out[:, 512 * (i % 2):512 * (i % 2) + 512])
                    ins.then_inc(step, 1)

        def overflow_scalar(act, n):
            nb = len(OVER_BLOCKS[n])
            step = sem(f"over_step{n}")
            with act.If(over_flag(act, n) == 1):
                with act.Fori(0, OVER_EXPERTS[n]) as it:
                    over_wait(act, n, it, 2)
                    for c in range(DC):
                        src = bank[7 - c // 4][:, (c % 4) * P:(c % 4 + 1) * P]
                        if n == 0:
                            act.activation(xeT[:, c, :], src, ACT.Copy)
                        else:
                            act.activation(xeT[:, c, :], src, ACT.Copy, scale=g_cols[:, 1, c:c + 1])
                    act.activation(selT, bank[3][:, 0:SEQ], ACT.Copy).then_inc(step, 1)
                    for b, nch in enumerate(OVER_BLOCKS[n]):
                        over_wait(act, n, it, 4 + 6 * b)
                        act.activation(e_silu[0][:, 0:nch * P], bank[0][:, 0:nch * P], ACT.Silu).then_inc(step, 1)
                    over_wait(act, n, it, 3 + 6 * nb)
                    for i in range(2):
                        ins = act.activation(e_out[:, 512 * i:512 * i + 512], bank[4 + i][:, :], ACT.Copy)
                    ins.then_inc(step, 1)

        def overflow_vector(v, n):
            nb = len(OVER_BLOCKS[n])
            step = sem(f"over_step{n}")
            rank, gate = ((mask1, comb1), (mask2, comb2), (mask2, comb2))[n]
            with v.If(over_flag(v, n) == 1):
                v.tensor_scalar(iota_over, iota, float(OVER_FIRST[n] + 1), None, ALU.add).then_inc(step, 1)
                with v.Fori(0, OVER_EXPERTS[n]) as it:
                    over_wait(v, n, it, 0)
                    for h in range(HALVES):
                        v.tensor_scalar(sel[:, h, :], iota_over, rank[:, h, it].unsqueeze(1), None, ALU.is_equal)
                    for h in range(HALVES):
                        ins = v.tensor_scalar(selg[:, h, :], iota_over, rank[:, h, it].unsqueeze(1), gate[:, h, it].unsqueeze(1),
                                              ALU.is_equal, ALU.mult)
                    ins.then_inc(step, 1)
                    for b, nch in enumerate(OVER_BLOCKS[n]):
                        over_wait(v, n, it, 5 + 6 * b)
                        v.tensor_tensor(e_hid[:, 0:nch * P], e_silu[0][:, 0:nch * P], bank[1][:, 0:nch * P], ALU.mult)\
                         .then_inc(step, 1)
                        over_wait(v, n, it, 7 + 6 * b)
                        v.tensor_copy(e_hidT[:, 0:nch, :], bank3(2)[:, 0:nch, :]).then_inc(step, 1)
                    over_wait(v, n, it, 5 + 6 * nb)
                    for i in range(4):
                        y = yacc[:, i // 2, 512 * (i % 2):512 * (i % 2) + 512]
                        ins = v.tensor_tensor(y, y, bank[i][:, :], ALU.add)
                    ins.then_inc(step, 1)
                over_wait(v, n, OVER_EXPERTS[n], 0)

        mw = Carver(work, moe_end, WORK)
        NC2 = CW // P
        zT = mw(NC2, SEQ + CONV2_TAPS - 1)
        cT = mw(NC2, SEQ)
        ycT = mw(NC2, SEQ)
        ug = mw(HALVES, CW)
        vg = mw(HALVES, CW)
        ysT = mw(NC2, SEQ)
        wsT = mw(SGU_HEADS, P)
        g_sgu = mw(CW)
        vst = mw(HALVES, 6)
        vmv = mw(HALVES, 2)
        vrs = mw(HALVES, 1)
        SD = CW // SGU_HEADS
        pT = mw(2, SEQ)
        extra = mw(UNITS_PACK - RING, UNIT)
        ple_g = ug.rearrange("p a b -> p (a b)")[:, 0:512]
        ple_t = vg.rearrange("p a b -> p (a b)")[:, 0:512]

        def mix2_tensor(pe):
            for j in range(3):
                unit_ready(pe, U_WIN2 + j)
                w = slot(U_WIN2 + j).rearrange("p (k n) -> p k n", k=DC)
                for c in range(NC2):
                    for k in range(DC):
                        ins = mm(bank[2 * j + c // 2][:, SEQ * (c % 2):SEQ * (c % 2) + SEQ], w[:, k, c * P:(c + 1) * P],
                                 xT[:, k, :], k == 0, k == DC - 1)
                    ins.then_inc(sem("cxb_ps"), 1)
            for j in range(2):
                unit_ready(pe, U_WIN2 + 3 + j)
                w = slot(U_WIN2 + 3 + j).rearrange("p (k n) -> p k n", k=DC)
                if j == 1:
                    pe.wait_ge(sem("c_done"), NC2)
                for h in range(HALVES):
                    for k in range(DC):
                        ins = mm(bank[6 + h if j == 0 else h][:, :], xT[:, k, h * P:(h + 1) * P], w[:, k, :], k == 0, k == DC - 1)
                    ins.then_inc(sem("uv_ps"), 1)
            pe.wait_ge(sem("z2_done"), NC2)
            pe.wait_ge(sem("ws_masked"), 1)
            for h in range(HALVES):
                pe.wait_ge(sem("v_normed"), h + 1)
                for e in range(SGU_HEADS):
                    ins = mm(bank[2 + h][:, SD * e:SD * (e + 1)], wsT[:, e, :], vg[:, h, SD * e:SD * (e + 1)])
                ins.then_inc(sem("mixed_ps"), 1)
            for h in range(HALVES):
                pe.wait_ge(sem("ysgu_done"), h + 1)
                for c in range(NC2):
                    ins = pe.transpose(bank[h][:, c * P:(c + 1) * P], vg[:, h, c * P:(c + 1) * P], ident)
                ins.then_inc(sem("ys_ps"), 1)
            pe.wait_ge(sem("conv2_done"), NC2)
            pe.wait_ge(sem("ys_done"), HALVES)
            pe.wait_ge(sem("gelu2_done"), 2 * HALVES)
            for j in range(2):
                unit_ready(pe, U_WOUT2 + j)
                w = slot(U_WOUT2 + j).rearrange("p (k n) -> p k n", k=DC)
                for h in range(HALVES):
                    for k in range(DC):
                        src = ycT if k < NC2 else ysT
                        ins = mm(bank[4 + 2 * j + h][:, :], src[:, k % NC2, h * P:(h + 1) * P], w[:, k, :], k == 0, k == DC - 1)
                    ins.then_inc(sem("wout2_ps"), 1)
            turn_tensor(pe, 5, xn)

        def mix2_loads(act):
            for name, dst in (("wsT", wsT), ("g_sgu", g_sgu), ("pT", pT)):
                act.dma_start(dst, I[name]).then_inc(sem("mix2_loaded"), 16)

        def mix2_scalar(act):
            mix2_loads(act)
            act.wait_ge(sem("lnp_used"), 1)
            act.dma_start(lnp[:, 0, :], I["g_final"]).then_inc(sem("lnp_loaded"), 16)
            for c in range(NC2):
                act.wait_ge(sem("cxb_ps"), 2 * (c // 2) + 2)
                act.activation(cT[:, c, :], bank[c // 2][:, SEQ * (c % 2):SEQ * (c % 2) + SEQ], ACT.Copy).then_inc(sem("c_done"), 1)
            for j in range(2):
                for h in range(HALVES):
                    act.wait_ge(sem("uv_ps"), 2 * j + h + 1)
                    act.activation((ug, vg)[j][:, h, :], bank[6 + h if j == 0 else h][:, :], ACT.Gelu_apprx_tanh)\
                       .then_inc(sem("gelu2_done"), 1)
            for h in range(HALVES):
                act.wait_ge(sem("v_var"), h + 1)
                act.activation(vrs[:, h, :], vrs[:, h, :], ACT.Sqrt).then_inc(sem("v_rstd"), 1)
            for h in range(HALVES):
                act.wait_ge(sem("ys_ps"), h + 1)
                act.activation(ysT[:, :, h * P:(h + 1) * P], bank3(h), ACT.Copy).then_inc(sem("ys_done"), 1)
            norm_scalar(act, 5)

        def mix2_vector(v):
            v.wait_ge(sem("mix2_loaded"), 48)
            v.memset(zT[:, :, 0:CONV2_TAPS - 1], 0.0)
            v.tensor_tensor(wsT[:, :, :], wsT[:, :, :], bc(upto_t, 1, SGU_HEADS), ALU.mult).then_inc(sem("ws_masked"), 1)
            for c in range(NC2):
                v.wait_ge(sem("cxb_ps"), NC2 + 2 * (c // 2) + 2)
                v.wait_ge(sem("c_done"), c + 1)
                v.tensor_tensor(zT[:, c, CONV2_TAPS - 1:], cT[:, c, :], bank[2 + c // 2][:, SEQ * (c % 2):SEQ * (c % 2) + SEQ],
                                ALU.mult).then_inc(sem("z2_done"), 1)
            v.wait_ge(sem("z2_done"), NC2)
            for c in range(NC2):
                dve_link(v, v.tensor_scalar(ycT[:, c, :], zT[:, c, 0:SEQ], conv2_w[:, c, 0:1], None, ALU.mult))
                for k in range(1, CONV2_TAPS):
                    dve_link(v, v.scalar_tensor_tensor(ycT[:, c, :], zT[:, c, k:k + SEQ], conv2_w[:, c, k:k + 1], ycT[:, c, :],
                                                       ALU.mult, ALU.add))
                v.wait_ge(sem("cxb_ps"), 2 * NC2 + 2 * (c // 2) + 2)
                v.tensor_tensor(ycT[:, c, :], ycT[:, c, :], bank[4 + c // 2][:, SEQ * (c % 2):SEQ * (c % 2) + SEQ], ALU.mult)\
                 .then_inc(sem("conv2_done"), 1)
            for h in range(HALVES):
                v.wait_ge(sem("gelu2_done"), HALVES + h + 1)
                dve_link(v, v.bn_stats(vst[:, h, :], vg[:, h, :]))
                dve_link(v, v.bn_aggr(vmv[:, h, :], vst[:, h, :]))
                dve_link(v, v.tensor_scalar(vrs[:, h, :], vmv[:, h, 1:2], NORM_EPS, None, ALU.add))
                v.reciprocal(vrs[:, h, :], vrs[:, h, :]).then_inc(sem("v_var"), 1)
            for h in range(HALVES):
                v.wait_ge(sem("v_rstd"), h + 1)
                dve_link(v, v.tensor_scalar(vg[:, h, :], vg[:, h, :], vmv[:, h, 0:1], vrs[:, h, :], ALU.subtract, ALU.mult))
                v.tensor_tensor(vg[:, h, :], vg[:, h, :], g_sgu, ALU.mult).then_inc(sem("v_normed"), 1)
            for h in range(HALVES):
                v.wait_ge(sem("mixed_ps"), h + 1)
                o = vg[:, h, :].rearrange("p (e d) -> p e d", e=SGU_HEADS)
                dve_link(v, v.tensor_tensor(o, bank[2 + h][:, :].rearrange("p (e d) -> p e d", e=SGU_HEADS), bc(b_sp, 2, SD), ALU.add))
                v.tensor_tensor(vg[:, h, :], vg[:, h, :], ug[:, h, :], ALU.mult).then_inc(sem("ysgu_done"), 1)
            for j in range(2):
                for h in range(HALVES):
                    v.wait_ge(sem("wout2_ps"), 2 * j + h + 1)
                    xs = xres[:, h, 512 * j:512 * j + 512]
                    ins = v.tensor_tensor(xs, xs, bank[4 + 2 * j + h][:, :], ALU.add)
                    norm_stats(v, 5, xres, h, j, ins)
            norm_vector(v, 5, xres, xn)
            turn_evacuate(v, 5, g_cols[:, 1, :])

        def emb_tensor(pe):
            unit_ready(pe, U_PLE)
            w = slot(U_PLE)[:, 0:2 * D].rearrange("p (k n) -> p k n", k=2)
            for j in range(2):
                for h in range(HALVES):
                    for k in range(2):
                        ins = mm(bank[2 * j + h][:, :], pT[:, k, h * P:(h + 1) * P], w[:, k, 512 * j:512 * j + 512], k == 0, k == 1)
                    ins.then_inc(sem("ple_ps"), 1)

        def ple_tensor(pe):
            for j in range(2):
                unit_ready(pe, U_PLE + 1 + j)
                w = slot(U_PLE + 1 + j).rearrange("p (k n) -> p k n", k=DC)
                for h in range(HALVES):
                    for k in range(DC):
                        ins = mm(bank[4 + 2 * j + h][:, :], xT[:, k, h * P:(h + 1) * P], w[:, k, :], k == 0, k == DC - 1)
                    ins.then_inc(sem("ple_ps"), 1)

        def ple_scalar(act):
            for i in range(4):
                act.wait_ge(sem("ple_ps"), 4 + i + 1)
                if i >= 1:
                    act.wait_ge(sem("ple_done"), i)
                act.activation(ple_g, bank[4 + i][:, :], ACT.Sigmoid).then_inc(sem("ple_sig"), 1)
            norm_scalar(act, 7)

        def ple_vector(v):
            for i in range(4):
                j, h = i // 2, i % 2
                v.wait_ge(sem("ple_sig"), i + 1)
                ins = v.tensor_tensor(ple_t, ple_g, bank[i][:, :], ALU.mult)
                ins.then_inc(sem("ple_done"), 1)
                v.wait_ge(sem("ple_done"), i + 1)
                xs = xres[:, h, 512 * j:512 * j + 512]
                norm_stats(v, 7, xres, h, j, v.tensor_tensor(xs, xs, ple_t, ALU.add))
            v.wait_ge(sem("lnp_loaded"), 32 * 4 + 16)
            norm_vector(v, 7, xres, xn)

        LAST = {"gdn": 1, "ffn": 2, "s5": 3, "moe1": 4, "mix2": 5, "moe2": 6, "all": 7}[upto]
        STORES = HALVES

        block = ctx.enter_context(nc.Block())

        @block.sync
        def _(sp):
            sp.dma_start(xT[:, :, :], I["x_cols"]).then_inc(sem("first_loaded"), 16)

            def load(u, src, n=UNIT):
                sp.dma_start(slot(u)[:, 0:n], src).then_inc(sem(f"unit_loaded{u % RING}"), 16)

            def dense(u, first):
                load(u, I["w_dense"][DENSE_AT[first] + u - first])

            def released(u):
                if u < 0:
                    return
                if u < U_Z:
                    sp.wait_ge(sem("qkv_ps"), 4 * (u + 1))
                elif u < U_WOUT:
                    sp.wait_ge(sem("z_ps"), 2 * (u - U_Z + 1))
                elif u < U_FFN:
                    sp.wait_ge(sem("wout_ps"), 2 * (u - U_WOUT + 1))
                elif u < U_S5IN:
                    sp.wait_ge(sem("ffn_used"), max(s for s in range(FF_PIECES) if ff_unit(s) == u) + 1)
                elif u < U_GLU:
                    sp.wait_ge(sem("u_ps"), 4 * (u - U_S5IN + 1))
                elif u < U_MOE1:
                    sp.wait_ge(sem("glu_ps"), 2 * (u - U_GLU + 1))
                elif u < U_WIN2:
                    sp.wait_ge(sem("m1_split"), 2 * (u - U_MOE1 + 1))
                elif u < U_WIN2 + 3:
                    sp.wait_ge(sem("cxb_ps"), NC2 * (u - U_WIN2 + 1))
                elif u < U_WOUT2:
                    sp.wait_ge(sem("uv_ps"), HALVES * (u - U_WIN2 - 2))
                elif u < U_MOE2:
                    sp.wait_ge(sem("wout2_ps"), 2 * (u - U_WOUT2 + 1))
                elif u < U_PLE:
                    g, i = divmod(u - U_MOE2, RING)
                    sp.wait_ge(sem("m2_pe"), at(M2_PE, g, M2_UNIT_STEP[i]))

            def dense_phase(first, n):
                for u in range(first, first + n):
                    released(u - RING)
                    dense(u, first)

            for u in range(RING):
                dense(u, U_QKV)
            for name, dst in (("w_ba", w_ba), ("a_log", a_log), ("dt_bias", dt_bias),
                              ("norm_g", norm_g), ("consts", consts[:, :, :]), ("x_rows", xres[:, :, :]),
                              ("g_cols", g_cols), ("conv2_w", conv2_w), ("b_sp", b_sp), ("s5_d", s5_d)):
                sp.dma_start(dst, I[name]).then_inc(sem("small_loaded"), 16)
            load_norm(sp, 0)
            for name, dst in (("w_r1", w_r1), ("b_r1", b_r1), ("w_r2", w_r2), ("b_r2", b_r2)):
                sp.dma_start(dst, I[name]).then_inc(sem("router_loaded"), 16)
            for u in range(RING, U_Z):
                released(u - RING)
                dense(u, U_QKV)
            dense_phase(U_Z, 2)
            dense_phase(U_WOUT, 2)
            if LAST >= 2:
                for u in range(U_FFN, U_S5IN):
                    e, i = divmod(u - U_FFN, 9)
                    released(u - RING)
                    if i < 6:
                        load(u, I["ffn_wide"][e, i])
                    else:
                        load(u, I["ffn_last"][e, i - 6], 3 * D)
            if LAST >= 3:
                dense_phase(U_S5IN, 2)
                dense_phase(U_GLU, 4)
            if LAST >= 4:
                WIDE, NARROW = ("g0", "u0", "g1", "u1", "d0", "d1"), ("g2", "u2", "d2")

                def expert_load(e, j):
                    s = M1_STREAM[j]
                    if s in WIDE:
                        load(U_MOE1 + j, I["moe1_wide"][e, WIDE.index(s)])
                    else:
                        load(U_MOE1 + j, I["moe1_last"][e, NARROW.index(s)], 3 * D)
                for j in range(UNITS_EXPERT):
                    released(U_MOE1 + j - RING)
                    expert_load(0, j)
                with sp.Fori(1, EXPERTS) as it:
                    for j in range(UNITS_EXPERT):
                        sp.wait_ge(sem("m1_split"), it * NH + 2 * (j - RING + 1))
                        expert_load(it, j)
                overflow_sync(sp, 0)
            def pack_load(g, j):
                src = I["moe2_up"][g, j] if j < UP_UNITS else I["moe2_down"][g, j - UP_UNITS]
                if j < RING:
                    load(U_MOE2 + j, src)
                else:
                    sp.dma_start(extra[:, j - RING, :], src).then_inc(sem(f"extra_loaded{j - RING}"), 16)
            if LAST >= 5:
                dense_phase(U_WIN2, 5)
                sp.wait_ge(sem("phase_done"), 4 * 4)
                for j in range(RING, UNITS_PACK):
                    pack_load(0, j)
                dense_phase(U_WOUT2, 2)
            if LAST >= 6:
                for j in range(RING):
                    released(U_MOE2 + j - RING)
                    pack_load(0, j)
                with sp.Fori(1, PACKS) as it:
                    for j in range(UNITS_PACK):
                        sp.wait_ge(sem("m2_pe"), at(M2_PE, it, M2_UNIT_STEP[j], 1))
                        pack_load(it, j)
                for n in (1, 2):
                    overflow_sync(sp, n)
            if LAST >= 7:
                released(U_PLE - RING)
                load(U_PLE, I["w_ple"], 2 * D)
                for u in (U_PLE + 1, U_PLE + 2):
                    released(u - RING)
                    dense(u, U_PLE)
            nst = {1: 0, 2: 1, 3: 2, 4: 4, 5: 5, 6: 6, 7: 7}[LAST]
            src = xn if LAST == 7 else xres
            for h in range(HALVES):
                sp.wait_ge(sem("rows_normed"), 2 * nst + h + 1)
                sp.dma_start(out[h], src[:, h, :]).then_inc(sem("stored"), 16)
            sp.wait_ge(sem("stored"), 16 * STORES)

        @block.tensor
        def _(pe):
            gdn_tensor(pe)
            turn_tensor(pe, 0, xres)
            phase_end(pe, 1)
            if LAST >= 2:
                ffn_tensor(pe)
                turn_tensor(pe, 1, xres)
                phase_end(pe, 2)
            if LAST >= 3:
                s5_tensor(pe)
                turn_tensor(pe, 2, xres)
                phase_end(pe, 3)
            if LAST >= 4:
                moe1_tensor(pe)
                overflow_tensor(pe, 0)
                turn_tensor(pe, 4, xn)
                phase_end(pe, 4)
            if LAST >= 5:
                mix2_tensor(pe)
                phase_end(pe, 5)
            if LAST >= 6:
                moe2_tensor(pe)
                for n in (1, 2):
                    overflow_tensor(pe, n)
                if LAST >= 7:
                    emb_tensor(pe)
                turn_tensor(pe, 6, xn)
                phase_end(pe, 6)
            if LAST >= 7:
                ple_tensor(pe)

        @block.scalar
        def _(act):
            gdn_scalar(act)
            phase_end(act, 1)
            if LAST >= 2:
                ffn_scalar(act)
                phase_end(act, 2)
            if LAST >= 3:
                s5_scalar(act)
                phase_end(act, 3)
            if LAST >= 4:
                moe1_scalar(act)
                overflow_scalar(act, 0)
                norm_scalar(act, 3)
                norm_scalar(act, 4)
                phase_end(act, 4)
            if LAST >= 5:
                mix2_scalar(act)
                phase_end(act, 5)
            if LAST >= 6:
                moe2_scalar(act)
                for n in (1, 2):
                    overflow_scalar(act, n)
                norm_scalar(act, 6)
                phase_end(act, 6)
            if LAST >= 7:
                ple_scalar(act)

        @block.vector
        def _(v):
            gdn_vector(v)
            phase_end(v, 1)
            if LAST >= 2:
                ffn_vector(v)
                phase_end(v, 2)
            if LAST >= 3:
                s5_vector(v)
                phase_end(v, 3)
            if LAST >= 4:
                moe1_vector(v)
                overflow_vector(v, 0)
                residual_vector(v, 3, ALPHA)
                norm_vector(v, 3, xres, xres)
                v.drain().then_inc(sem("lnp_used"), 1)
                for h in range(HALVES):
                    norm_stats(v, 4, xres, h, 0, v.drain())
                    norm_stats(v, 4, xres, h, 1, v.drain())
                norm_vector(v, 4, xres, xn)
                turn_evacuate(v, 4, g_cols[:, 0, :])
                phase_end(v, 4)
            if LAST >= 5:
                mix2_vector(v)
                phase_end(v, 5)
            if LAST >= 6:
                moe2_vector(v)
                for n in (1, 2):
                    overflow_vector(v, n)
                residual_vector(v, 6, 1.0)
                norm_vector(v, 6, xres, xn)
                turn_evacuate(v, 6, g_cols[:, 2, :])
                phase_end(v, 6)
            if LAST >= 7:
                ple_vector(v)

        @block.gpsimd
        def _(g):
            gdn_gpsimd(g)
            phase_end(g, 1)
            if LAST >= 2:
                ffn_gpsimd(g)
                phase_end(g, 2)
            if LAST >= 3:
                s5_gpsimd(g)
                phase_end(g, 3)
            for n in range(4, min(LAST, 6) + 1):
                phase_end(g, n)


def kernel(**inputs):
    import concourse.bacc as _bacc
    from concourse.bass_utils import run_bass_kernel_spmd as _run

    arrays = layouts(inputs)
    nc = _bacc.Bacc("TRN2", target_bir_lowering=False, num_devices=1)
    I = {name: nc.dram_tensor(name, a.shape, F32, kind="ExternalInput").ap() for name, a in arrays.items()}
    out = nc.dram_tensor("out", (HALVES, P, D), F32, kind="ExternalOutput").ap()
    program(nc, I, out)
    r = _run(nc, [arrays], core_ids=[0])
    return np.asarray(r.results[0]["out"]).reshape(1, SEQ, D)


def constants():
    k, m = np.arange(P)[:, None], np.arange(P)[None, :]
    same = (k // CHUNK) == (m // CHUNK)
    t = [k == m, same & (k <= m), np.where(same & (k <= m), 0.0, NEG)]
    for i in range(6):
        s = 1 << i
        t.append((k // (2 * s) == m // (2 * s)) & (m % (2 * s) >= s) & (k % (2 * s) < s))
    t += [same, (k < CHUNK) & (m >= 0), (k >= CHUNK) & (m >= 0), k < m, (k >= 0) & (m >= 0), m + 0 * k, k <= m,
          k // 32 == m // 32]
    half = np.zeros((P, P))
    half[:, 0] = (np.arange(P) // S5_CH) % 2 == 0
    half[:, 1] = (np.arange(P) // S5_CH) % 2 == 1
    t.append(half)
    return np.ascontiguousarray(np.stack([np.asarray(a, np.float32) for a in t], axis=1))


def layouts(inp):
    inp = {k: np.asarray(v) for k, v in inp.items()}
    f32 = np.float32
    A = {}

    def rep(row):
        return np.broadcast_to(row.reshape(1, -1), (P, row.size))

    def kchunks(w):
        return w.reshape(-1, P, w.shape[-1]).transpose(1, 0, 2)

    def chunkcols(vec):
        return vec.reshape(-1, P).T

    x = inp["x"].reshape(SEQ, D)
    A["x_rows"] = x.reshape(HALVES, P, D).transpose(1, 0, 2)
    A["x_cols"] = x.reshape(SEQ, DC, P).transpose(2, 1, 0)
    w_in = inp["gdn_w_in"][0]
    A["w_ba"] = kchunks(w_in[:, 4 * D:])
    A["conv_w"] = inp["gdn_conv_w"][0].reshape(TAPS, QKV, P).transpose(2, 1, 0)
    A["a_log"], A["dt_bias"] = rep(inp["gdn_a_log"][0]), rep(inp["gdn_dt_bias"][0])
    A["norm_g"] = rep(inp["gdn_norm_g"][0])
    A["consts"] = constants()
    A["g_cols"] = np.stack([chunkcols(inp[n][0]) for n in ("g_mix_2", "g_ffn_2", "g_ple_2")], axis=1)
    A["conv2_w"] = inp["w_conv_2"][0].reshape(CONV2_TAPS, CW // P, P).transpose(2, 1, 0)
    A["b_sp"] = inp["b_spatial_2"][0].T
    A["s5_d"] = chunkcols(inp["s5_d"][0])
    A["ln_rows"] = np.stack([np.stack([rep(inp[n][i, j]) for n in ("ln_g", "ln_b")]) for i in range(2) for j in range(2)])
    chan = 8 * np.arange(DC)[None, :] + (np.arange(P) // 32 * 2 + np.arange(P) // 16 % 2)[:, None]
    pair = 2 * np.arange(PAIRS)[None, :] + (np.arange(P) // S5_STATE)[:, None]
    state = np.arange(P)[:, None] % S5_STATE

    def both(lam):
        return np.concatenate([lam[chan].reshape(P, -1), lam[pair, state]], axis=1)
    A["lam_re"], A["lam_im"] = both(inp["s5_lam_re"][0]), both(inp["s5_lam_im"][0])
    A["log_dt"] = both(np.repeat(inp["s5_log_dt"][0][:, None], S5_STATE, axis=1))

    def paired(t):
        o = np.zeros((2, S5_STATE, PAIRS, 2, S5_CH), f32)
        t = t.reshape(PAIRS, 2, S5_STATE, S5_CH)
        for g in range(2):
            o[g, :, :, g, :] = t[:, g].transpose(1, 0, 2)
        return o.reshape(P, PAIRS, 32)
    for part in ("re", "im"):
        b, c = inp["s5_b_" + part][0], inp["s5_c_" + part][0]
        A["c_" + part] = paired(c.transpose(0, 2, 1))
        A["b1_" + part] = paired(b)
        A["b2_" + part] = b[chan, :, (np.arange(P) % S5_CH)[:, None]]
    A["w_r1"], A["b_r1"] = kchunks(inp["moe_w_router"][0]), rep(inp["moe_b_router"][0])
    A["w_r2"] = kchunks(np.concatenate([inp["w_group_2"][0], inp["w_router_2"][0].transpose(1, 0, 2).reshape(D, -1)], axis=1))
    A["b_r2"] = rep(np.concatenate([inp["b_group_2"][0], inp["b_router_2"][0].reshape(-1)]))
    A["wsT"] = inp["w_spatial_2"][0].transpose(2, 0, 1)
    A["g_sgu"] = rep(inp["g_sgu_2"][0])
    A["pT"] = inp["p_2"][0, 0].reshape(SEQ, 2, P).transpose(2, 1, 0)
    A["g_final"] = rep(inp["g_final_2"])

    def cols(w, at, n=1):
        return [kchunks(w[:, at + 512 * i:at + 512 * i + 512]).reshape(P, UNIT) for i in range(n)]
    glu, w2in = inp["s5_w_glu"][0], inp["w_in_2"][0]
    units = cols(w_in, 0, 8) + cols(inp["gdn_w_out"][0], 0, 2) + cols(inp["s5_w_in"][0], 0, 2)
    units += cols(glu, 0) + cols(glu, D) + cols(glu, 512) + cols(glu, D + 512)
    units += cols(w2in, CW) + cols(w2in, 2 * CW) + cols(w2in, 0) + cols(w2in, 3 * CW, 2)
    units += cols(inp["w_out_2"][0], 0, 2) + cols(inp["w_ple_gate_2"][0], 0, 2)
    A["w_dense"] = np.stack(units)
    A["w_ple"] = kchunks(inp["w_ple_proj_2"][0]).reshape(P, 2 * D)

    def blocks(w1, w3, w2):
        u = []
        at = 0
        for nch in FF_BLOCKS:
            n = nch * P
            u.append([kchunks(w1[:, at:at + n]).reshape(P, -1), kchunks(w3[:, at:at + n]).reshape(P, -1),
                      kchunks(w2[at:at + n]).reshape(P, -1)])
            at += n
        return u
    halves = [blocks(inp["ffn_w1"][0][:, s], inp["ffn_w3"][0][:, s], inp["ffn_w2"][0][s])
              for s in (slice(0, FF_E), slice(FF_E, 2 * FF_E))]
    A["ffn_wide"] = np.stack([np.stack(h[0] + h[1]) for h in halves])
    A["ffn_last"] = np.stack([np.stack(h[2]) for h in halves])
    exps = [blocks(inp["moe_w1"][0, e], inp["moe_w3"][0, e], inp["moe_w2"][0, e]) for e in range(EXPERTS)]
    A["moe1_wide"] = np.stack([np.stack([b0[0], b0[1], b1[0], b1[1], b0[2], b1[2]]) for b0, b1, _ in exps])
    A["moe1_last"] = np.stack([np.stack(b2) for _, _, b2 in exps])
    gate_up = np.stack([inp["w_gate_2"][0], inp["w_up_2"][0]], axis=3)
    A["moe2_up"] = gate_up.reshape(PACKS, PACK, UP_UNITS, UP_K, P, 2, FF2).transpose(0, 2, 4, 1, 5, 3, 6)\
        .reshape(PACKS, UP_UNITS, P, -1)
    A["moe2_down"] = inp["w_down_2"][0].reshape(PACKS, PACK, DOWN_UNITS, DOWN_C, P, D).transpose(0, 2, 4, 1, 3, 5)\
        .reshape(PACKS, DOWN_UNITS, P, -1)
    return {k: np.ascontiguousarray(v, dtype=f32) for k, v in A.items()}
```
